# Optimizing a Trainium2 kernel written in Bass

```python
import jax, jax.numpy as jnp
from jax import lax
import numpy as np
import math

D_MODEL = 2048
BATCH = 1
SEQ = 256
DEPTH = 1

MEM_LEN = 256
EPS = 1e-6
POOL_WINDOWS = (2, 4, 8, 16)
POOL_GROUP_DIM = D_MODEL // 8
POOL_DIM = POOL_GROUP_DIM * len(POOL_WINDOWS)
HGRN_DK = 128
HGRN_DV = 128
HGRN_HEADS = D_MODEL // 256
HGRN_DIM = HGRN_HEADS * HGRN_DK
MIX_DIM = POOL_DIM + HGRN_DIM
IN_DIM = POOL_DIM + 4 * HGRN_DIM
CHUNK = 64
XATTN_HEADS = 4
XATTN_HEAD_DIM = D_MODEL // XATTN_HEADS
N_GROUPS = 4
EXPERTS_PER_GROUP = 4
N_EXPERTS = N_GROUPS * EXPERTS_PER_GROUP
TOP_K_INNER = 2
D_EXPERT = D_MODEL // 4


def rmsnorm(x, gain):
    xf = x.astype(jnp.float32)
    y = xf * lax.rsqrt(jnp.mean(xf * xf, axis=-1, keepdims=True) + EPS)
    return (y * gain.astype(jnp.float32)).astype(x.dtype)

def causal_pool_mixer(u, pool_w, pool_scale):
    b, s, _ = u.shape
    uf = u.astype(jnp.float32)
    cs = jnp.concatenate([jnp.zeros((b, 1, POOL_DIM), jnp.float32), jnp.cumsum(uf, axis=1)], axis=1)
    t_plus_1 = jnp.arange(1, s + 1, dtype=jnp.int32)
    outs = []
    for g, w in enumerate(POOL_WINDOWS):
        sl = slice(g * POOL_GROUP_DIM, (g + 1) * POOL_GROUP_DIM)
        c = cs[:, :, sl]
        upper = c[:, 1:]
        lower = jnp.pad(c[:, : s + 1 - w], ((0, 0), (w - 1, 0), (0, 0)))
        count = jnp.minimum(t_plus_1, w).astype(jnp.float32)[None, :, None]
        pooled = (upper - lower) / count - uf[:, :, sl]
        outs.append(jnp.einsum('bsc,cd->bsd', pooled.astype(u.dtype), pool_w[g]))
    return (jnp.concatenate(outs, axis=-1) * pool_scale).astype(u.dtype)

def hgrn2_mixer(q_in, f_in, i_in, g_in, lb, norm_gain):
    b, s, _ = q_in.shape
    n_chunks = s // CHUNK
    q = jax.nn.silu(q_in.astype(jnp.float32))
    lb = lb.astype(jnp.float32)
    log_f = jnp.logaddexp(jnp.log(lb), jnp.log1p(-lb) + jax.nn.log_sigmoid(f_in.astype(jnp.float32)))
    k = -jnp.expm1(log_f)
    v = i_in.astype(jnp.float32)

    def to_chunks(t, d):
        return t.reshape(b, n_chunks, CHUNK, HGRN_HEADS, d).transpose(1, 0, 3, 2, 4)

    causal = jnp.tril(jnp.ones((CHUNK, CHUNK), dtype=bool))[None, None, :, :, None]

    def step(state, xs):
        qc, lfc, kc, vc = xs
        a = jnp.cumsum(lfc, axis=2)
        rel = a[:, :, :, None, :] - a[:, :, None, :, :]
        decay = jnp.exp(jnp.where(causal, rel, -jnp.inf))
        scores = jnp.einsum('bhtd,bhtsd,bhsd->bhts', qc, decay, kc)
        o = jnp.einsum('bhts,bhsv->bhtv', scores, vc) + jnp.einsum('bhtd,bhdv->bhtv', qc * jnp.exp(a), state)
        a_last = a[:, :, -1:, :]
        new_state = jnp.exp(a_last[:, :, 0, :])[..., None] * state + jnp.einsum(
            'bhsd,bhsv->bhdv', kc * jnp.exp(a_last - a), vc)
        return new_state, o

    s0 = jnp.zeros((b, HGRN_HEADS, HGRN_DK, HGRN_DV), jnp.float32)
    _, o = lax.scan(step, s0, (to_chunks(q, HGRN_DK), to_chunks(log_f, HGRN_DK),
                               to_chunks(k, HGRN_DK), to_chunks(v, HGRN_DV)))
    o = o.transpose(1, 0, 3, 2, 4).reshape(b, s, HGRN_HEADS, HGRN_DV)
    o = rmsnorm(o, norm_gain)
    gate = jax.nn.silu(g_in.astype(jnp.float32)).reshape(b, s, HGRN_HEADS, HGRN_DV)
    return (o * gate).reshape(b, s, HGRN_HEADS * HGRN_DV).astype(q_in.dtype)

def memory_cross_attention(h, mem_n, wq, wk, wv, wo):
    b, s, _ = h.shape
    m = mem_n.shape[1]
    q = (h @ wq).reshape(b, s, XATTN_HEADS, XATTN_HEAD_DIM)
    k = (mem_n @ wk).reshape(b, m, XATTN_HEADS, XATTN_HEAD_DIM)
    v = (mem_n @ wv).reshape(b, m, XATTN_HEADS, XATTN_HEAD_DIM)
    scores = jnp.einsum('bshd,bmhd->bhsm', q, k).astype(jnp.float32) * (XATTN_HEAD_DIM ** -0.5)
    p = jax.nn.softmax(scores, axis=-1).astype(v.dtype)
    o = jnp.einsum('bhsm,bmhd->bshd', p, v).reshape(b, s, D_MODEL)
    return o @ wo

def hierarchical_moe(h, router_group, router_expert, w_gate, w_up, w_down):
    b, s, _ = h.shape
    p_group = jax.nn.softmax(jnp.einsum('bsd,dg->bsg', h, router_group).astype(jnp.float32), axis=-1)
    pg_top, g_idx = lax.top_k(p_group, 1)
    logits_e = jnp.einsum('bsd,de->bse', h, router_expert).astype(jnp.float32)
    logits_e = logits_e.reshape(b, s, N_GROUPS, EXPERTS_PER_GROUP)
    g_onehot = jax.nn.one_hot(g_idx[..., 0], N_GROUPS, dtype=jnp.float32)
    sel = jnp.einsum('bsg,bsge->bse', g_onehot, logits_e)
    top_vals, top_idx = lax.top_k(sel, TOP_K_INNER)
    w_inner = jax.nn.softmax(top_vals, axis=-1)
    expert_id = g_idx * EXPERTS_PER_GROUP + top_idx
    combine = jnp.sum(jax.nn.one_hot(expert_id, N_EXPERTS, dtype=jnp.float32)
                      * (pg_top * w_inner)[..., None], axis=2).astype(h.dtype)
    y = jnp.zeros_like(h)
    for e in range(N_EXPERTS):
        hid = jax.nn.silu(h @ w_gate[e]) * (h @ w_up[e])
        y = y + combine[..., e:e + 1] * (hid @ w_down[e])
    return y

def first_inputs(seed: int = 0) -> dict:
    key = jax.random.key(seed)
    ks = jax.random.split(key, 24)
    f32 = jnp.float32

    def nrm(k, shape, scale):
        return jax.random.normal(k, shape, f32) * scale

    def gain(k, shape):
        return 1.0 + 0.02 * jax.random.normal(k, shape, f32)

    return {
        "x": nrm(ks[0], (BATCH, SEQ, D_MODEL), 1.0),
        "mem": nrm(ks[1], (BATCH, MEM_LEN, D_MODEL), 1.0),
        "norm_mix": gain(ks[2], (DEPTH, D_MODEL)),
        "w_in": nrm(ks[3], (DEPTH, D_MODEL, IN_DIM), D_MODEL ** -0.5),
        "pool_w": nrm(ks[4], (DEPTH, len(POOL_WINDOWS), POOL_GROUP_DIM, POOL_GROUP_DIM), POOL_GROUP_DIM ** -0.5),
        "pool_scale": gain(ks[5], (DEPTH, POOL_DIM)),
        "hgrn_lb_logits": nrm(ks[6], (DEPTH + 1, HGRN_DIM), 0.5),
        "hgrn_norm": gain(ks[7], (DEPTH, HGRN_DV)),
        "w_out": nrm(ks[8], (DEPTH, MIX_DIM, D_MODEL), MIX_DIM ** -0.5),
        "norm_xattn": gain(ks[9], (DEPTH, D_MODEL)),
        "norm_mem": gain(ks[10], (DEPTH, D_MODEL)),
        "xattn_wq": nrm(ks[11], (DEPTH, D_MODEL, D_MODEL), D_MODEL ** -0.5),
        "xattn_wk": nrm(ks[12], (DEPTH, D_MODEL, D_MODEL), D_MODEL ** -0.5),
        "xattn_wv": nrm(ks[13], (DEPTH, D_MODEL, D_MODEL), D_MODEL ** -0.5),
        "xattn_wo": nrm(ks[14], (DEPTH, D_MODEL, D_MODEL), D_MODEL ** -0.5),
        "norm_ffn": gain(ks[15], (DEPTH, D_MODEL)),
        "router_group": nrm(ks[16], (DEPTH, D_MODEL, N_GROUPS), D_MODEL ** -0.5),
        "router_expert": nrm(ks[17], (DEPTH, D_MODEL, N_EXPERTS), D_MODEL ** -0.5),
        "w_gate": nrm(ks[18], (DEPTH, N_EXPERTS, D_MODEL, D_EXPERT), D_MODEL ** -0.5),
        "w_up": nrm(ks[19], (DEPTH, N_EXPERTS, D_MODEL, D_EXPERT), D_MODEL ** -0.5),
        "w_down": nrm(ks[20], (DEPTH, N_EXPERTS, D_EXPERT, D_MODEL), D_EXPERT ** -0.5),
        "norm_final": gain(ks[21], (D_MODEL,)),
    }

def first_block(x, mem, norm_mix, w_in, pool_w, pool_scale, hgrn_lb_logits, hgrn_norm, w_out,
              norm_xattn, norm_mem, xattn_wq, xattn_wk, xattn_wv, xattn_wo, norm_ffn,
              router_group, router_expert, w_gate, w_up, w_down, norm_final):
    lower_bounds = jnp.cumsum(jax.nn.softmax(hgrn_lb_logits.astype(jnp.float32), axis=0), axis=0)
    splits = [POOL_DIM, POOL_DIM + HGRN_DIM, POOL_DIM + 2 * HGRN_DIM, POOL_DIM + 3 * HGRN_DIM]
    for l in range(DEPTH):
        h = rmsnorm(x, norm_mix[l])
        proj = h @ w_in[l]
        u, q_in, f_in, i_in, g_in = jnp.split(proj, splits, axis=-1)
        pool_out = causal_pool_mixer(u, pool_w[l], pool_scale[l])
        hgrn_out = hgrn2_mixer(q_in, f_in, i_in, g_in, lower_bounds[l], hgrn_norm[l])
        x = x + jnp.concatenate([pool_out, hgrn_out], axis=-1) @ w_out[l]
        h = rmsnorm(x, norm_xattn[l])
        m = rmsnorm(mem, norm_mem[l])
        x = x + memory_cross_attention(h, m, xattn_wq[l], xattn_wk[l], xattn_wv[l], xattn_wo[l])
        h = rmsnorm(x, norm_ffn[l])
        x = x + hierarchical_moe(h, router_group[l], router_expert[l], w_gate[l], w_up[l], w_down[l])
    return rmsnorm(x, norm_final)


DEPTH_2 = 2

GRID_W = 64
D_MIX = D_MODEL
N_MIXERS = 4
D_GROUP = D_MIX // N_MIXERS
HEAD_DIM = 64
N_NA_HEADS = D_GROUP // HEAD_DIM
N_RET_HEADS = D_GROUP // HEAD_DIM
N_FFT_GROUPS = 4
FFT_GROUP_DIM = D_GROUP // N_FFT_GROUPS
NA_KH_MAX = 8
NA_KW = 16
RET_CHUNK = 128
CONV_WIDTH = 31
ROPE_BASE = 10000.0
N_IN_PIECES = 13
D_IN = N_IN_PIECES * D_GROUP


def _rmsnorm(x, g):
    xf = x.astype(jnp.float32)
    ms = jnp.mean(xf * xf, axis=-1, keepdims=True)
    return (xf * lax.rsqrt(ms + EPS)).astype(x.dtype) * g

def _fourier_mix(u, w_fft):
    B, S, _ = u.shape
    uf = u.astype(jnp.float32).reshape(B, S, N_FFT_GROUPS, FFT_GROUP_DIM)
    y = jnp.real(jnp.fft.fft2(uf, axes=(1, 3), norm="ortho"))
    return y.reshape(B, S, D_GROUP).astype(u.dtype) @ w_fft

def _neighbourhood_attention(q, k, v, rel_bias):
    B, S, _ = q.shape
    rows = S // GRID_W
    kh = min(NA_KH_MAX, rows)

    def grid(t):
        return t.reshape(B, rows, GRID_W, N_NA_HEADS, HEAD_DIM)

    qg = grid(q) * (HEAD_DIM ** -0.5)
    kg, vg = grid(k), grid(v)
    r = jnp.arange(rows)
    row_start = jnp.clip(r - kh // 2, 0, rows - kh)
    key_rows = row_start[:, None] + jnp.arange(kh)[None, :]
    kb = kg[:, key_rows]
    vb = vg[:, key_rows]
    col = jnp.arange(GRID_W)
    col_start = jnp.clip(col - NA_KW // 2, 0, GRID_W - NA_KW)
    rel_c = col[None, :] - col_start[:, None]
    col_in = (rel_c >= 0) & (rel_c < NA_KW)
    dc = col[None, :] - col[:, None]
    dr = key_rows - r[:, None]
    bias = rel_bias[:, (dr + NA_KH_MAX - 1)[:, :, None, None],
                    jnp.clip(dc + NA_KW - 1, 0, 2 * NA_KW - 2)[None, None]]
    bias = bias.transpose(0, 1, 3, 2, 4)
    s = jnp.einsum('brqhd,brakhd->bhrqak', qg, kb).astype(jnp.float32)
    s = s + bias[None].astype(jnp.float32)
    s = jnp.where(col_in[:, None, :], s, -jnp.inf)
    p = jax.nn.softmax(s.reshape(B, N_NA_HEADS, rows, GRID_W, kh * GRID_W), axis=-1)
    p = p.reshape(B, N_NA_HEADS, rows, GRID_W, kh, GRID_W).astype(v.dtype)
    o = jnp.einsum('bhrqak,brakhd->brqhd', p, vb)
    return o.reshape(B, S, D_GROUP)

def _rotary(t):
    S = t.shape[2]
    half = HEAD_DIM // 2
    inv = ROPE_BASE ** (-jnp.arange(half, dtype=jnp.float32) / half)
    ang = jnp.arange(S, dtype=jnp.float32)[:, None] * inv[None, :]
    cos, sin = jnp.cos(ang), jnp.sin(ang)
    t1, t2 = t[..., :half], t[..., half:]
    return jnp.concatenate([t1 * cos - t2 * sin, t1 * sin + t2 * cos], axis=-1)

def _retention_direction(q, k, v, log_gamma, include_diag):
    B, H, S, Dh = q.shape
    C = RET_CHUNK
    n = S // C
    qc = q.reshape(B, H, n, C, Dh)
    kc = k.reshape(B, H, n, C, Dh)
    vc = v.reshape(B, H, n, C, Dh)
    idx = jnp.arange(C, dtype=jnp.float32)
    diff = idx[:, None] - idx[None, :]
    mask = (diff >= 0) if include_diag else (diff > 0)
    lg = log_gamma[:, None, None]
    d_intra = jnp.where(mask, jnp.exp(lg * jnp.where(mask, diff, 0.0)), 0.0)
    scores = jnp.einsum('bhnid,bhnjd->bhnij', qc, kc) * d_intra[None, :, None]
    o_intra = jnp.einsum('bhnij,bhnjd->bhnid', scores, vc)
    k_decay = jnp.exp(log_gamma[:, None] * (C - 1 - idx)[None, :])
    kv = jnp.einsum('bhnjd,bhnje->nbhde', kc * k_decay[None, :, None, :, None], vc)
    chunk_decay = jnp.exp(log_gamma * C)[None, :, None, None]

    def step(state, kv_n):
        return chunk_decay * state + kv_n, state

    _, prev = lax.scan(step, jnp.zeros((B, H, Dh, Dh), jnp.float32), kv)
    q_decay = jnp.exp(log_gamma[:, None] * (idx + 1.0)[None, :])
    o_cross = jnp.einsum('bhnid,nbhde->bhnie', qc * q_decay[None, :, None, :, None], prev)
    return (o_intra + o_cross).reshape(B, H, S, Dh)

def _retention(q, k, v, logit_fwd, logit_bwd):
    B, S, _ = q.shape

    def heads(t):
        return t.astype(jnp.float32).reshape(B, S, N_RET_HEADS, HEAD_DIM).transpose(0, 2, 1, 3)

    qh = _rotary(heads(q)) * (HEAD_DIM ** -0.5)
    kh = _rotary(heads(k))
    vh = heads(v)
    lf = jax.nn.log_sigmoid(logit_fwd.astype(jnp.float32))
    lb = jax.nn.log_sigmoid(logit_bwd.astype(jnp.float32))
    fwd = _retention_direction(qh, kh, vh, lf, True)
    bwd = _retention_direction(qh[:, :, ::-1], kh[:, :, ::-1], vh[:, :, ::-1], lb, False)[:, :, ::-1]
    o = fwd + bwd
    o = o * lax.rsqrt(jnp.mean(o * o, axis=-1, keepdims=True) + EPS)
    return o.transpose(0, 2, 1, 3).reshape(B, S, D_GROUP).astype(q.dtype)

def _conformer_conv(a, b, conv_w, conv_b, ln_g, ln_b, w_pw):
    u = a * jax.nn.sigmoid(b)
    y = lax.conv_general_dilated(
        u, conv_w[:, None, :].astype(u.dtype), window_strides=(1,),
        padding=[(CONV_WIDTH // 2, CONV_WIDTH // 2)],
        dimension_numbers=('NWC', 'WIO', 'NWC'), feature_group_count=D_GROUP) + conv_b
    yf = y.astype(jnp.float32)
    mu = jnp.mean(yf, axis=-1, keepdims=True)
    var = jnp.mean((yf - mu) ** 2, axis=-1, keepdims=True)
    y = ((yf - mu) * lax.rsqrt(var + EPS)).astype(u.dtype) * ln_g + ln_b
    return jax.nn.silu(y) @ w_pw

def second_inputs(seed: int = 0) -> dict:
    key = jax.random.key(seed)
    ks = jax.random.split(key, 17)
    f32 = jnp.float32
    nrm = lambda k, shape, s: jax.random.normal(k, shape, f32) * s
    gam = 1.0 - 2.0 ** (-5.0 - jnp.arange(N_RET_HEADS, dtype=f32))
    ret_logit0 = jnp.log(gam) - jnp.log1p(-gam)
    return {
        "x": nrm(ks[0], (BATCH, SEQ, D_MODEL), 1.0),
        "c": nrm(ks[1], (BATCH, D_MODEL), 1.0),
        "norm_g": 1.0 + nrm(ks[2], (DEPTH_2, D_MODEL), 0.01),
        "w_ada": nrm(ks[3], (DEPTH_2, D_MODEL, 3 * D_MODEL), 0.5 * D_MODEL ** -0.5),
        "b_ada": nrm(ks[4], (DEPTH_2, 3 * D_MODEL), 0.01),
        "w_in": nrm(ks[5], (DEPTH_2, D_MODEL, D_IN), D_MODEL ** -0.5),
        "w_fft": nrm(ks[6], (DEPTH_2, D_GROUP, D_GROUP), D_GROUP ** -0.5),
        "na_rel_bias": nrm(ks[7], (DEPTH_2, N_NA_HEADS, 2 * NA_KH_MAX - 1, 2 * NA_KW - 1), 0.02),
        "ret_logit_fwd": ret_logit0[None] + nrm(ks[8], (DEPTH_2, N_RET_HEADS), 0.01),
        "ret_logit_bwd": ret_logit0[None] + nrm(ks[9], (DEPTH_2, N_RET_HEADS), 0.01),
        "conv_w": nrm(ks[10], (DEPTH_2, CONV_WIDTH, D_GROUP), CONV_WIDTH ** -0.5),
        "conv_b": nrm(ks[11], (DEPTH_2, D_GROUP), 0.01),
        "conv_ln_g": 1.0 + nrm(ks[12], (DEPTH_2, D_GROUP), 0.01),
        "conv_ln_b": nrm(ks[13], (DEPTH_2, D_GROUP), 0.01),
        "conv_w_pw": nrm(ks[14], (DEPTH_2, D_GROUP, D_GROUP), D_GROUP ** -0.5),
        "w_out": nrm(ks[15], (DEPTH_2, D_MIX, D_MODEL), D_MIX ** -0.5),
        "final_g": 1.0 + nrm(ks[16], (D_MODEL,), 0.01),
    }

def second_block(x, c, norm_g, w_ada, b_ada, w_in, w_fft, na_rel_bias, ret_logit_fwd, ret_logit_bwd,
              conv_w, conv_b, conv_ln_g, conv_ln_b, conv_w_pw, w_out, final_g):
    c_act = jax.nn.silu(c)
    for l in range(DEPTH_2):
        mod = c_act @ w_ada[l] + b_ada[l]
        shift, scale, gate = jnp.split(mod, 3, axis=-1)
        h = _rmsnorm(x, norm_g[l]) * (1.0 + scale[:, None, :]) + shift[:, None, :]
        z = h @ w_in[l]
        (f_x, f_g, na_q, na_k, na_v, na_g, r_q, r_k, r_v, r_g,
         cv_a, cv_b, cv_g) = jnp.split(z, N_IN_PIECES, axis=-1)
        o_fft = _fourier_mix(f_x, w_fft[l]) * jax.nn.silu(f_g)
        o_na = _neighbourhood_attention(na_q, na_k, na_v, na_rel_bias[l]) * jax.nn.silu(na_g)
        o_ret = _retention(r_q, r_k, r_v, ret_logit_fwd[l], ret_logit_bwd[l]) * jax.nn.silu(r_g)
        o_cv = _conformer_conv(cv_a, cv_b, conv_w[l], conv_b[l], conv_ln_g[l], conv_ln_b[l],
                               conv_w_pw[l]) * jax.nn.silu(cv_g)
        y = jnp.concatenate([o_fft, o_na, o_ret, o_cv], axis=-1) @ w_out[l]
        x = x + gate[:, None, :] * y
    return _rmsnorm(x, final_g)


def setup_inputs(seed=0):
    out = dict(first_inputs(seed))
    for name, value in second_inputs(seed + 1).items():
        if name != "x":
            out[name + "_2"] = value
    return out


def reference(
    x, mem, norm_mix, w_in, pool_w, pool_scale, hgrn_lb_logits, hgrn_norm, w_out, norm_xattn,
    norm_mem, xattn_wq, xattn_wk, xattn_wv, xattn_wo, norm_ffn, router_group, router_expert,
    w_gate, w_up, w_down, norm_final, c_2, norm_g_2, w_ada_2, b_ada_2, w_in_2, w_fft_2,
    na_rel_bias_2, ret_logit_fwd_2, ret_logit_bwd_2, conv_w_2, conv_b_2, conv_ln_g_2,
    conv_ln_b_2, conv_w_pw_2, w_out_2, final_g_2,
):
    x = first_block(
        x, mem, norm_mix, w_in, pool_w, pool_scale, hgrn_lb_logits, hgrn_norm, w_out,
        norm_xattn, norm_mem, xattn_wq, xattn_wk, xattn_wv, xattn_wo, norm_ffn, router_group,
        router_expert, w_gate, w_up, w_down, norm_final,
    )
    return second_block(
        x, c_2, norm_g_2, w_ada_2, b_ada_2, w_in_2, w_fft_2, na_rel_bias_2, ret_logit_fwd_2,
        ret_logit_bwd_2, conv_w_2, conv_b_2, conv_ln_g_2, conv_ln_b_2, conv_w_pw_2, w_out_2,
        final_g_2,
    )


_drawn_inputs = setup_inputs


def setup_inputs(seed=0):
    import zlib

    import numpy as np

    out = dict(_drawn_inputs(seed))
    spreads = {}
    factors = {'norm_mix': 2.734,
     'pool_scale': 3.293,
     'hgrn_norm': 3.107,
     'norm_xattn': 4.638,
     'norm_mem': 8.0,
     'norm_ffn': 3.586,
     'norm_g_2': 8.0,
     'b_ada_2': 6.231,
     'na_rel_bias_2': 8.0,
     'conv_b_2': 8.0,
     'conv_ln_g_2': 8.0,
     'conv_ln_b_2': 8.0,
     'final_g_2': 5.522}
    for name, (base, spread) in spreads.items():
        noise = np.random.default_rng([zlib.crc32(name.encode()), seed]).standard_normal(out[name].shape)
        drawn = base * np.exp(spread * noise) if base else spread * noise
        out[name] = __import__('jax').numpy.asarray(drawn.astype(out[name].dtype))
    for name, factor in factors.items():
        out[name] = (out[name] * factor).astype(out[name].dtype)
    return out
```

```python
from contextlib import ExitStack

import numpy as np

import concourse.bass as bass
from concourse import mybir

F32 = mybir.dt.float32
F16 = mybir.dt.float16
ALU = mybir.AluOpType
ACT = mybir.ActivationFunctionType
AX = mybir.AxisListType

P = 128
T = 256
TT = T // P
D = 2048
KC = D // P
EPS = 1e-6
W_SCALE = 256.0
BLK = 2048
RAW = 4
SPL = 2
POOL_WINDOWS = (2, 4, 8, 16)
HEADS = 8
SUB = 32
HALF = SUB // 2
NCH = T // SUB
X_HEADS = 4
X_DH = D // X_HEADS
GROUPS, PER_GROUP = 4, 4
N_EXP = GROUPS * PER_GROUP
D_EXP = 512
LAYERS = 2
N_SUMS = LAYERS * 3
GRID_W, NA_KW, NA_KH = 64, 16, 8
REL_H, REL_W = 2 * NA_KH - 1, 2 * NA_KW - 1
TAPS = 31
DH = 64
NEG = -1.0e30


def constants():
    p, t = np.arange(P), np.arange(T)
    out = {"ident": np.eye(P)}
    ang = 2 * np.pi * np.outer(p, p) / P
    out["dft_ch"] = np.concatenate([np.cos(ang), np.sin(ang)], 1)
    ang = 2 * np.pi * (np.outer(t, t) % T) / T
    norm = 1.0 / np.sqrt(T * P)
    for name, m in (("dft_cos", np.cos(ang) * norm), ("dft_nsin", -np.sin(ang) * norm)):
        out[name] = m.reshape(TT, P, T).transpose(1, 0, 2).reshape(P, TT * T)
    half = DH // 2
    inv = (np.float32(10000.0) ** (-np.arange(half, dtype=np.float32) / np.float32(half))).astype(np.float32)
    rope = (t.astype(np.float32)[None, :] * inv[p % half][:, None]).astype(np.float32)
    out["rope_cos"], out["rope_sin"] = np.cos(rope), np.sin(rope)
    rot = np.zeros((P, P))
    for m in range(P):
        if m % DH < half:
            rot[m + half, m] = -1.0
        else:
            rot[m - half, m] = 1.0
    out["rot"] = rot
    d = t[None, :] - t[:, None]
    for name, m in (("ahead", np.maximum(d, 0)), ("behind", np.maximum(-d, 0))):
        out[name] = m.reshape(TT, P, T).transpose(1, 0, 2).reshape(P, TT * T)
    c, k = GRID_W - 1 - p % GRID_W, t % GRID_W
    start = np.clip(c - NA_KW // 2, 0, GRID_W - NA_KW)
    rel = k[None, :] - start[:, None]
    out["na_mask"] = np.where((rel >= 0) & (rel < NA_KW), 0.0, NEG)
    out["unflip"] = ((p[:, None] // GRID_W == p[None, :] // GRID_W) & (p[:, None] % GRID_W == GRID_W - 1 - p[None, :] % GRID_W)) * DH ** 0.5
    out["causal"] = (p[:, None] % SUB <= np.arange(SUB)[None, :]) * 1.0
    out["prio"] = np.tile(np.arange(4, 0, -1), (P, 1))
    out["pair"] = (p[:, None] // DH == p[None, :] // DH) * 1.0
    return {n: np.ascontiguousarray(v, dtype=np.float32) for n, v in out.items()}


def counts():
    t = np.arange(T)
    return np.concatenate([np.tile(1.0 / np.minimum(t + 1, w), (P, 1)) for w in POOL_WINDOWS], 1).astype(np.float32)


ROWS = [("norm_mix", 16), ("pool_scale", 8), ("hgrn_lb_logits", 16), ("hgrn_norm", 1), ("norm_xattn", 16),
        ("norm_mem", 16), ("norm_ffn", 16), ("norm_final", 16), ("c_2", 16), ("norm_g_2", 32),
        ("b_ada_2", 96), ("conv_w_2", 248), ("conv_b_2", 8), ("conv_ln_g_2", 8), ("conv_ln_b_2", 8),
        ("final_g_2", 16)]
N_ROWS = sum(n for _, n in ROWS)
ROW_TILES = -(-N_ROWS // P)

STREAM = [("w_in", 40, True), ("pool_w", 1, False), ("w_out", 16, True), ("wk", 16, True), ("wv", 16, True),
          ("wq", 16, True), ("wo", 16, True), ("moe", 12 * N_EXP, True)]
for _l in range(LAYERS):
    STREAM += [(f"z{_l}", 52, True), (f"fft{_l}", 1, False), (f"pw{_l}", 1, False),
               (f"mix{_l}", 16, True)]


def places():
    out, b, s = {}, 0, 0
    for name, n, split in STREAM:
        out[name] = (b, s, n)
        b, s = b + n, s + n * split
    return out


def bank_uses():
    out, used = {}, [0] * 4
    for name, n, split in STREAM:
        out[name] = list(used)
        if name == "moe":
            used = [x + 3 * N_EXP for x in used]
        elif split:
            used = [used[0] + n // 4, used[1] + n // 4] + used[2:]
    out["end"] = used
    return out


def build(nc, A, table, const_at, window_counts, out, dbg=()):
    ctx = ExitStack()
    with ctx:
        def sb(name, shape, dt=F32):
            return ctx.enter_context(nc.sbuf_tensor(name, shape, dt))

        sems = {}

        def S(name):
            if name not in sems:
                sems[name] = ctx.enter_context(nc.semaphore(name))
            return sems[name]

        raw_full = [S(f"raw_full{j}") for j in range(RAW)]
        raw_taken = [S(f"raw_taken{j}") for j in range(RAW)]
        hi_done = S("hi_done")
        block_done = [S(f"block_done{j}") for j in range(SPL)]
        ada_full = [S(f"ada_full{j}") for j in range(2)]
        ada_used = [S(f"ada_used{j}") for j in range(2)]
        bank_free = [S(f"bank_free{j}") for j in range(4)]

        raw = sb("raw", [P, RAW, BLK])
        w_hi = sb("w_hi", [P, SPL, BLK], F16)
        w_lo = sb("w_lo", [P, SPL, BLK], F16)
        XT = sb("XT", [P, KC, T])
        H = sb("H", [P, 2 * BLK])
        xh = H[:, 0:BLK].bitcast(F16).rearrange("p (c t) -> p c t", t=T)
        xl = H[:, BLK:2 * BLK].bitcast(F16).rearrange("p (c t) -> p c t", t=T)
        H0 = H[:, 0:BLK]
        Z = sb("Z", [P, 52, T])
        Y = sb("Y", [P, KC, T])
        W = sb("W", [P, 4 * BLK])
        w0, w1, w2, w3 = (W[:, k * BLK:(k + 1) * BLK] for k in range(4))
        CT = sb("CT", [P, table.shape[1]])
        PR = w3[:, 0:ROW_TILES * P].rearrange("p (a b) -> p a b", b=P)
        PCt = sb("PCt", [P, ROW_TILES, P])
        PC = PCt[:, :, :].rearrange("p a b -> p (a b)")
        ones = sb("ones", [P, P])
        eps = sb("eps", [P, 1])
        NS = sb("NS", [P, 3, T])
        ssum, nstd, rstd = NS[:, 0, :], NS[:, 1, :], NS[:, 2, :]
        RW = sb("RW", [P, KC, GROUPS + N_EXP])
        RT = sb("RT", [P, 400])
        MOD = sb("MOD", [P, LAYERS, 3 * KC])
        GAIN = sb("GAIN", [P, KC])
        SM = sb("SM", [P, 64])
        LG = sb("LG", [P, 96])
        NAS = sb("NAS", [P, 32])
        CMB = sb("CMB", [P, TT * N_EXP])
        CU = H[:, 0:4 * (T + TAPS - 1)].rearrange("p (c t) -> p c t", c=4)
        RO = H[:, BLK:BLK + 2 * T].rearrange("p (c t) -> p c t", t=T)
        GB = ctx.enter_context(nc.psum_tensor("GB", [P, 4, 512], F32))
        MB = ctx.enter_context(nc.psum_tensor("MB", [P, 4, 512], F32))

        def const(name, rows=P):
            at, n = const_at[name]
            return CT[0:rows, at:at + n]

        ident = const("ident")
        row_at, n = {}, 0
        for name, k in ROWS:
            row_at[name] = n
            n += k

        def col(name, i=0, n=1):
            return PC[:, row_at[name] + i:row_at[name] + i + n]

        def chunks(ap):
            return ap.rearrange("p (c t) -> p c t", t=T)

        at = places()
        uses = bank_uses()
        Zn = Z[:, 32:48, :]
        SUMS = Z[:, 0:48, :].rearrange("p c t -> p (c t)")
        ADA = W[:, :].rearrange("p (a b n) -> p a b n", b=2, n=BLK)[:, :, 1, :]
        INV = 1.0 / W_SCALE

        def taken(eng, ph, j, i=0):
            b = at[ph][0] + j
            eng.wait_ge(raw_taken[b % RAW], b // RAW + 1 + i)

        def done(eng, ph, j, i=0):
            s = at[ph][1] + j
            eng.wait_ge(block_done[s % SPL], s // SPL + 1 + 2 * i)

        def read_out(eng, ph):
            for b in range(4):
                eng.wait_ge(bank_free[b], uses[ph][b])

        LIN = {"w_in": ("w_in", None), "w_out": ("w_out", None), "wk": ("xattn_wk", None), "wv": ("xattn_wv", None),
               "wq": ("xattn_wq", None), "wo": ("xattn_wo", None)}
        for l in range(LAYERS):
            LIN |= {f"z{l}": ("w_in_2", l), f"mix{l}": ("w_out_2", l)}
        AFTER = {}
        names = [n for n, _, _ in STREAM]
        for a, b in zip(names, names[1:] + ["end"]):
            AFTER[a] = b

        block = ctx.enter_context(nc.Block())

        @block.sync
        def _(sp):
            sp.dma_start(CT[:, :], table).then_inc(S("consts"), 16)
            sp.dma_start(Z[:, 48:52, :].rearrange("p c t -> p (c t)"), window_counts).then_inc(S("counts_in"), 16)
            sp.dma_start(chunks(W[:, 0:2 * BLK]).rearrange("p (a c) t -> p a (c t)", a=TT),
                         A["x"].rearrange("o (a p) d -> p (o a) d", p=P)).then_inc(S("x_in"), 16)

            def load(ph, j, src, shape, i=0):
                b = at[ph][0] + j
                sp.wait_ge(raw_taken[b % RAW], b // RAW + i)
                n = int(np.prod(shape[1:]))
                dst = raw[:, b % RAW, 0:n].rearrange("p (c n) -> p c n", n=shape[-1])
                sp.dma_start(dst, src).then_inc(raw_full[b % RAW], 16)

            def linear(ph):
                name, l = LIN[ph]
                w = A[name][l or 0].rearrange("(h c p) n -> h p c n", c=8, p=P)
                with sp.Fori(0, at[ph][2] // 4) as i:
                    for j in range(4):
                        load(ph, j, w[j % 2][:, :, bass.ds(i * 512 + j // 2 * 256, 256)], [P, 8, 256], i)

            linear("w_in")
            load("pool_w", 0, A["pool_w"].rearrange("o g (c p) n -> p (o g c) n", p=P), [P, 8, 256])
            for ph in ("w_out", "wk", "wv", "wq", "wo"):
                linear(ph)
            wg = A["w_gate"].rearrange("o e (h c p) n -> h p (o e) c n", c=8, p=P)
            wu = A["w_up"].rearrange("o e (h c p) n -> h p (o e) c n", c=8, p=P)
            wd = A["w_down"].rearrange("o e (c p) n -> p (o e) c n", p=P)
            with sp.Fori(0, N_EXP) as e:
                for j in range(12):
                    b = at["moe"][0] + j
                    sp.wait_ge(raw_taken[b % RAW], b // RAW + 3 * e)
                    if j < 8:
                        w = wg if j // 2 % 2 == 0 else wu
                        src = w[j % 2][:, bass.ds(e, 1), :, j // 4 * 256:j // 4 * 256 + 256]
                    else:
                        src = wd[:, bass.ds(e, 1), :, (j - 8) * 512:(j - 7) * 512]
                    dst = raw[:, b % RAW, :].rearrange("p (a c n) -> p a c n", a=1, n=src.shape[-1])
                    sp.dma_start(dst, src).then_inc(raw_full[b % RAW], 16)
            for l in range(LAYERS):
                linear(f"z{l}")
                load(f"fft{l}", 0, A["w_fft_2"][l].rearrange("(c p) n -> p c n", p=P), [P, 4, 512])
                load(f"pw{l}", 0, A["conv_w_pw_2"][l].rearrange("(c p) n -> p c n", p=P), [P, 4, 512])
                linear(f"mix{l}")
            sp.wait_ge(S("out_rows"), 8)
            sp.dma_start(out.rearrange("o (a p) d -> p (o a) d", p=P),
                         chunks(W[:, 0:2 * BLK]).rearrange("p (a c) t -> p a (c t)", a=TT)).then_inc(S("stored"), 16)
            sp.wait_ge(S("stored"), 16)

        @block.gpsimd
        def _(gp):
            gp.memset(ones[:, :], 1.0).then_inc(S("fills"), 1)
            gp.memset(eps[:, :], EPS).then_inc(S("fills"), 1)
            gp.memset(PR[:, ROW_TILES - 1, :], 0.0).then_inc(S("fills"), 1)
            gp.wait_ge(S("fills"), 3)
            loads = 0
            for name, n in ROWS:
                v = A[name]
                while len(v.shape) > 1:
                    v = v.rearrange("a b c -> (a b) c" if len(v.shape) == 3 else "a b -> (a b)")
                v = v.rearrange("(r f) -> r f", f=P)
                a, r = row_at[name], 0
                while r < n:
                    k = min(n - r, P - (a + r) % P)
                    gp.dma_start(PR[(a + r) % P:(a + r) % P + k, (a + r) // P, :], v[r:r + k]).then_inc(S("rows_in"), 16)
                    loads += 1
                    r += k
            assert loads == N_LOADS
            gp.dma_start(RW[:, :, 0:GROUPS], A["router_group"].rearrange("o (c p) n -> p (o c) n", p=P)).then_inc(S("router_in"), 16)
            gp.dma_start(RW[:, :, GROUPS:], A["router_expert"].rearrange("o (c p) n -> p (o c) n", p=P)).then_inc(S("router_in"), 16)
            for k, name in enumerate(("ret_logit_fwd_2", "ret_logit_bwd_2")):
                gp.dma_start(LG[:, 16 * k:16 * k + 16], A[name].rearrange("a b -> (a b)").partition_broadcast(P)).then_inc(S("logits_in"), 16)
            gp.wait_ge(S("cols"), ROW_TILES)
            gp.memset(w3, 0.0).then_inc(S("bd_zero"), 1)
            gp.wait_ge(S("pooled"), 4)
            gp.memset(Z[:, 0:8, :].rearrange("p h (c s) -> p (h c) s", s=SUB)[:, :, HALF:SUB], 0.0).then_inc(S("k0_zero"), 1)
            gp.wait_ge(S("mix_lo"), 1)
            gp.dma_start(chunks(W[:, 0:2 * BLK]).rearrange("p (a c) t -> p a (c t)", a=TT),
                         A["mem"].rearrange("o (a p) d -> p (o a) d", p=P)).then_inc(S("mem_in"), 16)
            gp.wait_ge(S("r_mm"), TT)
            wa = A["w_ada_2"].rearrange("l (c p) (u n) -> l u p c n", p=P, n=BLK)
            with gp.Fori(0, N_EXP) as e:
                for q in range(N_SUMS):
                    gp.wait_ge(ada_used[q % 2], e * (N_SUMS // 2) + q // 2)
                    gp.dma_start(ADA[:, q % 2:q % 2 + 1, :], wa[q // 3, q % 3][:, bass.ds(e, 1), :]).then_inc(ada_full[q % 2], 16)
            bias = W[:, 0:2 * BLK].rearrange("p (q h k) -> p q h k", q=TT, k=T)
            mask = const("na_mask")
            for l in range(LAYERS):
                gp.wait_ge(S("hid_free"), 1) if l == 0 else gp.wait_ge(S("conv_done"), l)
                rb = A["na_rel_bias_2"]
                for h in range(HEADS):
                    for r in range(T // GRID_W):
                        src = bass.AP(rb.tensor, ((l * HEADS + h) * REL_H + NA_KH - 1 - r) * REL_W + NA_KW - GRID_W,
                                      [[1, GRID_W], [REL_W, T // GRID_W], [1, GRID_W]])
                        q = r * GRID_W % P
                        dst = bias[q:q + GRID_W, r * GRID_W // P, h].rearrange("p (a k) -> p a k", k=GRID_W)
                        gp.dma_start(dst, src).then_inc(S("bias_in"), 16)
                gp.wait_ge(S("bias_in"), 16 * HEADS * (T // GRID_W) * (l + 1))
                gp.wait_ge(S("consts"), 16)
                for q in range(TT):
                    gp.tensor_tensor(bias[:, q], bias[:, q], mask[:, None, :].broadcast_to([P, HEADS, T]), ALU.add).then_inc(S("bias_masked"), 1)

        @block.scalar
        def _(act):
            def split(ph, j, i=0):
                b, s = at[ph][0] + j, at[ph][1] + j
                act.wait_ge(raw_full[b % RAW], 16 * (b // RAW + 1) + 16 * i)
                act.wait_ge(block_done[s % SPL], s // SPL + 2 * i)
                act.activation(w_hi[:, s % SPL, :], raw[:, b % RAW, :], ACT.Copy, scale=W_SCALE).then_inc(hi_done, 1)

            def linear(ph, z=None):
                def evict(u, i):
                    done(act, ph, 2 * u + 1, i)
                    act.activation(Z[:, bass.ds(i * 4 + z + 2 * u, 2), :], GB[:, u, :].rearrange("p (c t) -> p c t", t=T),
                                   ACT.Copy, scale=INV).then_inc(bank_free[u], 1)

                def body(i, first):
                    for u in range(2):
                        split(ph, 2 * u, i)
                        split(ph, 2 * u + 1, i)
                        if z is not None and not (first and u == 0):
                            evict(1 - u, i - 1 + u)
                n = at[ph][2] // 4
                body(0, True)
                with act.Fori(1, n) as i:
                    body(i, False)
                if z is not None:
                    evict(1, n - 1)

            def norm_sq(n, src, squares=Zn):
                act.activation(squares, src, ACT.Square).then_inc(S("norm_sq"), 1)
                act.wait_ge(S("norm_var"), n + 1)
                act.activation(nstd, ssum, ACT.Sqrt).then_inc(S("norm_std"), 1)

            def norm_parts(k):
                for g in range(4):
                    act.wait_ge(S("norm_h"), 4 * k + g + 1)
                    act.activation(xh[:, 4 * g:4 * g + 4, :], Zn[:, 4 * g:4 * g + 4, :], ACT.Copy).then_inc(S("norm_hi"), 1)

            def mix_parts(k, name, n):
                act.wait_ge(S(name), n)
                act.activation(xh, Y[:, :, :], ACT.Copy).then_inc(S("mix_hi"), 1)

            for g in range(ROW_TILES):
                act.wait_ge(S("rows_t"), g + 1)
                act.activation(PCt[:, g, :], MB[:, g % 4, 0:P], ACT.Copy).then_inc(S("cols"), 1)
            act.wait_ge(S("cols"), ROW_TILES)
            act.activation(SM[:, 24:40], col("c_2", 0, 16), ACT.Silu).then_inc(S("c_silu"), 1)
            for g in range(8):
                act.wait_ge(S("x_tr"), g + 1)
                act.activation(XT[:, g % 4 * 4:g % 4 * 4 + 4, g // 4 * P:g // 4 * P + P],
                               MB[:, g % 4, :].rearrange("p (c t) -> p c t", t=P), ACT.Copy).then_inc(S("x_t"), 1)
            act.wait_ge(S("x_t"), 8)
            act.wait_ge(S("fills"), 2)
            norm_sq(0, XT[:, :, :])
            norm_parts(0)
            linear("w_in", 0)

            read_out(act, "pool_w")
            act.activation(Z[:, 16:24, :], Z[:, 16:24, :], ACT.Sigmoid).then_inc(S("f_sig"), 1)
            act.wait_ge(S("cols"), ROW_TILES)
            act.wait_ge(S("lb_diff"), 1)
            act.activation(SM[:, 8:16], SM[:, 0:8], ACT.Sigmoid).then_inc(S("lb"), 1)
            act.activation(SM[:, 16:24], SM[:, 0:8], ACT.Sigmoid, scale=-1.0).then_inc(S("lb"), 1)
            act.activation(Z[:, 8:16, :], Z[:, 8:16, :], ACT.Silu).then_inc(S("q_silu"), 1)
            act.activation(Z[:, 32:40, :], Z[:, 32:40, :], ACT.Silu).then_inc(S("g_silu"), 1)
            for g in range(4):
                act.wait_ge(S("v_tr"), g + 1)
                act.activation(Z[:, 40 + 2 * g:42 + 2 * g, :].rearrange("p c t -> p (c t)"), MB[:, g, :], ACT.Copy).then_inc(S("v_rows"), 1)
            act.wait_ge(S("k_ready"), 1)
            act.activation(Z[:, 16:24, :], Z[:, 16:24, :], ACT.Ln).then_inc(S("log_f"), 1)
            for c in range(8):
                act.wait_ge(S("pool_mm"), 1)
                act.activation(Y[:, c, :], MB[:, c // 2, c % 2 * T:c % 2 * T + T], ACT.Copy, scale=col("pool_scale", c)).then_inc(S("pool_out"), 1)
            F = Z[:, 16:24, :].rearrange("p h t -> p (h t)")
            EO = Z[:, 48:52, :].rearrange("p h t -> p (h t)")
            Y1 = Y[:, 8:16, :].rearrange("p h t -> p (h t)")
            act.wait_ge(S("exponents"), 3)
            act.activation(w2, F, ACT.Exp).then_inc(S("exp_q"), 1)
            act.wait_ge(S("exp_q"), 1)
            act.activation(F, F, ACT.Exp, scale=-1.0).then_inc(S("exp_k"), 1)
            act.activation(EO, EO, ACT.Exp).then_inc(S("exp_k"), 1)
            act.activation(Y1, Y1, ACT.Exp).then_inc(S("exp_k"), 1)
            act.activation(H0, w1, ACT.Exp).then_inc(S("exp_a"), 1)
            act.wait_ge(S("state_k"), 1)
            for g in range(4):
                act.wait_ge(S("kt_tr"), g + 1)
                act.activation(w0[:, g * 512:g * 512 + 512], MB[:, 2 + g % 2, :], ACT.Copy).then_inc(S("kt_rows"), 1)
            Fh = Z[:, 16:24, :]
            for a in range(TT):
                act.wait_ge(S("o_done"), a + 1)
                act.activation(Fh[:, :, a * P:a * P + P], MB[:, 0:2, :].rearrange("p b (h t) -> p (b h) t", t=P), ACT.Copy).then_inc(S("o_copied"), 1)
            act.wait_ge(S("o_copied"), TT)
            act.activation(Z[:, 0:8, :], Fh, ACT.Square).then_inc(S("o_sq"), 1)
            act.wait_ge(S("o_var"), 1)
            act.activation(Z[:, 24:32, :], Z[:, 0:8, :], ACT.Sqrt).then_inc(S("o_std"), 1)
            mix_parts(0, "hgrn_y", 1)
            linear("w_out")

            for g in range(8):
                act.wait_ge(S("x_tr"), 8 + g + 1)
                act.activation(Y[:, g % 4 * 4:g % 4 * 4 + 4, g // 4 * P:g // 4 * P + P],
                               MB[:, g % 4, :].rearrange("p (c t) -> p c t", t=P), ACT.Copy).then_inc(S("x_t"), 1)
            act.wait_ge(S("x_t"), 16)
            norm_sq(1, Y[:, :, :])
            norm_parts(1)
            linear("wk", 0)
            linear("wv", 16)
            read_out(act, "wk")
            norm_sq(2, XT[:, :, :])
            norm_parts(2)
            linear("wq", 32)
            p = w2.rearrange("p (b a k) -> p b a k", b=4, k=T)
            pT = w3.rearrange("p (b a k) -> p b a k", b=4, k=T)
            for g in range(8):
                act.wait_ge(S("xv_tr"), g + 1)
                act.activation(W[:, g * 512:g * 512 + 512], MB[:, 2 + g % 2, :], ACT.Copy).then_inc(S("xv_rows"), 1)
            for h in range(X_HEADS):
                act.wait_ge(S("x_max"), h + 1)
                for a in range(TT):
                    act.activation(p[:, h, a, :], MB[:, h % 2, a * T:a * T + T], ACT.Exp, bias=NAS[:, 4 * h + a:4 * h + a + 1],
                                   scale=X_DH ** -0.5, accum_out=NAS[:, 4 * h + 2 + a:4 * h + 3 + a]).then_inc(S("x_exp"), 1)
            for h in range(X_HEADS):
                act.wait_ge(S("x_ptr"), h + 1)
                act.activation(pT[:, h], MB[:, 2, :].rearrange("p (a k) -> p a k", k=T), ACT.Copy).then_inc(S("x_pt"), 1)
                for b in range(2):
                    act.wait_ge(S("x_o"), 2 * h + b + 1)
                    act.activation(Y[:, 4 * h + 2 * b:4 * h + 2 * b + 2, :], MB[:, b, :].rearrange("p (a k) -> p a k", k=T), ACT.Copy).then_inc(S("x_y"), 1)
            act.wait_ge(S("x_y"), 8)
            mix_parts(1, "x_y", 8)
            linear("wo")
            read_out(act, "moe")
            norm_sq(3, XT[:, :, :])
            norm_parts(3)
            for a in range(TT):
                act.wait_ge(S("r_mm"), TT)
                act.activation(RT[:, 20 * a:20 * a + 20], MB[:, 1, 20 * a:20 * a + 20], ACT.Copy).then_inc(S("r_logits"), 1)
            act.wait_ge(S("r_exp_in"), 1)
            act.activation(RT[:, 48:56], RT[:, 48:56], ACT.Exp).then_inc(S("r_exp"), 1)
            act.wait_ge(S("r_exp_in"), 2)
            act.activation(RT[:, 116:118], RT[:, 116:118], ACT.Exp).then_inc(S("r_exp"), 1)
            act.wait_ge(S("r_tr"), 1)
            act.activation(RT[0:16, 136:392], MB[0:16, 1, 0:T], ACT.Copy).then_inc(S("r_t"), 1)
            comb = Y
            for g in range(8):
                act.wait_ge(S("r_bc"), g + 1)
                act.activation(comb[:, 2 * g:2 * g + 2, :], MB[:, 2 + g % 2, :].rearrange("p (a k) -> p a k", k=T), ACT.Copy).then_inc(S("comb"), 1)
            sg = w0[:, 0:1024].rearrange("p (u c t) -> p u c t", u=2, t=T)
            hid = w0[:, 1024:2048].rearrange("p (u c t) -> p u c t", u=2, t=T)
            hh = w2[:, 0:512].bitcast(F16).rearrange("p (c t) -> p c t", t=T)
            with act.Fori(0, N_EXP) as e:
                i = e * 3

                def silu(u):
                    done(act, "moe", 4 * u + 1, i)
                    act.activation(sg[:, u], GB[:, 2 * u, :].rearrange("p (c t) -> p c t", t=T), ACT.Silu, scale=INV).then_inc(bank_free[2 * u], 1)

                def hid_hi(u):
                    act.wait_ge(S("hid"), e * 2 + u + 1)
                    act.activation(hh[:, 2 * u:2 * u + 2, :], hid[:, u], ACT.Copy).then_inc(S("hid_hi"), 1)
                for j in range(12):
                    split("moe", j, i) if j < 4 else split("moe", j % 4, i + j // 4)
                    if j == 3:
                        silu(0)
                    if j == 6:
                        hid_hi(0)
                    if j == 7:
                        silu(1)
                    if j == 9:
                        hid_hi(1)
            read_out(act, "z0")
            norm_sq(4, XT[:, :, :], Y[:, :, :])

            act.wait_ge(S("logits_in"), 32)
            act.wait_ge(S("lg_abs"), 1)
            act.activation(LG[:, 64:96], LG[:, 32:64], ACT.Exp, scale=-1.0).then_inc(S("lg_exp"), 1)
            act.wait_ge(S("lg_u"), 1)
            act.activation(RT[:, 64:96], LG[:, 32:64], ACT.Ln).then_inc(S("lg_ln"), 1)
            for l in range(LAYERS):
                act.wait_ge(S("x_ready"), l + 1)
                norm_sq(5 + l, XT[:, :, :])
                norm_parts(4 + l)
                linear(f"z{l}", 0)
                read_out(act, f"fft{l}")
                act.activation(Z[:, 44:48, :], Z[:, 44:48, :], ACT.Sigmoid).then_inc(S("b_sig"), 1)
                for g, c in enumerate((4, 20, 36, 48)):
                    act.activation(Z[:, c:c + 4, :], Z[:, c:c + 4, :], ACT.Silu).then_inc(S("gates"), 1)
                nv = w3[:, 1024:2048].rearrange("p (a n) -> p a n", a=TT)
                rv = w3[:, 0:1024].rearrange("p (a n) -> p a n", a=TT)
                for k, dst in enumerate((nv, rv)):
                    for a in range(TT):
                        act.wait_ge(S("zv_tr"), 4 * l + 2 * k + a + 1)
                        act.activation(dst[:, a, :], MB[:, 2 * k + a, :], ACT.Copy).then_inc(S("zv_rows"), 1)
                fa = w2.rearrange("p (b n) -> p b n", n=512)
                for b in range(4):
                    act.wait_ge(S("fft_ch"), 4 * l + b + 1)
                    act.activation(fa[:, b, :], MB[:, b, :], ACT.Copy).then_inc(S("fft_a"), 1)
                fy = Z[:, 0:4, :]
                for b in range(2):
                    act.wait_ge(S("fft_tok"), 2 * l + b + 1)
                    act.activation(fy[:, 2 * b:2 * b + 2, :], MB[:, b, :].rearrange("p (a k) -> p a k", k=T), ACT.Copy).then_inc(S("fft_y"), 1)
                for h in range(HEADS):
                    pr = w2[:, h % 2 * 512:h % 2 * 512 + 512].rearrange("p (a k) -> p a k", k=T)
                    pt = w2[:, 1024 + h % 2 * 512:1536 + h % 2 * 512]
                    act.wait_ge(S("na_max"), 8 * l + h + 1)
                    for a in range(TT):
                        act.activation(pr[:, a, :], MB[:, h % 2, a * T:a * T + T], ACT.Exp, scale=DH ** -0.5, bias=NAS[:, 4 * (h % 2) + a:4 * (h % 2) + a + 1],
                                       accum_out=NAS[:, 4 * (h % 2) + 2 + a:4 * (h % 2) + 3 + a]).then_inc(S("na_exp"), 1)
                    act.wait_ge(S("na_ptr"), 8 * l + h + 1)
                    act.activation(pt, MB[:, 2, :], ACT.Copy).then_inc(S("na_pt"), 1)
                for h in range(HEADS):
                    dt = w2[:, h % 2 * 512:h % 2 * 512 + 512]
                    act.wait_ge(S("decay_e"), 8 * l + h + 1)
                    act.activation(dt, dt, ACT.Exp).then_inc(S("decay"), 1)
                act.wait_ge(S("ret_o"), 4 * l + 4)
                act.activation(Z[:, 8:12, :], Z[:, 28:32, :], ACT.Square).then_inc(S("ret_sq"), 1)
                act.wait_ge(S("ret_ms"), l + 1)
                act.activation(Z[:, 8:12, :].rearrange("p c t -> p (c t)"), MB[:, 0:2, :].rearrange("p b n -> p (b n)"), ACT.Sqrt,
                               bias=eps[:, :], scale=1.0 / DH).then_inc(S("ret_std"), 1)
                act.wait_ge(S("conv_sum"), l + 1)
                act.activation(ssum, MB[:, 2, 0:T], ACT.Copy, scale=1.0 / 512).then_inc(S("conv_mean"), 1)
                act.wait_ge(S("conv_c"), l + 1)
                act.activation(Z[:, 16:20, :], Z[:, 12:16, :], ACT.Square).then_inc(S("conv_sq"), 1)
                act.wait_ge(S("conv_var"), l + 1)
                act.activation(nstd, MB[:, 3, 0:T], ACT.Sqrt, bias=eps[:, :], scale=1.0 / 512).then_inc(S("conv_std"), 1)
                act.wait_ge(S("conv_n"), 4 * l + 4)
                act.activation(Z[:, 12:16, :], Z[:, 12:16, :], ACT.Silu).then_inc(S("conv_s"), 1)
                mix_parts(2 + l, "mixed", 4 * l + 4)
                linear(f"mix{l}")
            read_out(act, "end")
            norm_sq(7, XT[:, :, :])
            for g in range(8):
                act.wait_ge(S("out_tr"), g + 1)
                act.activation(W[:, g * 512:g * 512 + 512], MB[:, g % 4, :], ACT.Copy).then_inc(S("out_rows"), 1)

        @block.vector
        def _(dve):
            steps = [0]

            def link(ins, wait=True):
                steps[0] += 1
                ins.then_inc(S("dve_step"), 1)
                if wait:
                    dve.wait_ge(S("dve_step"), steps[0])

            def split(ph, j, i=0):
                b, s = at[ph][0] + j, at[ph][1] + j
                dve.wait_ge(hi_done, s + 1 + 4 * i)
                dve.scalar_tensor_tensor(w_lo[:, s % SPL, :], raw[:, b % RAW, :], W_SCALE, w_hi[:, s % SPL, :],
                                         ALU.mult, ALU.subtract).then_inc(raw_taken[b % RAW], 1)

            def linear(ph, add=False, gate=None):
                def evict(u, i):
                    done(dve, ph, 2 * u + 1, i)
                    if gate is None:
                        x = XT[:, bass.ds(i * 4 + 2 * u, 2), :]
                        dve.scalar_tensor_tensor(x, GB[:, u, :].rearrange("p (c t) -> p c t", t=T), INV, x,
                                                 ALU.mult, ALU.add).then_inc(bank_free[u], 1)
                        return
                    for k in range(2):
                        x = XT[:, bass.ds(i * 4 + 2 * u + k, 1), :]
                        ins = dve.scalar_tensor_tensor(x, GB[:, u:u + 1, k * T:k * T + T], gate[:, bass.ds(i * 4 + 2 * u + k, 1)], x,
                                                       ALU.mult, ALU.add)
                    ins.then_inc(bank_free[u], 1)

                def body(i, first):
                    for u in range(2):
                        split(ph, 2 * u, i)
                        split(ph, 2 * u + 1, i)
                        if add and not (first and u == 0):
                            evict(1 - u, i - 1 + u)
                n = at[ph][2] // 4
                body(0, True)
                with dve.Fori(1, n) as i:
                    body(i, False)
                if add:
                    evict(1, n - 1)

            def inverse_root(r, root, v):
                link(dve.reciprocal(r, root))
                link(dve.tensor_tensor(root, r, r, ALU.mult))
                link(dve.scalar_tensor_tensor(root, root, -0.5, v, ALU.mult, ALU.mult))
                link(dve.scalar_tensor_tensor(r, root, 1.5, r, ALU.add, ALU.mult))

            def norm(n, src, gain, parts=None, dst=None, shift=None, squares=Zn):
                dve.wait_ge(S("norm_sq"), n + 1)
                dve.tensor_reduce(ssum, squares.rearrange("p c t -> p t c"), AX.X, ALU.add).then_inc(S("norm_sum"), 1)
                dve.wait_ge(S("norm_ms"), n + 1)
                dve.tensor_scalar(ssum, MB[:, 0, 0:T], 1.0 / D, EPS, ALU.mult, ALU.add).then_inc(S("norm_var"), 1)
                dve.wait_ge(S("norm_std"), n + 1)
                inverse_root(rstd, nstd, ssum)
                dst = Zn if dst is None else dst
                for g in range(4):
                    for c in range(4 * g, 4 * g + 4):
                        ins = dve.scalar_tensor_tensor(dst[:, c, :], src[:, c, :], gain(c), rstd, ALU.mult, ALU.mult)
                        if shift is not None:
                            link(ins)
                            ins = dve.tensor_scalar(dst[:, c, :], dst[:, c, :], shift(c), None, ALU.add)
                    ins.then_inc(S("norm_h" if parts is not None else f"norm_out{n}"), 1)
                if parts is not None:
                    for g in range(4):
                        dve.wait_ge(S("norm_hi"), 4 * parts + g + 1)
                        dve.tensor_tensor(xl[:, 4 * g:4 * g + 4, :], Zn[:, 4 * g:4 * g + 4, :], xh[:, 4 * g:4 * g + 4, :],
                                          ALU.subtract).then_inc(S("norm_lo"), 1)

            def mix_parts(k):
                dve.wait_ge(S("mix_hi"), k + 1)
                dve.tensor_tensor(xl, Y[:, :, :], xh, ALU.subtract).then_inc(S("mix_lo"), 1)

            dve.wait_ge(S("cols"), ROW_TILES)
            dve.tensor_tensor(SM[:, 0:8], col("hgrn_lb_logits", 0, 8), col("hgrn_lb_logits", 8, 8), ALU.subtract).then_inc(S("lb_diff"), 1)
            norm(0, XT, lambda c: col("norm_mix", c), parts=0)
            linear("w_in")

            read_out(dve, "pool_w")
            dve.wait_ge(S("consts"), 16)
            dve.wait_ge(S("counts_in"), 16)
            u = Z[:, 0:8, :]
            src, sums = u, []
            for k in range(4):
                dst = chunks((w0, w1)[k % 2])
                d = 1 << k
                link(dve.tensor_copy(dst[:, 2 * k:, 0:d], src[:, 2 * k:, 0:d]), wait=False)
                link(dve.tensor_tensor(dst[:, 2 * k:, d:], src[:, 2 * k:, d:], src[:, 2 * k:, 0:T - d], ALU.add))
                sums.append(dst[:, 2 * k:2 * k + 2, :])
                src = dst
            count = Z[:, 48:52, :]
            for g in range(4):
                link(dve.tensor_tensor(sums[g], sums[g], count[:, g:g + 1, :].broadcast_to([P, 2, T]), ALU.mult))
                dve.tensor_tensor(chunks(H0)[:, 2 * g:2 * g + 2, :], sums[g], u[:, 2 * g:2 * g + 2, :], ALU.subtract).then_inc(S("pooled"), 1)

            Fh = Z[:, 16:24, :]
            F = Fh.rearrange("p h t -> p (h t)")
            Q = Z[:, 8:16, :].rearrange("p h t -> p (h t)")
            dve.wait_ge(S("f_sig"), 1)
            dve.wait_ge(S("lb"), 2)
            for h in range(HEADS):
                link(dve.tensor_scalar(Fh[:, h, :], Fh[:, h, :], SM[:, 16 + h:17 + h], SM[:, 8 + h:9 + h], ALU.mult, ALU.add), wait=h == HEADS - 1)
            dve.wait_ge(S("pooled"), 4)
            dve.tensor_scalar(w0, F, -1.0, 1.0, ALU.mult, ALU.add).then_inc(S("k_ready"), 1)
            dve.wait_ge(S("log_f"), 1)

            def by_chunk(ap):
                return ap.rearrange("p (g s) -> p g s", s=SUB)
            src = by_chunk(F)
            for k in range(5):
                dst = by_chunk(w1 if k % 2 == 0 else F)
                d = 1 << k
                link(dve.tensor_copy(dst[:, :, 0:d], src[:, :, 0:d]), wait=False)
                link(dve.tensor_tensor(dst[:, :, d:], src[:, :, d:], src[:, :, 0:SUB - d], ALU.add))
                src = dst
            a = by_chunk(w1)
            ah = w1.rearrange("p (g s) -> p g s", s=HALF)
            EO = Z[:, 48:52, :].rearrange("p h t -> p (h t)").rearrange("p (g s) -> p g s", s=HALF)
            Y1 = Y[:, 8:16, :].rearrange("p h t -> p (h t)")
            NG = HEADS * NCH
            dve.tensor_tensor(F.rearrange("p (g s) -> p g s", s=HALF), ah, ah[:, :, HALF // 2 - 1:HALF // 2].broadcast_to([P, 2 * NG, HALF]),
                              ALU.subtract).then_inc(S("exponents"), 1)
            dve.tensor_tensor(EO, a[:, :, HALF + HALF // 2 - 1:HALF + HALF // 2].broadcast_to([P, NG, HALF]), a[:, :, 0:HALF], ALU.subtract).then_inc(S("exponents"), 1)
            dve.tensor_tensor(by_chunk(Y1), a[:, :, SUB - 1:SUB].broadcast_to([P, NG, SUB]), a, ALU.subtract).then_inc(S("exponents"), 1)
            k0 = by_chunk(Z[:, 0:8, :].rearrange("p h t -> p (h t)"))
            k1 = by_chunk(Z[:, 24:32, :].rearrange("p h t -> p (h t)"))
            kk = by_chunk(w0)
            dve.wait_ge(S("exp_q"), 1)
            dve.wait_ge(S("q_silu"), 1)
            dve.tensor_tensor(w2, w2, Q, ALU.mult).then_inc(S("q_intra"), 1)
            dve.wait_ge(S("exp_k"), 3)
            dve.wait_ge(S("k0_zero"), 1)
            dve.wait_ge(S("v_tr"), 4)
            fk = by_chunk(F)
            dve.tensor_tensor(k0[:, :, 0:HALF], kk[:, :, 0:HALF], fk[:, :, 0:HALF], ALU.mult).then_inc(S("k_intra"), 1)
            dve.tensor_tensor(k1[:, :, HALF:], kk[:, :, HALF:], fk[:, :, HALF:], ALU.mult).then_inc(S("k_intra"), 1)
            dve.tensor_tensor(k1[:, :, 0:HALF], kk[:, :, 0:HALF], EO, ALU.mult).then_inc(S("k_intra"), 1)
            dve.tensor_tensor(Y1, Y1, w0, ALU.mult).then_inc(S("state_k"), 1)
            dve.wait_ge(S("exp_a"), 1)
            dve.wait_ge(S("q_intra"), 1)
            dve.tensor_tensor(Q, Q, H0, ALU.mult).then_inc(S("q_inter"), 1)
            bd = w3.rearrange("p (a h t) -> p a h t", a=TT, t=P)
            causal = const("causal")
            dve.wait_ge(S("bd_zero"), 1)
            for t in range(TT):
                dve.wait_ge(S("scores"), t + 1)
                for c in range(4):
                    r = slice(SUB * c, SUB * c + SUB)
                    dve.tensor_tensor(bd[r, t, :, r], MB[r, t, 0:T].rearrange("p (h s) -> p h s", s=SUB),
                                      causal[r, None, :].broadcast_to([SUB, HEADS, SUB]), ALU.mult).then_inc(S("bd"), 1)
            dec = H0.rearrange("p (h t) -> p h t", t=T)
            st = w1.rearrange("p (b h v) -> p b h v", b=2, v=P)
            tmp = EO.rearrange("p g s -> p (g s)").rearrange("p (h v) -> p h v", v=P)
            dve.wait_ge(S("exp_a"), 1)
            for c in range(NCH - 1):
                kv = MB[:, 2:4, :].rearrange("p b (h v) -> p (b h) v", v=P)
                if c:
                    last = dec[:, :, c * SUB + SUB - 1:c * SUB + SUB]
                    dve.wait_ge(S("state"), c)
                    link(dve.tensor_tensor(tmp, st[:, c % 2], last.broadcast_to([P, HEADS, P]), ALU.mult))
                dve.wait_ge(S("kv"), c + 1)
                if c:
                    dve.tensor_tensor(st[:, (c + 1) % 2], tmp, kv, ALU.add).then_inc(S("state"), 1)
                else:
                    dve.tensor_copy(st[:, 1], kv).then_inc(S("state"), 1)
            R = Z[:, 24:32, :].rearrange("p h t -> p (h t)")
            VAR = Z[:, 0:8, :].rearrange("p h t -> p (h t)")
            dve.wait_ge(S("o_ms"), 1)
            dve.tensor_scalar(VAR, MB[:, :, :].rearrange("p b n -> p (b n)"), 1.0 / P, EPS, ALU.mult, ALU.add).then_inc(S("o_var"), 1)
            dve.wait_ge(S("o_std"), 1)
            inverse_root(w0, R, VAR)
            R = w0
            link(dve.scalar_tensor_tensor(Y1, F, col("hgrn_norm"), R, ALU.mult, ALU.mult))
            dve.wait_ge(S("g_silu"), 1)
            dve.wait_ge(S("pool_out"), 8)
            dve.tensor_tensor(Y1, Y1, Z[:, 32:40, :].rearrange("p h t -> p (h t)"), ALU.mult).then_inc(S("hgrn_y"), 1)
            mix_parts(0)
            linear("w_out", add=True)

            norm(1, Y, lambda c: col("norm_mem", c), parts=1)
            linear("wk")
            linear("wv")
            norm(2, XT, lambda c: col("norm_xattn", c), parts=2)
            linear("wq")
            p = w2.rearrange("p (b a k) -> p b a k", b=4, k=T)
            for h in range(X_HEADS):
                dve.wait_ge(S("x_sc"), h + 1)
                m = NAS[:, 4 * h:4 * h + 2]
                link(dve.tensor_reduce(m, MB[:, h % 2, :].rearrange("p (a k) -> p a k", k=T), AX.X, ALU.max))
                dve.tensor_scalar(m, m, -(X_DH ** -0.5), None, ALU.mult).then_inc(S("x_max"), 1)
                dve.wait_ge(S("x_exp"), 2 * h + 2)
                s = NAS[:, 4 * h + 2:4 * h + 4]
                link(dve.reciprocal(s, s))
                for t in range(TT):
                    dve.tensor_scalar(p[:, h, t, :], p[:, h, t, :], s[:, t:t + 1], None, ALU.mult).then_inc(S("x_p"), 1)
            mix_parts(1)
            linear("wo", add=True)
            norm(3, XT, lambda c: col("norm_ffn", c), parts=3)

            def v2(a, n):
                return RT[:, a:a + 2 * n].rearrange("p (t n) -> p t n", t=2)

            def spread(ap, n):
                return ap.broadcast_to([P, 2, n])
            lg = RT[:, 0:40].rearrange("p (t n) -> p t n", t=2)
            lgg = lg[:, :, 0:GROUPS]
            prio = const("prio")[:, None, :].broadcast_to([P, 2, 4])
            mx, shift, ssm, pg, eq, gsel = v2(40, 1), v2(48, 4), v2(56, 1), v2(58, 1), v2(60, 4), v2(68, 4)
            sel, m1, oh1, sel2, m2, oh2 = v2(76, 4), v2(84, 1), v2(86, 4), v2(94, 4), v2(102, 1), v2(104, 4)
            gap, den, wa, wb, ce = v2(116, 1), v2(118, 1), v2(120, 1), v2(122, 1), v2(124, 4)
            big = CMB[:, :].rearrange("p (t g e) -> p t g e", t=2, e=4)
            dve.wait_ge(S("r_logits"), 2)

            def first_max(dst, vals, m):
                link(dve.tensor_reduce(m, vals, AX.X, ALU.max))
                link(dve.tensor_tensor(eq, vals, spread(m, 4), ALU.is_ge))
                link(dve.tensor_tensor(eq, eq, prio, ALU.mult))
                link(dve.tensor_reduce(ssm, eq, AX.X, ALU.max))
                link(dve.tensor_tensor(dst, eq, spread(ssm, 4), ALU.is_ge))
            first_max(gsel, lgg, mx)
            dve.tensor_tensor(shift, lgg, spread(mx, 4), ALU.subtract).then_inc(S("r_exp_in"), 1)
            dve.wait_ge(S("r_exp"), 1)
            link(dve.tensor_reduce(ssm, shift, AX.X, ALU.add))
            link(dve.reciprocal(pg, ssm))
            for g in range(GROUPS):
                part = lg[:, :, GROUPS + 4 * g:GROUPS + 4 * g + 4]
                link(dve.tensor_tensor(big[:, :, g, :], part, spread(gsel[:, :, g:g + 1], 4), ALU.mult))
            link(dve.tensor_reduce(sel, big.rearrange("p t g e -> p t e g"), AX.X, ALU.add))
            first_max(oh1, sel, m1)
            link(dve.scalar_tensor_tensor(sel2, oh1, NEG, sel, ALU.mult, ALU.add))
            first_max(oh2, sel2, m2)
            dve.tensor_tensor(gap, m2, m1, ALU.subtract).then_inc(S("r_exp_in"), 1)
            dve.wait_ge(S("r_exp"), 2)
            link(dve.tensor_scalar(den, gap, 1.0, None, ALU.add))
            link(dve.reciprocal(wa, den))
            link(dve.tensor_tensor(wa, wa, pg, ALU.mult))
            link(dve.tensor_tensor(wb, wa, gap, ALU.mult))
            link(dve.tensor_tensor(oh1, oh1, spread(wa, 4), ALU.mult))
            link(dve.tensor_tensor(oh2, oh2, spread(wb, 4), ALU.mult))
            link(dve.tensor_tensor(ce, oh1, oh2, ALU.add))
            for g in range(GROUPS):
                dve.tensor_tensor(big[:, :, g, :], ce, spread(gsel[:, :, g:g + 1], 4), ALU.mult).then_inc(S("combine"), 1)

            sg = w0[:, 0:1024].rearrange("p (u c t) -> p u c t", u=2, t=T)
            hid = w0[:, 1024:2048].rearrange("p (u c t) -> p u c t", u=2, t=T)
            hh = w2[:, 0:512].bitcast(F16).rearrange("p (c t) -> p c t", t=T)
            hl = w2[:, 512:1024].bitcast(F16).rearrange("p (c t) -> p c t", t=T)
            comb = Y
            dve.wait_ge(S("comb"), 8)
            dve.wait_ge(S("c_silu"), 1)
            dve.wait_ge(S("norm_lo"), 16)
            dve.wait_ge(S("r_mm"), TT)

            def modulate(e, q, first):
                n = e * (N_SUMS // 2) + q // 2
                dve.wait_ge(ada_full[q % 2], n * 16 + 16)
                sums, w = SUMS[:, q * BLK:(q + 1) * BLK], ADA[:, q % 2, :]
                if first:
                    dve.tensor_scalar(sums, w, SM[:, 24:25], None, ALU.mult).then_inc(ada_used[q % 2], 1)
                    return
                dve.wait_ge(ada_used[q % 2], n - (N_SUMS // 2 - 1))
                dve.scalar_tensor_tensor(sums, w, SM[:, bass.ds(e + 24, 1)], sums, ALU.mult, ALU.add).then_inc(ada_used[q % 2], 1)

            def expert(e, first):
                i = e * 3
                base = uses["moe"]

                def lo(j):
                    split("moe", j % 4, i + j // 4)

                def make_hid(u):
                    done(dve, "moe", 3, i + u)
                    dve.wait_ge(bank_free[2 * u], 3 * e + base[2 * u] + 1)
                    step = e * 2 + u + 1
                    dve.tensor_tensor(sg[:, u], sg[:, u], comb[:, bass.ds(e, 1), :].broadcast_to([P, 2, T]), ALU.mult).then_inc(S("weighted"), 1)
                    dve.wait_ge(S("weighted"), step)
                    dve.scalar_tensor_tensor(hid[:, u], GB[:, 2 * u + 1, :].rearrange("p (c t) -> p c t", t=T), INV, sg[:, u],
                                             ALU.mult, ALU.mult).then_inc(S("hid"), 1)
                    dve.wait_ge(S("hid"), step)
                    dve.sem_inc(bank_free[2 * u + 1], 1)

                def hid_lo(u):
                    dve.wait_ge(S("hid_hi"), e * 2 + u + 1)
                    dve.tensor_tensor(hl[:, 2 * u:2 * u + 2, :], hid[:, u], hh[:, 2 * u:2 * u + 2, :], ALU.subtract).then_inc(S("hid_lo"), 1)

                def add(j, i):
                    done(dve, "moe", j % 4, i + 2)
                    for q in range(2):
                        c = 4 * j + 2 * q
                        b = (2 * j + q) % 4
                        dve.scalar_tensor_tensor(XT[:, c:c + 2, :], GB[:, b, :].rearrange("p (c t) -> p c t", t=T), INV, XT[:, c:c + 2, :],
                                                 ALU.mult, ALU.add).then_inc(bank_free[b], 1)
                lo(0)
                modulate(e, 0, first)
                if not first:
                    add(2, i - 3)
                lo(1)
                if not first:
                    add(3, i - 3)
                for j in range(2, 12):
                    lo(j)
                    if j % 2 == 0:
                        modulate(e, j // 2, first)
                    if j == 5:
                        make_hid(0)
                    if j == 7:
                        hid_lo(0)
                    if j == 9:
                        make_hid(1)
                        hid_lo(1)
                    if j == 10:
                        add(0, i)
                    if j == 11:
                        add(1, i)
                return add
            expert(0, True)
            with dve.Fori(1, N_EXP) as e:
                expert(e, False)
            for j in (2, 3):
                i = 3 * (N_EXP - 1)
                done(dve, "moe", j % 4, i + 2)
                for q in range(2):
                    c, b = 4 * j + 2 * q, (2 * j + q) % 4
                    dve.scalar_tensor_tensor(XT[:, c:c + 2, :], GB[:, b, :].rearrange("p (c t) -> p c t", t=T), INV, XT[:, c:c + 2, :],
                                             ALU.mult, ALU.add).then_inc(bank_free[b], 1)
            norm(4, XT, lambda c: col("norm_final", c), dst=XT, squares=Y)
            dve.wait_ge(S("norm_out4"), 4)
            dve.sem_inc(S("hid_free"), 1)

            dve.wait_ge(S("logits_in"), 32)
            dve.scalar_tensor_tensor(LG[:, 32:64], LG[:, 0:32], -1.0, LG[:, 0:32], ALU.mult, ALU.max).then_inc(S("lg_abs"), 1)
            dve.wait_ge(S("lg_exp"), 1)
            y1p, y = LG[:, 32:64], LG[:, 64:96]
            dve.tensor_scalar(y1p, y, 1.0, None, ALU.add).then_inc(S("lg_u"), 1)
            dve.wait_ge(S("lg_u"), 1)
            um, isone = RT[:, 0:32], RT[:, 32:64]
            link(dve.tensor_scalar(um, y1p, -1.0, 1e-30, ALU.add, ALU.max))
            link(dve.reciprocal(um, um))
            link(dve.tensor_scalar(isone, y1p, 1.0, None, ALU.is_le))
            link(dve.tensor_tensor(isone, isone, y, ALU.mult))
            dve.wait_ge(S("lg_ln"), 1)
            link(dve.tensor_tensor(um, um, y, ALU.mult))
            link(dve.tensor_tensor(um, um, RT[:, 64:96], ALU.mult))
            link(dve.tensor_tensor(um, um, isone, ALU.add))
            link(dve.scalar_tensor_tensor(LG[:, 0:32], LG[:, 0:32], 0.0, um, ALU.min, ALU.subtract))

            for l in range(LAYERS):
                read_out(dve, f"z{l}")
                if l == 0:
                    dve.wait_ge(S("ada"), LAYERS)
                    link(dve.tensor_tensor(MOD[:, :, :].rearrange("p l c -> p (l c)"), MB[:, 1, 0:LAYERS * 3 * KC], col("b_ada_2", 0, LAYERS * 3 * KC), ALU.add))
                link(dve.scalar_tensor_tensor(GAIN[:, :], MOD[:, l, KC:2 * KC], 1.0, col("norm_g_2", KC * l, KC), ALU.add, ALU.mult))
                link(dve.tensor_scalar(MOD[:, l, 2 * KC:], MOD[:, l, 2 * KC:], INV, None, ALU.mult))
                dve.sem_inc(S("x_ready"), 1)
                norm(5 + l, XT, lambda c: GAIN[:, c:c + 1], parts=4 + l, shift=lambda c: MOD[:, l, c:c + 1])
                linear(f"z{l}")
                read_out(dve, f"fft{l}")
                cos, sin = const("rope_cos"), const("rope_sin")
                for c in range(8):
                    tmp = RO[:, c % 2, :]
                    dve.wait_ge(S("rot"), 8 * l + c + 1)
                    link(dve.tensor_tensor(tmp, MB[:, c % 2 + 2, 0:T], sin, ALU.mult))
                    link(dve.tensor_tensor(Z[:, 24 + c, :], Z[:, 24 + c, :], cos, ALU.mult))
                    dve.tensor_tensor(Z[:, 24 + c, :], Z[:, 24 + c, :], tmp, ALU.add).then_inc(S("rotated"), 1)
                pad = TAPS // 2
                up = CU
                link(dve.memset(up[:, :, 0:pad], 0.0), wait=False)
                link(dve.memset(up[:, :, pad + T:], 0.0), wait=False)
                dve.wait_ge(S("b_sig"), l + 1)
                link(dve.tensor_tensor(up[:, :, pad:pad + T], Z[:, 40:44, :], Z[:, 44:48, :], ALU.mult))
                dve.wait_ge(S("gates"), 4 * l + 4)
                dve.wait_ge(S("fft_w"), l + 1)
                dve.tensor_tensor(Y[:, 0:4, :], MB[:, 2:4, :].rearrange("p b (a k) -> p (b a) k", k=T), Z[:, 4:8, :], ALU.mult).then_inc(S("mixed"), 1)

                def na_gate(c):
                    dve.wait_ge(S("na_o"), 4 * l + c + 1)
                    ins = dve.tensor_tensor(Y[:, 4 + c, :], GB[:, c % 2, 0:T], Z[:, 20 + c, :], ALU.mult)
                    ins.then_inc(S("na_y"), 1)
                for h in range(HEADS):
                    pr = w2[:, h % 2 * 512:h % 2 * 512 + 512].rearrange("p (a k) -> p a k", k=T)
                    dve.wait_ge(S("na_sc"), 8 * l + h + 1)
                    m, s = NAS[:, 4 * (h % 2):4 * (h % 2) + 2], NAS[:, 4 * (h % 2) + 2:4 * (h % 2) + 4]
                    link(dve.tensor_reduce(m, MB[:, h % 2, :].rearrange("p (a k) -> p a k", k=T), AX.X, ALU.max))
                    dve.tensor_scalar(m, m, -(DH ** -0.5), None, ALU.mult).then_inc(S("na_max"), 1)
                    dve.wait_ge(S("na_exp"), 16 * l + 2 * h + 2)
                    link(dve.reciprocal(s, s))
                    for t in range(TT):
                        dve.tensor_scalar(pr[:, t, :], pr[:, t, :], s[:, t:t + 1], None, ALU.mult).then_inc(S("na_p"), 1)
                    if h % 2:
                        na_gate(h // 2)
                dve.wait_ge(S("na_y"), 4 * l + 4)
                dve.sem_inc(S("mixed"), 1)
                ahead, behind = const("ahead"), const("behind")
                for h in range(HEADS):
                    dt = w2[:, h % 2 * 512:h % 2 * 512 + 512]
                    pw = w2[:, 1024 + h % 2 * 512:1536 + h % 2 * 512]
                    if h >= 2:
                        dve.wait_ge(S("ret_pv"), 8 * l + h - 1)
                    link(dve.tensor_scalar(dt, behind, LG[:, 16 + 8 * l + h:17 + 8 * l + h], None, ALU.mult))
                    dve.scalar_tensor_tensor(dt, ahead, LG[:, 8 * l + h:8 * l + h + 1], dt, ALU.mult, ALU.add).then_inc(S("decay_e"), 1)
                    dve.wait_ge(S("decay"), 8 * l + h + 1)
                    dve.wait_ge(S("ret_sc"), 8 * l + h + 1)
                    dve.scalar_tensor_tensor(pw, MB[:, h % 2, :], DH ** -0.5, dt, ALU.mult, ALU.mult).then_inc(S("ret_p"), 1)
                    if h % 2:
                        c = h // 2
                        dve.wait_ge(S("ret_pv"), 8 * l + h + 1)
                        dve.tensor_copy(Z[:, 28 + c, :], GB[:, 2 + c % 2, 0:T]).then_inc(S("ret_o"), 1)
                r = Z[:, 8:12, :]
                dve.wait_ge(S("ret_std"), l + 1)
                link(dve.reciprocal(r, r))
                link(dve.tensor_tensor(Y[:, 8:12, :], Z[:, 28:32, :], r, ALU.mult))
                dve.tensor_tensor(Y[:, 8:12, :], Y[:, 8:12, :], Z[:, 36:40, :], ALU.mult).then_inc(S("mixed"), 1)
                ca = Z[:, 12:16, :]
                for k in range(TAPS):
                    for c in range(4):
                        wcol = col("conv_w_2", (l * TAPS + k) * 4 + c)
                        if k == 0:
                            link(dve.tensor_scalar(ca[:, c, :], up[:, c, 0:T], wcol, col("conv_b_2", 4 * l + c), ALU.mult, ALU.add), wait=False)
                        else:
                            dve.wait_ge(S("dve_step"), steps[0] - 3)
                            link(dve.scalar_tensor_tensor(ca[:, c, :], up[:, c, k:k + T], wcol, ca[:, c, :], ALU.mult, ALU.add), wait=False)
                dve.wait_ge(S("dve_step"), steps[0])
                dve.sem_inc(S("conv_a"), 1)
                dve.wait_ge(S("conv_mean"), l + 1)
                dve.tensor_tensor(ca, ca, ssum[:, None, :].broadcast_to([P, 4, T]), ALU.subtract).then_inc(S("conv_c"), 1)
                dve.wait_ge(S("conv_std"), l + 1)
                dve.wait_ge(S("conv_c"), l + 1)
                link(dve.reciprocal(rstd, nstd))
                link(dve.tensor_tensor(ca, ca, rstd[:, None, :].broadcast_to([P, 4, T]), ALU.mult))
                for c in range(4):
                    dve.tensor_scalar(ca[:, c, :], ca[:, c, :], col("conv_ln_g_2", 4 * l + c), col("conv_ln_b_2", 4 * l + c), ALU.mult, ALU.add).then_inc(S("conv_n"), 1)
                dve.wait_ge(S("conv_w"), l + 1)
                dve.tensor_tensor(Y[:, 12:16, :], MB[:, 0:2, :].rearrange("p b (a k) -> p (b a) k", k=T), Z[:, 48:52, :], ALU.mult).then_inc(S("mixed"), 1)
                dve.wait_ge(S("mixed"), 4 * l + 4)
                dve.sem_inc(S("conv_done"), 1)
                mix_parts(2 + l)
                linear(f"mix{l}", add=True, gate=MOD[:, l, 2 * KC:])
            norm(7, XT, lambda c: col("final_g_2", c))

        @block.tensor
        def _(pe):
            def product(ph, j, i, b, kc, k0, cols, uses_b, xs, start, stop):
                s = at[ph][1] + j
                x_hi, x_lo = xs
                hi = w_hi[:, s % SPL, :].rearrange("p (c n) -> p c n", c=kc)
                lo = w_lo[:, s % SPL, :].rearrange("p (c n) -> p c n", c=kc)
                for q, n in enumerate(cols):
                    o = GB[:, b, q * T:q * T + T]
                    for k in range(kc):
                        w, v = hi[:, k, n * P:n * P + P], lo[:, k, n * P:n * P + P]
                        first = start and q == 0 and k == 0
                        pe.matmul(o, w, x_hi[:, k0 + k, :], start=first, stop=False, skip_group_check=True)
                        pe.matmul(o, w, x_lo[:, k0 + k, :], start=False, stop=False, skip_group_check=True)
                        last = pe.matmul(o, v, x_hi[:, k0 + k, :], start=False, stop=stop and k == kc - 1, skip_group_check=True)
                return last

            def linear(ph):
                with pe.Fori(0, at[ph][2] // 4) as i:
                    for j in range(4):
                        s = at[ph][1] + j
                        taken(pe, ph, j, i)
                        if j % 2 == 0:
                            pe.wait_ge(bank_free[j // 2], uses[ph][j // 2] + i)
                        last = product(ph, j, i, j // 2, 8, j % 2 * 8, (0, 1), None, (xh, xl), j % 2 == 0, j % 2 == 1)
                        last.then_inc(block_done[s % SPL], 1)

            def norm(n):
                pe.wait_ge(S("norm_sum"), n + 1)
                pe.matmul(MB[:, 0, 0:T], ones[:, :], ssum, start=True, stop=True).then_inc(S("norm_ms"), 1)

            pe.wait_ge(S("consts"), 16)
            pe.wait_ge(S("rows_in"), 16 * N_LOADS)
            for g in range(ROW_TILES):
                if g >= 4:
                    pe.wait_ge(S("cols"), g - 3)
                pe.transpose(MB[:, g % 4, 0:P], PR[:, g, :], ident).then_inc(S("rows_t"), 1)

            def turn(src, ready, copied, before):
                for g in range(8):
                    pe.wait_ge(*before(g))
                    for k in range(4):
                        c = g % 4 * 4 + k
                        ins = pe.transpose(MB[:, g % 4, k * P:k * P + P], src[:, g // 4, c * P:c * P + P], ident)
                    ins.then_inc(S(ready), 1)
            rows = W[:, 0:2 * BLK].rearrange("p (a d) -> p a d", a=TT)
            pe.wait_ge(S("x_in"), 16)
            turn(rows, "x_tr", "x_t", lambda g: (S("cols"), ROW_TILES) if g < 4 else (S("x_t"), g - 3))
            pe.wait_ge(S("fills"), 2)
            norm(0)
            pe.wait_ge(S("norm_lo"), 4)
            linear("w_in")

            read_out(pe, "pool_w")
            for g in range(4):
                for k in range(4):
                    h = g % 2 * 4 + k
                    ins = pe.transpose(MB[:, g, k * P:k * P + P], Z[:, 24 + h, g // 2 * P:g // 2 * P + P], ident)
                ins.then_inc(S("v_tr"), 1)
            b = at["pool_w"][0]
            pe.wait_ge(raw_full[b % RAW], 16 * (b // RAW + 1))
            pe.wait_ge(S("pooled"), 4)
            pe.wait_ge(S("v_rows"), 4)
            pw = raw[:, b % RAW, :].rearrange("p (k n) -> p k n", n=T)
            pooled = chunks(H0)
            for g in range(4):
                for n in range(2):
                    for k in range(2):
                        ins = pe.matmul(MB[:, g, n * T:n * T + T], pw[:, 2 * g + k, n * P:n * P + P], pooled[:, 2 * g + k, :],
                                        start=n == 0 and k == 0, stop=k == 1, skip_group_check=True)
            ins.then_inc(raw_taken[b % RAW], 1)
            pe.wait_ge(raw_taken[b % RAW], b // RAW + 1)
            pe.sem_inc(S("pool_mm"), 1)
            k0 = Z[:, 0:8, :].rearrange("p h t -> p (h t)")
            k1 = Z[:, 24:32, :].rearrange("p h t -> p (h t)")
            pe.wait_ge(S("pool_out"), 8)
            pe.wait_ge(S("q_intra"), 1)
            pe.wait_ge(S("k_intra"), 3)
            for t in range(TT):
                for c in range(4):
                    r = slice(SUB * c, SUB * c + SUB)
                    for h in range(HEADS):
                        at_ = h * T + t * P + c * SUB
                        for half, k in enumerate((k0, k1)):
                            q = w2[:, at_ + half * HALF:at_ + half * HALF + HALF]
                            ins = pe.matmul(MB[r, t, h * SUB + half * HALF:h * SUB + half * HALF + HALF], k[:, at_:at_ + SUB], q,
                                            start=h == 0 and half == 0, stop=True, skip_group_check=True)
                ins.then_inc(S("scores"), 1)
            pe.wait_ge(S("state_k"), 1)
            for g in range(4):
                if g >= 2:
                    pe.wait_ge(S("kt_rows"), g - 1)
                for k in range(4):
                    h = g % 2 * 4 + k
                    ins = pe.transpose(MB[:, 2 + g % 2, k * P:k * P + P], Y[:, 8 + h, g // 2 * P:g // 2 * P + P], ident)
                ins.then_inc(S("kt_tr"), 1)
            V = Z[:, 40:48, :].rearrange("p c t -> p (c t)").rearrange("p (a h v) -> p a h v", a=TT, v=P)
            Kt = w0.rearrange("p (a h d) -> p a h d", a=TT, d=P)
            bd = w3.rearrange("p (a h t) -> p a h t", a=TT, t=P)
            st = w1.rearrange("p (b h v) -> p b h v", b=2, v=P)
            Q = Z[:, 8:16, :]
            pe.wait_ge(S("kt_rows"), 4)
            pe.wait_ge(S("bd"), 8)
            pe.wait_ge(S("q_inter"), 1)
            for t in range(TT):
                if t:
                    pe.wait_ge(S("o_copied"), t)
                for h in range(HEADS):
                    pe.matmul(MB[:, h // 4, h % 4 * P:h % 4 * P + P], V[:, t, h, :], bd[:, t, h, :], start=h % 4 == 0, stop=False, skip_group_check=True)
                for c in range(4):
                    n = 4 * t + c
                    r = slice(SUB * c, SUB * c + SUB)
                    if n:
                        pe.wait_ge(S("state"), n)
                    if n < NCH - 1:
                        for h in range(HEADS):
                            ins = pe.matmul(MB[:, 2 + h // 4, h % 4 * P:h % 4 * P + P], Kt[r, t, h, :], V[r, t, h, :],
                                            start=h % 4 == 0, stop=True, skip_group_check=True)
                        ins.then_inc(S("kv"), 1)
                    if n:
                        for h in range(HEADS):
                            ins = pe.matmul(MB[:, h // 4, h % 4 * P + c * SUB:h % 4 * P + c * SUB + SUB], st[:, n % 2, h, :],
                                            Q[:, h, n * SUB:n * SUB + SUB], start=False, stop=True, skip_group_check=True)
                ins.then_inc(S("o_done"), 1)
            pe.wait_ge(S("o_sq"), 1)
            for b in range(4):
                ins = pe.matmul(MB[:, b, :], ones[:, :], Z[:, 2 * b:2 * b + 2, :].rearrange("p h t -> p (h t)"), start=True, stop=True)
            ins.then_inc(S("o_ms"), 1)
            pe.wait_ge(S("mix_lo"), 1)
            linear("w_out")

            pe.wait_ge(S("mem_in"), 16)
            pe.wait_ge(S("o_std"), 1)
            turn(rows, "x_tr", "x_t", lambda g: (S("o_std"), 1) if g < 4 else (S("x_t"), 8 + g - 3))
            norm(1)
            pe.wait_ge(S("norm_lo"), 8)
            linear("wk")
            linear("wv")
            norm(2)
            pe.wait_ge(S("norm_lo"), 12)
            linear("wq")
            read_out(pe, "wo")
            K, V, Q = Z[:, 0:16, :], Z[:, 16:32, :], Z[:, 32:48, :]
            pe.wait_ge(S("norm_std"), 3)
            for g in range(8):
                if g >= 2:
                    pe.wait_ge(S("xv_rows"), g - 1)
                for k in range(4):
                    ins = pe.transpose(MB[:, 2 + g % 2, k * P:k * P + P], V[:, g % 4 * 4 + k, g // 4 * P:g // 4 * P + P], ident)
                ins.then_inc(S("xv_tr"), 1)
            Vs = W[:, 0:2 * BLK].rearrange("p (a d) -> p a d", a=TT)
            p = w2.rearrange("p (b a k) -> p b a k", b=4, k=T)
            pT = w3.rearrange("p (b a k) -> p b a k", b=4, k=T)
            for h in range(X_HEADS):
                if h >= 2:
                    pe.wait_ge(S("x_exp"), 2 * h - 2)
                for a in range(TT):
                    for c in range(4):
                        ins = pe.matmul(MB[:, h % 2, a * T:a * T + T], Q[:, 4 * h + c, a * P:a * P + P], K[:, 4 * h + c, :],
                                        start=a == 0 and c == 0, stop=c == 3, skip_group_check=True)
                ins.then_inc(S("x_sc"), 1)
            pe.wait_ge(S("xv_rows"), 8)
            for h in range(X_HEADS):
                pe.wait_ge(S("x_p"), 2 * h + 2)
                if h:
                    pe.wait_ge(S("x_pt"), h)
                for k in range(TT):
                    for a in range(TT):
                        ins = pe.transpose(MB[:, 2, k * T + a * P:k * T + a * P + P], p[:, h, a, k * P:k * P + P], ident)
                ins.then_inc(S("x_ptr"), 1)
                pe.wait_ge(S("x_pt"), h + 1)
                for b in range(2):
                    if h == 0:
                        pe.wait_ge(S("x_exp"), 8)
                    else:
                        pe.wait_ge(S("x_y"), 2 * h - 1 + b)
                    for c in range(2):
                        for k in range(TT):
                            d = h * X_DH + (2 * b + c) * P
                            ins = pe.matmul(MB[:, b, c * T:c * T + T], Vs[:, k, d:d + P], pT[:, h, k, :], start=c == 0 and k == 0, stop=k == 1, skip_group_check=True)
                    ins.then_inc(S("x_o"), 1)
            pe.wait_ge(S("mix_lo"), 2)
            linear("wo")
            norm(3)
            pe.wait_ge(S("norm_h"), 16)
            pe.wait_ge(S("router_in"), 32)
            for a in range(TT):
                for c in range(KC):
                    ins = pe.matmul(MB[:, 1, 20 * a:20 * a + 20], Zn[:, c, a * P:a * P + P], RW[:, c, :], start=a == 0 and c == 0, stop=c == KC - 1, skip_group_check=True)
                ins.then_inc(S("r_mm"), 1)
            pe.wait_ge(S("combine"), 4)
            pe.wait_ge(S("r_logits"), 2)
            for a in range(TT):
                ins = pe.transpose(MB[0:16, 1, a * P:a * P + P], CMB[:, 16 * a:16 * a + 16], ident)
            ins.then_inc(S("r_tr"), 1)
            pe.wait_ge(S("r_t"), 1)
            for g in range(8):
                if g >= 2:
                    pe.wait_ge(S("comb"), g - 1)
                for k in range(2):
                    e = 2 * g + k
                    ins = pe.matmul(MB[:, 2 + g % 2, k * T:k * T + T], ident[0:16, e:e + 1].broadcast_to([16, P]), RT[0:16, 136:392],
                                    start=k == 0, stop=True, skip_group_check=True)
                ins.then_inc(S("r_bc"), 1)
            pe.wait_ge(S("norm_lo"), 16)
            hh = w2[:, 0:512].bitcast(F16).rearrange("p (c t) -> p c t", t=T)
            hl = w2[:, 512:1024].bitcast(F16).rearrange("p (c t) -> p c t", t=T)
            with pe.Fori(0, N_EXP) as e:
                for j in range(12):
                    i = e * 3 + j // 4
                    s = at["moe"][1] + j
                    taken(pe, "moe", j % 4, i)
                    if j < 8:
                        b = j // 2
                        if j % 2 == 0:
                            pe.wait_ge(bank_free[b], uses["moe"][b] + 3 * e)
                        last = product("moe", j, e, b, 8, j % 2 * 8, (0, 1), None, (xh, xl), j % 2 == 0, j % 2 == 1)
                    else:
                        if j == 8:
                            pe.wait_ge(S("hid_lo"), e * 2 + 2)
                        for q in range(2):
                            b = (2 * j + q) % 4
                            pe.wait_ge(bank_free[b], uses["moe"][b] + 1 + (j - 8) // 2 + 3 * e)
                            last = product("moe", j, e, b, 4, 0, (2 * q, 2 * q + 1), None, (hh, hl), True, True)
                    last.then_inc(block_done[s % SPL], 1)
            def modulation(l):
                for j in range(2):
                    pe.wait_ge(ada_used[j], N_EXP * N_SUMS // 2)
                for n in range(3 * KC):
                    at_ = (l * 3 * KC + n) * P
                    ins = pe.matmul(MB[:, 1, l * 3 * KC + n:l * 3 * KC + n + 1], SUMS[:, at_:at_ + P], ones[:, 0:1],
                                    start=l == 0 and n == 0, stop=True, skip_group_check=True)
                ins.then_inc(S("ada"), 1)
            modulation(0)
            norm(4)
            modulation(1)

            for l in range(LAYERS):
                norm(5 + l)
                pe.wait_ge(S("norm_lo"), 20 + 4 * l)
                linear(f"z{l}")
                read_out(pe, f"fft{l}")
                pe.wait_ge(S("norm_std"), 6 + l)
                pe.wait_ge(S("x_ready"), l + 1)
                for k, z in enumerate((16, 32)):
                    for a in range(TT):
                        for c in range(4):
                            ins = pe.transpose(MB[:, 2 * k + a, c * P:c * P + P], Z[:, z + c, a * P:a * P + P], ident)
                        ins.then_inc(S("zv_tr"), 1)
                rot = const("rot")
                for c in range(8):
                    if c < 2:
                        pe.wait_ge(S("zv_rows"), 4 * l + 4)
                    else:
                        pe.wait_ge(S("rotated"), 8 * l + c - 1)
                    pe.matmul(MB[:, c % 2 + 2, 0:T], rot, Z[:, 24 + c, :], start=True, stop=True).then_inc(S("rot"), 1)
                pe.wait_ge(S("rotated"), 8 * l + 8)
                for a in range(TT):
                    for g in range(4):
                        ins = pe.matmul(MB[:, 2 * a + g // 2, g % 2 * T:g % 2 * T + T], Z[:, g, a * P:a * P + P], const("dft_ch"),
                                        start=g % 2 == 0, stop=True, skip_group_check=True)
                        if g % 2:
                            ins.then_inc(S("fft_ch"), 1)
                fa = w2.rearrange("p (a g n) -> p a g n", a=TT, g=4)
                dcos = const("dft_cos").rearrange("p (a t) -> p a t", t=T)
                dsin = const("dft_nsin").rearrange("p (a t) -> p a t", t=T)
                pe.wait_ge(S("fft_a"), 4 * l + 4)
                for g in range(4):
                    for a in range(TT):
                        for k, m in enumerate((dcos, dsin)):
                            ins = pe.matmul(MB[:, g // 2, g % 2 * T:g % 2 * T + T], fa[:, a, g, k * P:k * P + P], m[:, a, :],
                                            start=g % 2 == 0 and a == 0 and k == 0, stop=a == 1 and k == 1, skip_group_check=True)
                    if g % 2:
                        ins.then_inc(S("fft_tok"), 1)

                def small(ph, x, banks, ready):
                    b = at[ph][0]
                    pe.wait_ge(raw_full[b % RAW], 16 * (b // RAW + 1))
                    w = raw[:, b % RAW, :].rearrange("p (c n) -> p c n", n=512)
                    for n in range(4):
                        for k in range(4):
                            ins = pe.matmul(MB[:, banks + n // 2, n % 2 * T:n % 2 * T + T], w[:, k, n * P:n * P + P], x[:, k, :],
                                            start=n % 2 == 0 and k == 0, stop=k == 3, skip_group_check=True)
                    ins.then_inc(raw_taken[b % RAW], 1)
                    pe.wait_ge(raw_taken[b % RAW], b // RAW + 1)
                    pe.sem_inc(S(ready), 1)
                pe.wait_ge(S("fft_y"), 2 * l + 2)
                small(f"fft{l}", Z[:, 0:4, :], 2, "fft_w")
                nv = w3[:, 1024:2048].rearrange("p (a n) -> p a n", a=TT)

                def na_scores(h):
                    c, r = h // 2, slice(DH * (h % 2), DH * (h % 2) + DH)
                    if h < 2:
                        pe.wait_ge(S("fft_y"), 2 * l + 2)
                    else:
                        pe.wait_ge(S("na_exp"), 16 * l + 2 * h - 2)
                    for a in range(TT):
                        o = MB[:, h % 2, a * T:a * T + T]
                        pe.matmul(o, const("unflip"), bias[:, a, h, :], start=a == 0, stop=False, skip_group_check=True)
                        ins = pe.matmul(o, Z[r, 8 + c, a * P:a * P + P], Z[r, 12 + c, :], start=False, stop=True, skip_group_check=True)
                    ins.then_inc(S("na_sc"), 1)
                bias = W[:, 0:2 * BLK].rearrange("p (q h k) -> p q h k", q=TT, k=T)
                pe.wait_ge(S("bias_masked"), 2 * l + 2)
                pe.wait_ge(S("mixed"), 4 * l + 1)
                na_scores(0)
                for h in range(HEADS):
                    c, r = h // 2, slice(DH * (h % 2), DH * (h % 2) + DH)
                    if h + 1 < HEADS:
                        na_scores(h + 1)
                    pr = w2[:, h % 2 * 512:h % 2 * 512 + 512].rearrange("p (a k) -> p a k", k=T)
                    pt = w2[:, 1024 + h % 2 * 512:1536 + h % 2 * 512].rearrange("p (a k) -> p a k", k=T)
                    pe.wait_ge(S("na_p"), 16 * l + 2 * h + 2)
                    if h:
                        pe.wait_ge(S("na_pt"), 8 * l + h)
                    for k in range(TT):
                        for a in range(TT):
                            ins = pe.transpose(MB[:, 2, k * T + a * P:k * T + a * P + P], pr[:, a, k * P:k * P + P], ident)
                    ins.then_inc(S("na_ptr"), 1)
                    pe.wait_ge(S("na_pt"), 8 * l + h + 1)
                    if h % 2 == 0 and c >= 2:
                        pe.wait_ge(S("na_y"), 4 * l + c - 1)
                    for k in range(TT):
                        ins = pe.matmul(GB[r, c % 2, 0:T], nv[:, k, h * DH:h * DH + DH], pt[:, k, :], start=k == 0, stop=k == 1, skip_group_check=True)
                    if h % 2:
                        ins.then_inc(S("na_o"), 1)
                rv = w3[:, 0:1024].rearrange("p (a n) -> p a n", a=TT)

                def ret_scores(h):
                    c, r = h // 2, slice(DH * (h % 2), DH * (h % 2) + DH)
                    if h < 2:
                        pe.wait_ge(S("na_exp"), 16 * l + 16)
                    else:
                        pe.wait_ge(S("ret_p"), 8 * l + h - 1)
                    for a in range(TT):
                        ins = pe.matmul(MB[:, h % 2, a * T:a * T + T], Z[r, 28 + c, a * P:a * P + P], Z[r, 24 + c, :], start=a == 0, stop=True, skip_group_check=True)
                    ins.then_inc(S("ret_sc"), 1)
                pe.wait_ge(S("na_pt"), 8 * l + 8)
                ret_scores(0)
                for h in range(HEADS):
                    c, r = h // 2, slice(DH * (h % 2), DH * (h % 2) + DH)
                    if h + 1 < HEADS:
                        ret_scores(h + 1)
                    pw = w2[:, 1024 + h % 2 * 512:1536 + h % 2 * 512].rearrange("p (a k) -> p a k", k=T)
                    pe.wait_ge(S("ret_p"), 8 * l + h + 1)
                    if h % 2 == 0 and c >= 2:
                        pe.wait_ge(S("ret_o"), 4 * l + c - 1)
                    for k in range(TT):
                        ins = pe.matmul(GB[r, 2 + c % 2, 0:T], rv[:, k, h * DH:h * DH + DH], pw[:, k, :], start=k == 0, stop=k == 1, skip_group_check=True)
                    ins.then_inc(S("ret_pv"), 1)
                pe.wait_ge(S("ret_sq"), l + 1)
                for b in range(2):
                    ins = pe.matmul(MB[:, b, :], const("pair"), Z[:, 8 + 2 * b:10 + 2 * b, :].rearrange("p c t -> p (c t)"), start=True, stop=True)
                ins.then_inc(S("ret_ms"), 1)
                pe.wait_ge(S("conv_a"), l + 1)
                for c in range(4):
                    ins = pe.matmul(MB[:, 2, 0:T], ones[:, :], Z[:, 12 + c, :], start=c == 0, stop=c == 3)
                ins.then_inc(S("conv_sum"), 1)
                pe.wait_ge(S("conv_sq"), l + 1)
                pe.wait_ge(S("na_y"), 4 * l + 4)
                for c in range(4):
                    ins = pe.matmul(MB[:, 3, 0:T], ones[:, :], Z[:, 16 + c, :], start=c == 0, stop=c == 3)
                ins.then_inc(S("conv_var"), 1)
                pe.wait_ge(S("conv_s"), l + 1)
                pe.wait_ge(S("ret_std"), l + 1)
                small(f"pw{l}", Z[:, 12:16, :], 0, "conv_w")
                pe.wait_ge(S("mix_lo"), 3 + l)
                linear(f"mix{l}")
            norm(7)
            for g in range(8):
                pe.wait_ge(S("norm_out7"), g % 4 + 1)
                if g >= 4:
                    pe.wait_ge(S("out_rows"), g - 3)
                for k in range(4):
                    ins = pe.transpose(MB[:, g % 4, k * P:k * P + P], Zn[:, g % 4 * 4 + k, g // 4 * P:g // 4 * P + P], ident)
                ins.then_inc(S("out_tr"), 1)


def row_loads():
    n, loads = 0, 0
    for _, k in ROWS:
        r = 0
        while r < k:
            r += min(k - r, P - (n + r) % P)
            loads += 1
        n += k
    return loads


N_LOADS = row_loads()


INPUTS = ["x", "mem", "norm_mix", "w_in", "pool_w", "pool_scale", "hgrn_lb_logits", "hgrn_norm", "w_out",
          "norm_xattn", "norm_mem", "xattn_wq", "xattn_wk", "xattn_wv", "xattn_wo", "norm_ffn", "router_group",
          "router_expert", "w_gate", "w_up", "w_down", "norm_final", "c_2", "norm_g_2", "w_ada_2", "b_ada_2",
          "w_in_2", "w_fft_2", "na_rel_bias_2", "ret_logit_fwd_2", "ret_logit_bwd_2", "conv_w_2", "conv_b_2",
          "conv_ln_g_2", "conv_ln_b_2", "conv_w_pw_2", "w_out_2", "final_g_2"]


def lay_out(inputs, nc):
    tables = constants()
    arrays, A, const_at, at = {}, {}, {}, 0
    for name in INPUTS:
        arrays[name] = np.ascontiguousarray(inputs[name])
        A[name] = nc.dram_tensor(name, arrays[name].shape, F32, kind="ExternalInput").ap()
    for name, v in tables.items():
        const_at[name] = (at, v.shape[1])
        at += v.shape[1]
    arrays["table"] = np.concatenate(list(tables.values()), 1)
    arrays["window_counts"] = counts()
    table = nc.dram_tensor("table", arrays["table"].shape, F32, kind="ExternalInput").ap()
    window_counts = nc.dram_tensor("window_counts", arrays["window_counts"].shape, F32, kind="ExternalInput").ap()
    out = nc.dram_tensor("out", (1, T, D), F32, kind="ExternalOutput").ap()
    build(nc, A, table, const_at, window_counts, out)
    return arrays


def kernel(**inputs):
    from concourse import bacc
    from concourse.bass_utils import run_bass_kernel_spmd

    nc = bacc.Bacc("TRN2", target_bir_lowering=False, num_devices=1)
    arrays = lay_out(inputs, nc)
    r = run_bass_kernel_spmd(nc, [arrays], core_ids=[0])
    return r.results[0]["out"]
```

```python
from contextlib import ExitStack

import numpy as np

import concourse.bass as bass
from concourse import mybir

F32 = mybir.dt.float32
F16 = mybir.dt.float16
ALU = mybir.AluOpType
ACT = mybir.ActivationFunctionType
AX = mybir.AxisListType

P = 128
T = 256
TT = T // P
D = 2048
KC = D // P
EPS = 1e-6
W_SCALE = 256.0
BLK = 2048
RAW = 4
SPL = 2
POOL_WINDOWS = (2, 4, 8, 16)
HEADS = 8
SUB = 32
HALF = SUB // 2
NCH = T // SUB
X_HEADS = 4
X_DH = D // X_HEADS
GROUPS, PER_GROUP = 4, 4
N_EXP = GROUPS * PER_GROUP
D_EXP = 512
LAYERS = 2
PIECES = 13
EARLY = 10
N_SUMS = LAYERS * 3
GRID_W, NA_KW, NA_KH = 64, 16, 8
REL_H, REL_W = 2 * NA_KH - 1, 2 * NA_KW - 1
TAPS = 31
DH = 64
NEG = -1.0e30


def constants():
    p, t = np.arange(P), np.arange(T)
    out = {"ident": np.eye(P)}
    ang = 2 * np.pi * np.outer(p, p) / P
    out["dft_ch"] = np.concatenate([np.cos(ang), np.sin(ang)], 1)
    ang = 2 * np.pi * (np.outer(t, t) % T) / T
    norm = 1.0 / np.sqrt(T * P)
    for name, m in (("dft_cos", np.cos(ang) * norm), ("dft_nsin", -np.sin(ang) * norm)):
        out[name] = m.reshape(TT, P, T).transpose(1, 0, 2).reshape(P, TT * T)
    half = DH // 2
    inv = (np.float32(10000.0) ** (-np.arange(half, dtype=np.float32) / np.float32(half))).astype(np.float32)
    rope = (t.astype(np.float32)[None, :] * inv[p % half][:, None]).astype(np.float32)
    out["rope_cos"], out["rope_sin"] = np.cos(rope), np.sin(rope)
    rot = np.zeros((P, P))
    for m in range(P):
        if m % DH < half:
            rot[m + half, m] = -1.0
        else:
            rot[m - half, m] = 1.0
    out["rot"] = rot
    d = t[None, :] - t[:, None]
    for name, m in (("ahead", np.maximum(d, 0)), ("behind", np.maximum(-d, 0))):
        out[name] = m.reshape(TT, P, T).transpose(1, 0, 2).reshape(P, TT * T)
    c, k = GRID_W - 1 - p % GRID_W, t % GRID_W
    start = np.clip(c - NA_KW // 2, 0, GRID_W - NA_KW)
    rel = k[None, :] - start[:, None]
    out["na_mask"] = np.where((rel >= 0) & (rel < NA_KW), 0.0, NEG)
    out["unflip"] = ((p[:, None] // GRID_W == p[None, :] // GRID_W) & (p[:, None] % GRID_W == GRID_W - 1 - p[None, :] % GRID_W)) * DH ** 0.5
    out["causal"] = (p[:, None] % SUB <= np.arange(SUB)[None, :]) * 1.0
    out["prio"] = np.tile(np.arange(4, 0, -1), (P, 1))
    out["pair"] = (p[:, None] // DH == p[None, :] // DH) * 1.0
    return {n: np.ascontiguousarray(v, dtype=np.float32) for n, v in out.items()}


def counts():
    t = np.arange(T)
    return np.concatenate([np.tile(1.0 / np.minimum(t + 1, w), (P, 1)) for w in POOL_WINDOWS], 1).astype(np.float32)


ROWS = [("norm_mix", 16), ("pool_scale", 8), ("hgrn_lb_logits", 16), ("hgrn_norm", 1), ("norm_xattn", 16),
        ("norm_mem", 16), ("norm_ffn", 16), ("norm_final", 16), ("c_2", 16), ("norm_g_2", 32),
        ("b_ada_2", 96), ("conv_w_2", 248), ("conv_b_2", 8), ("conv_ln_g_2", 8), ("conv_ln_b_2", 8),
        ("final_g_2", 16)]
N_ROWS = sum(n for _, n in ROWS)
ROW_TILES = -(-N_ROWS // P)

STREAM = [("w_in", 40, True), ("pool_w", 1, False), ("w_out", 16, True), ("wk", 16, True), ("wv", 16, True),
          ("wq", 16, True), ("wo", 16, True), ("moe", 12 * N_EXP, True)]
for _l in range(LAYERS):
    STREAM += [(f"z{_l}", 52, True), (f"fft{_l}", 1, False), (f"pw{_l}", 1, False),
               (f"mix{_l}", 16, True)]


def places():
    out, b, s = {}, 0, 0
    for name, n, split in STREAM:
        out[name] = (b, s, n)
        b, s = b + n, s + n * split
    return out


def bank_uses():
    out, used = {}, [0] * 4
    for name, n, split in STREAM:
        out[name] = list(used)
        if name == "moe":
            used = [x + 3 * N_EXP for x in used]
        elif split:
            used = [used[0] + n // 4, used[1] + n // 4] + used[2:]
    out["end"] = used
    return out


def build(nc, A, table, const_at, window_counts, out, dbg=()):
    ctx = ExitStack()
    with ctx:
        def sb(name, shape, dt=F32):
            return ctx.enter_context(nc.sbuf_tensor(name, shape, dt))

        sems = {}

        def S(name):
            if name not in sems:
                sems[name] = ctx.enter_context(nc.semaphore(name))
            return sems[name]

        raw_full = [S(f"raw_full{j}") for j in range(RAW)]
        raw_taken = [S(f"raw_taken{j}") for j in range(RAW)]
        hi_done = S("hi_done")
        block_done = [S(f"block_done{j}") for j in range(SPL)]
        ada_full = [S(f"ada_full{j}") for j in range(2)]
        ada_used = [S(f"ada_used{j}") for j in range(2)]
        bank_free = [S(f"bank_free{j}") for j in range(4)]

        raw = sb("raw", [P, RAW, BLK])
        w_hi = sb("w_hi", [P, SPL, BLK], F16)
        w_lo = sb("w_lo", [P, SPL, BLK], F16)
        XT = sb("XT", [P, KC, T])
        H = sb("H", [P, 2 * BLK])
        xh = H[:, 0:BLK].bitcast(F16).rearrange("p (c t) -> p c t", t=T)
        xl = H[:, BLK:2 * BLK].bitcast(F16).rearrange("p (c t) -> p c t", t=T)
        H0 = H[:, 0:BLK]
        Z = sb("Z", [P, 52, T])
        Y = sb("Y", [P, KC, T])
        W = sb("W", [P, 4 * BLK])
        w0, w1, w2, w3 = (W[:, k * BLK:(k + 1) * BLK] for k in range(4))
        CT = sb("CT", [P, table.shape[1]])
        PR = w3[:, 0:ROW_TILES * P].rearrange("p (a b) -> p a b", b=P)
        PCt = sb("PCt", [P, ROW_TILES, P])
        PC = PCt[:, :, :].rearrange("p a b -> p (a b)")
        ones = sb("ones", [P, P])
        eps = sb("eps", [P, 1])
        NS = sb("NS", [P, 3, T])
        ssum, nstd, rstd = NS[:, 0, :], NS[:, 1, :], NS[:, 2, :]
        RW = sb("RW", [P, KC, GROUPS + N_EXP])
        RT = sb("RT", [P, 400])
        MOD = sb("MOD", [P, LAYERS, 3 * KC])
        GAIN = sb("GAIN", [P, KC])
        SM = sb("SM", [P, 64])
        LG = sb("LG", [P, 96])
        NAS = sb("NAS", [P, 32])
        CMB = sb("CMB", [P, TT * N_EXP])
        CU = Y[:, :, :].rearrange("p c t -> p (c t)")[:, 0:4 * (T + TAPS - 1)].rearrange("p (c t) -> p c t", c=4)
        ca, csq = Y[:, 12:16, :], Y[:, 8:12, :]
        RO = H[:, BLK:BLK + 2 * T].rearrange("p (c t) -> p c t", t=T)
        GB = ctx.enter_context(nc.psum_tensor("GB", [P, 4, 512], F32))
        MB = ctx.enter_context(nc.psum_tensor("MB", [P, 4, 512], F32))

        def const(name, rows=P):
            at, n = const_at[name]
            return CT[0:rows, at:at + n]

        ident = const("ident")
        row_at, n = {}, 0
        for name, k in ROWS:
            row_at[name] = n
            n += k

        def col(name, i=0, n=1):
            return PC[:, row_at[name] + i:row_at[name] + i + n]

        def chunks(ap):
            return ap.rearrange("p (c t) -> p c t", t=T)

        at = places()
        uses = bank_uses()
        Zn = Z[:, 32:48, :]
        SUMS = Z[:, 0:48, :].rearrange("p c t -> p (c t)")
        ADA = W[:, :].rearrange("p (a b n) -> p a b n", b=2, n=BLK)[:, :, 1, :]
        INV = 1.0 / W_SCALE

        def taken(eng, ph, j, i=0):
            b = at[ph][0] + j
            eng.wait_ge(raw_taken[b % RAW], b // RAW + 1 + i)

        def done(eng, ph, j, i=0):
            s = at[ph][1] + j
            eng.wait_ge(block_done[s % SPL], s // SPL + 1 + 2 * i)

        def read_out(eng, ph):
            for b in range(4):
                eng.wait_ge(bank_free[b], uses[ph][b])

        LIN = {"w_in": ("w_in", None), "w_out": ("w_out", None), "wk": ("xattn_wk", None), "wv": ("xattn_wv", None),
               "wq": ("xattn_wq", None), "wo": ("xattn_wo", None)}
        for l in range(LAYERS):
            LIN |= {f"z{l}": ("w_in_2", l), f"mix{l}": ("w_out_2", l)}
        AFTER = {}
        names = [n for n, _, _ in STREAM]
        for a, b in zip(names, names[1:] + ["end"]):
            AFTER[a] = b

        block = ctx.enter_context(nc.Block())

        @block.sync
        def _(sp):
            sp.dma_start(CT[:, :], table).then_inc(S("consts"), 16)
            sp.dma_start(Z[:, 48:52, :].rearrange("p c t -> p (c t)"), window_counts).then_inc(S("counts_in"), 16)
            sp.dma_start(chunks(W[:, 0:2 * BLK]).rearrange("p (a c) t -> p a (c t)", a=TT),
                         A["x"].rearrange("o (a p) d -> p (o a) d", p=P)).then_inc(S("x_in"), 16)

            def load(ph, j, src, shape, i=0):
                b = at[ph][0] + j
                sp.wait_ge(raw_taken[b % RAW], b // RAW + i)
                n = int(np.prod(shape[1:]))
                dst = raw[:, b % RAW, 0:n].rearrange("p (c n) -> p c n", n=shape[-1])
                sp.dma_start(dst, src).then_inc(raw_full[b % RAW], 16)

            def linear(ph, pieces=None):
                name, l = LIN[ph]
                w = A[name][l or 0].rearrange("(h c p) n -> h p c n", c=8, p=P)
                before = 0
                for start, end in pieces or [(0, at[ph][2] // 4)]:
                    with sp.Fori(0, end - start) as i:
                        for j in range(4):
                            load(ph, j + 4 * before, w[j % 2][:, :, bass.ds(i * 512 + start * 512 + j // 2 * 256, 256)], [P, 8, 256], i)
                    before += end - start

            linear("w_in")
            load("pool_w", 0, A["pool_w"].rearrange("o g (c p) n -> p (o g c) n", p=P), [P, 8, 256])
            for ph in ("w_out", "wk", "wv", "wq", "wo"):
                linear(ph)
            wg = A["w_gate"].rearrange("o e (h c p) n -> h p (o e) c n", c=8, p=P)
            wu = A["w_up"].rearrange("o e (h c p) n -> h p (o e) c n", c=8, p=P)
            wd = A["w_down"].rearrange("o e (c p) n -> p (o e) c n", p=P)

            def load_moe(j, i, src):
                b = at["moe"][0] + j
                sp.wait_ge(raw_taken[b % RAW], b // RAW + 3 * i)
                dst = raw[:, b % RAW, :].rearrange("p (a c n) -> p a c n", a=1, n=src.shape[-1])
                sp.dma_start(dst, src).then_inc(raw_full[b % RAW], 16)

            def load_unit(j, i, e, u):
                for k in range(4):
                    load_moe(j + k, i, (wg, wu)[k // 2][k % 2][:, bass.ds(e, 1), :, u * 256:u * 256 + 256])

            def load_down(j, i, e):
                for k in range(4):
                    load_moe(j + k, i, wd[:, bass.ds(e, 1), :, k * 512:(k + 1) * 512])
            load_unit(0, 0, 0, 0)
            load_unit(4, 0, 0, 1)
            with sp.Fori(0, N_EXP - 1) as i:
                load_unit(8, i, i + 1, 0)
                load_down(12, i, i)
                load_unit(16, i, i + 1, 1)
            load_down(8, N_EXP - 1, N_EXP - 1)
            for l in range(LAYERS):
                linear(f"z{l}", [(EARLY, PIECES), (0, EARLY)])
                load(f"fft{l}", 0, A["w_fft_2"][l].rearrange("(c p) n -> p c n", p=P), [P, 4, 512])
                load(f"pw{l}", 0, A["conv_w_pw_2"][l].rearrange("(c p) n -> p c n", p=P), [P, 4, 512])
                linear(f"mix{l}")
            sp.wait_ge(S("out_rows"), 8)
            sp.dma_start(out.rearrange("o (a p) d -> p (o a) d", p=P),
                         chunks(W[:, 0:2 * BLK]).rearrange("p (a c) t -> p a (c t)", a=TT)).then_inc(S("stored"), 16)
            sp.wait_ge(S("stored"), 16)

        @block.gpsimd
        def _(gp):
            gp.memset(ones[:, :], 1.0).then_inc(S("fills"), 1)
            gp.memset(eps[:, :], EPS).then_inc(S("fills"), 1)
            gp.memset(PR[:, ROW_TILES - 1, :], 0.0).then_inc(S("fills"), 1)
            gp.wait_ge(S("fills"), 3)
            loads = 0
            for name, n in ROWS:
                v = A[name]
                while len(v.shape) > 1:
                    v = v.rearrange("a b c -> (a b) c" if len(v.shape) == 3 else "a b -> (a b)")
                v = v.rearrange("(r f) -> r f", f=P)
                a, r = row_at[name], 0
                while r < n:
                    k = min(n - r, P - (a + r) % P)
                    gp.dma_start(PR[(a + r) % P:(a + r) % P + k, (a + r) // P, :], v[r:r + k]).then_inc(S("rows_in"), 16)
                    loads += 1
                    r += k
            assert loads == N_LOADS
            gp.dma_start(RW[:, :, 0:GROUPS], A["router_group"].rearrange("o (c p) n -> p (o c) n", p=P)).then_inc(S("router_in"), 16)
            gp.dma_start(RW[:, :, GROUPS:], A["router_expert"].rearrange("o (c p) n -> p (o c) n", p=P)).then_inc(S("router_in"), 16)
            for k, name in enumerate(("ret_logit_fwd_2", "ret_logit_bwd_2")):
                gp.dma_start(LG[:, 16 * k:16 * k + 16], A[name].rearrange("a b -> (a b)").partition_broadcast(P)).then_inc(S("logits_in"), 16)
            gp.wait_ge(S("cols"), ROW_TILES)
            gp.memset(w3, 0.0).then_inc(S("bd_zero"), 1)
            gp.wait_ge(S("pooled"), 4)
            gp.memset(Z[:, 0:8, :].rearrange("p h (c s) -> p (h c) s", s=SUB)[:, :, HALF:SUB], 0.0).then_inc(S("k0_zero"), 1)
            gp.wait_ge(S("mix_lo"), 1)
            gp.dma_start(chunks(W[:, 0:2 * BLK]).rearrange("p (a c) t -> p a (c t)", a=TT),
                         A["mem"].rearrange("o (a p) d -> p (o a) d", p=P)).then_inc(S("mem_in"), 16)
            gp.wait_ge(S("r_mm"), TT)
            wa = A["w_ada_2"].rearrange("l (c p) (u n) -> l u p c n", p=P, n=BLK)
            with gp.Fori(0, N_EXP) as e:
                for q in range(N_SUMS):
                    gp.wait_ge(ada_used[q % 2], e * (N_SUMS // 2) + q // 2)
                    gp.dma_start(ADA[:, q % 2:q % 2 + 1, :], wa[q // 3, q % 3][:, bass.ds(e, 1), :]).then_inc(ada_full[q % 2], 16)
            bias = W[:, 0:2 * BLK].rearrange("p (q h k) -> p q h k", q=TT, k=T)
            mask = const("na_mask")
            for l in range(LAYERS):
                gp.wait_ge(S("hid_free"), 1) if l == 0 else gp.wait_ge(S("na_sc"), HEADS * l)
                rb = A["na_rel_bias_2"]
                for h in range(HEADS):
                    for r in range(T // GRID_W):
                        src = bass.AP(rb.tensor, ((l * HEADS + h) * REL_H + NA_KH - 1 - r) * REL_W + NA_KW - GRID_W,
                                      [[1, GRID_W], [REL_W, T // GRID_W], [1, GRID_W]])
                        q = r * GRID_W % P
                        dst = bias[q:q + GRID_W, r * GRID_W // P, h].rearrange("p (a k) -> p a k", k=GRID_W)
                        gp.dma_start(dst, src).then_inc(S("bias_in"), 16)
                gp.wait_ge(S("bias_in"), 16 * HEADS * (T // GRID_W) * (l + 1))
                gp.wait_ge(S("consts"), 16)
                for q in range(TT):
                    gp.tensor_tensor(bias[:, q], bias[:, q], mask[:, None, :].broadcast_to([P, HEADS, T]), ALU.add).then_inc(S("bias_masked"), 1)

        @block.scalar
        def _(act):
            def split(ph, j, i=0):
                b, s = at[ph][0] + j, at[ph][1] + j
                act.wait_ge(raw_full[b % RAW], 16 * (b // RAW + 1) + 16 * i)
                act.wait_ge(block_done[s % SPL], s // SPL + 2 * i)
                act.activation(w_hi[:, s % SPL, :], raw[:, b % RAW, :], ACT.Copy, scale=W_SCALE).then_inc(hi_done, 1)

            def linear(ph, z=None):
                def evict(u, i):
                    done(act, ph, 2 * u + 1, i)
                    act.activation(Z[:, bass.ds(i * 4 + z + 2 * u, 2), :], GB[:, u, :].rearrange("p (c t) -> p c t", t=T),
                                   ACT.Copy, scale=INV).then_inc(bank_free[u], 1)

                def body(i, first):
                    for u in range(2):
                        split(ph, 2 * u, i)
                        split(ph, 2 * u + 1, i)
                        if z is not None and not (first and u == 0):
                            evict(1 - u, i - 1 + u)
                n = at[ph][2] // 4
                body(0, True)
                with act.Fori(1, n) as i:
                    body(i, False)
                if z is not None:
                    evict(1, n - 1)

            def norm_sq(n, src, squares=Zn):
                act.activation(squares, src, ACT.Square).then_inc(S("norm_sq"), 1)
                act.wait_ge(S("norm_var"), n + 1)
                act.activation(nstd, ssum, ACT.Sqrt).then_inc(S("norm_std"), 1)

            def norm_parts(k):
                for g in range(4):
                    act.wait_ge(S("norm_h"), 4 * k + g + 1)
                    act.activation(xh[:, 4 * g:4 * g + 4, :], Zn[:, 4 * g:4 * g + 4, :], ACT.Copy).then_inc(S("norm_hi"), 1)

            def mix_parts(k, name, n):
                act.wait_ge(S(name), n)
                act.activation(xh, Y[:, :, :], ACT.Copy).then_inc(S("mix_hi"), 1)

            for g in range(ROW_TILES):
                act.wait_ge(S("rows_t"), g + 1)
                act.activation(PCt[:, g, :], MB[:, g % 4, 0:P], ACT.Copy).then_inc(S("cols"), 1)
            act.wait_ge(S("cols"), ROW_TILES)
            act.activation(SM[:, 24:40], col("c_2", 0, 16), ACT.Silu).then_inc(S("c_silu"), 1)
            for g in range(8):
                act.wait_ge(S("x_tr"), g + 1)
                act.activation(XT[:, g % 4 * 4:g % 4 * 4 + 4, g // 4 * P:g // 4 * P + P],
                               MB[:, g % 4, :].rearrange("p (c t) -> p c t", t=P), ACT.Copy).then_inc(S("x_t"), 1)
            act.wait_ge(S("x_t"), 8)
            act.wait_ge(S("fills"), 2)
            norm_sq(0, XT[:, :, :])
            norm_parts(0)
            linear("w_in", 0)

            read_out(act, "pool_w")
            act.activation(Z[:, 16:24, :], Z[:, 16:24, :], ACT.Sigmoid).then_inc(S("f_sig"), 1)
            act.wait_ge(S("cols"), ROW_TILES)
            act.wait_ge(S("lb_diff"), 1)
            act.activation(SM[:, 8:16], SM[:, 0:8], ACT.Sigmoid).then_inc(S("lb"), 1)
            act.activation(SM[:, 16:24], SM[:, 0:8], ACT.Sigmoid, scale=-1.0).then_inc(S("lb"), 1)
            act.activation(Z[:, 8:16, :], Z[:, 8:16, :], ACT.Silu).then_inc(S("q_silu"), 1)
            act.activation(Z[:, 32:40, :], Z[:, 32:40, :], ACT.Silu).then_inc(S("g_silu"), 1)
            for g in range(4):
                act.wait_ge(S("v_tr"), g + 1)
                act.activation(Z[:, 40 + 2 * g:42 + 2 * g, :].rearrange("p c t -> p (c t)"), MB[:, g, :], ACT.Copy).then_inc(S("v_rows"), 1)
            act.wait_ge(S("k_ready"), 1)
            act.activation(Z[:, 16:24, :], Z[:, 16:24, :], ACT.Ln).then_inc(S("log_f"), 1)
            for c in range(8):
                act.wait_ge(S("pool_mm"), 1)
                act.activation(Y[:, c, :], MB[:, c // 2, c % 2 * T:c % 2 * T + T], ACT.Copy, scale=col("pool_scale", c)).then_inc(S("pool_out"), 1)
            F = Z[:, 16:24, :].rearrange("p h t -> p (h t)")
            EO = Z[:, 48:52, :].rearrange("p h t -> p (h t)")
            Y1 = Y[:, 8:16, :].rearrange("p h t -> p (h t)")
            act.wait_ge(S("exponents"), 3)
            act.activation(w2, F, ACT.Exp).then_inc(S("exp_q"), 1)
            act.wait_ge(S("exp_q"), 1)
            act.activation(F, F, ACT.Exp, scale=-1.0).then_inc(S("exp_k"), 1)
            act.activation(EO, EO, ACT.Exp).then_inc(S("exp_k"), 1)
            act.activation(Y1, Y1, ACT.Exp).then_inc(S("exp_k"), 1)
            act.activation(H0, w1, ACT.Exp).then_inc(S("exp_a"), 1)
            act.wait_ge(S("state_k"), 1)
            for g in range(4):
                act.wait_ge(S("kt_tr"), g + 1)
                act.activation(w0[:, g * 512:g * 512 + 512], MB[:, 2 + g % 2, :], ACT.Copy).then_inc(S("kt_rows"), 1)
            Fh = Z[:, 16:24, :]
            for a in range(TT):
                act.wait_ge(S("o_done"), a + 1)
                act.activation(Fh[:, :, a * P:a * P + P], MB[:, 0:2, :].rearrange("p b (h t) -> p (b h) t", t=P), ACT.Copy).then_inc(S("o_copied"), 1)
            act.wait_ge(S("o_copied"), TT)
            act.activation(Z[:, 0:8, :], Fh, ACT.Square).then_inc(S("o_sq"), 1)
            act.wait_ge(S("o_var"), 1)
            act.activation(Z[:, 24:32, :], Z[:, 0:8, :], ACT.Sqrt).then_inc(S("o_std"), 1)
            mix_parts(0, "hgrn_y", 1)
            linear("w_out")

            for g in range(8):
                act.wait_ge(S("x_tr"), 8 + g + 1)
                act.activation(Y[:, g % 4 * 4:g % 4 * 4 + 4, g // 4 * P:g // 4 * P + P],
                               MB[:, g % 4, :].rearrange("p (c t) -> p c t", t=P), ACT.Copy).then_inc(S("x_t"), 1)
            act.wait_ge(S("x_t"), 16)
            norm_sq(1, Y[:, :, :])
            norm_parts(1)
            linear("wk", 0)
            linear("wv", 16)
            read_out(act, "wk")
            norm_sq(2, XT[:, :, :])
            norm_parts(2)
            linear("wq", 32)
            p = w2.rearrange("p (b a k) -> p b a k", b=4, k=T)
            pT = w3.rearrange("p (b a k) -> p b a k", b=4, k=T)
            for g in range(8):
                act.wait_ge(S("xv_tr"), g + 1)
                act.activation(W[:, g * 512:g * 512 + 512], MB[:, 2 + g % 2, :], ACT.Copy).then_inc(S("xv_rows"), 1)
            for h in range(X_HEADS):
                act.wait_ge(S("x_max"), h + 1)
                for a in range(TT):
                    act.activation(p[:, h, a, :], MB[:, h % 2, a * T:a * T + T], ACT.Exp, bias=NAS[:, 4 * h + a:4 * h + a + 1],
                                   scale=X_DH ** -0.5, accum_out=NAS[:, 4 * h + 2 + a:4 * h + 3 + a]).then_inc(S("x_exp"), 1)
            for h in range(X_HEADS):
                act.wait_ge(S("x_ptr"), h + 1)
                act.activation(pT[:, h], MB[:, 2, :].rearrange("p (a k) -> p a k", k=T), ACT.Copy).then_inc(S("x_pt"), 1)
                for b in range(2):
                    act.wait_ge(S("x_o"), 2 * h + b + 1)
                    act.activation(Y[:, 4 * h + 2 * b:4 * h + 2 * b + 2, :], MB[:, b, :].rearrange("p (a k) -> p a k", k=T), ACT.Copy).then_inc(S("x_y"), 1)
            act.wait_ge(S("x_y"), 8)
            mix_parts(1, "x_y", 8)
            linear("wo")
            read_out(act, "moe")
            norm_sq(3, XT[:, :, :])
            norm_parts(3)
            for a in range(TT):
                act.wait_ge(S("r_mm"), TT)
                act.activation(RT[:, 20 * a:20 * a + 20], MB[:, 1, 20 * a:20 * a + 20], ACT.Copy).then_inc(S("r_logits"), 1)
            act.wait_ge(S("r_exp_in"), 1)
            act.activation(RT[:, 48:56], RT[:, 48:56], ACT.Exp).then_inc(S("r_exp"), 1)
            act.wait_ge(S("r_exp_in"), 2)
            act.activation(RT[:, 116:118], RT[:, 116:118], ACT.Exp).then_inc(S("r_exp"), 1)
            act.wait_ge(S("r_tr"), 1)
            act.activation(RT[0:16, 136:392], MB[0:16, 1, 0:T], ACT.Copy).then_inc(S("r_t"), 1)
            comb = Y
            for g in range(8):
                act.wait_ge(S("r_bc"), g + 1)
                act.activation(comb[:, 2 * g:2 * g + 2, :], MB[:, 2 + g % 2, :].rearrange("p (a k) -> p a k", k=T), ACT.Copy).then_inc(S("comb"), 1)
            sg = w0[:, 0:1024].rearrange("p (u c t) -> p u c t", u=2, t=T)
            hid = w0[:, 1024:2048].rearrange("p (u c t) -> p u c t", u=2, t=T)
            hh = w2[:, 0:512].bitcast(F16).rearrange("p (c t) -> p c t", t=T)

            def silu(e, u, j, i):
                done(act, "moe", j, i)
                act.activation(sg[:, u], GB[:, 2 * u, :].rearrange("p (c t) -> p c t", t=T), ACT.Silu, scale=INV).then_inc(bank_free[2 * u], 1)

            def hid_hi(e, u):
                act.wait_ge(S("hid"), e * 2 + u + 1)
                act.activation(hh[:, 2 * u:2 * u + 2, :], hid[:, u], ACT.Copy).then_inc(S("hid_hi"), 1)
            for j in range(8):
                split("moe", j)
                if j == 3:
                    silu(0, 0, 1, 0)
                if j == 5:
                    hid_hi(0, 0)
                if j == 7:
                    silu(0, 1, 5, 0)
            with act.Fori(0, N_EXP - 1) as n:
                e, i = n + 1, n * 3
                for j in range(12):
                    split("moe", 8 + j, i)
                    if j == 1:
                        hid_hi(n, 1)
                    if j == 3:
                        silu(e, 0, 8 + 1, i)
                    if j == 9:
                        done(act, "moe", 8 + 7, i)
                        hid_hi(e, 0)
                    if j == 11:
                        silu(e, 1, 8 + 9, i)
            for j in range(4):
                split("moe", 8 + j, 3 * (N_EXP - 1))
                if j == 1:
                    hid_hi(N_EXP - 1, 1)
            read_out(act, "z0")
            norm_sq(4, XT[:, :, :], Y[:, :, :])

            act.wait_ge(S("logits_in"), 32)
            act.wait_ge(S("lg_abs"), 1)
            act.activation(LG[:, 64:96], LG[:, 32:64], ACT.Exp, scale=-1.0).then_inc(S("lg_exp"), 1)
            act.wait_ge(S("lg_u"), 1)
            act.activation(RT[:, 64:96], LG[:, 32:64], ACT.Ln).then_inc(S("lg_ln"), 1)
            for l in range(LAYERS):
                act.wait_ge(S("x_ready"), l + 1)
                norm_sq(5 + l, XT[:, :, :])
                norm_parts(4 + l)
                ph = f"z{l}"

                def evict(chunk, u, i, j=0):
                    done(act, ph, 2 * u + 1 + j, i)
                    act.activation(Z[:, bass.ds(chunk, 2), :], GB[:, u, :].rearrange("p (c t) -> p c t", t=T),
                                   ACT.Copy, scale=INV).then_inc(bank_free[u], 1)

                def piece(n, i, j, before):
                    split(ph, j, i)
                    split(ph, j + 1, i)
                    if before is not None:
                        evict(before, 1, i, j - 4)
                    split(ph, j + 2, i)
                    split(ph, j + 3, i)
                    evict(n * 4, 0, i, j)
                piece(EARLY, 0, 0, None)
                with act.Fori(0, PIECES - EARLY - 1) as i:
                    piece(i + EARLY + 1, i, 4, i * 4 + (4 * EARLY + 2))
                late = 4 * (PIECES - EARLY)
                piece(0, 0, late, 4 * PIECES - 2)
                read_early = uses[ph][1] + PIECES - EARLY
                act.wait_ge(bank_free[1], read_early)
                act.activation(Z[:, 44:48, :], Z[:, 44:48, :], ACT.Sigmoid).then_inc(S("b_sig"), 1)
                act.activation(Z[:, 48:52, :], Z[:, 48:52, :], ACT.Silu).then_inc(S("gates"), 1)
                with act.Fori(0, EARLY - 1) as i:
                    piece(i + 1, i, late + 4, i * 4 + 2)
                evict(4 * EARLY - 2, 1, EARLY - 1, late)
                read_out(act, f"fft{l}")
                act.wait_ge(S("conv_sum"), l + 1)
                act.activation(ssum, GB[:, 2, 0:T], ACT.Copy, scale=1.0 / 512).then_inc(S("conv_mean"), 1)
                for c in (4, 20, 36):
                    act.activation(Z[:, c:c + 4, :], Z[:, c:c + 4, :], ACT.Silu).then_inc(S("gates"), 1)
                nv = w3[:, 1024:2048].rearrange("p (a n) -> p a n", a=TT)
                rv = w3[:, 0:1024].rearrange("p (a n) -> p a n", a=TT)
                for k, dst in enumerate((nv, rv)):
                    for a in range(TT):
                        act.wait_ge(S("zv_tr"), 4 * l + 2 * k + a + 1)
                        act.activation(dst[:, a, :], MB[:, 2 * k + a, :], ACT.Copy).then_inc(S("zv_rows"), 1)
                act.wait_ge(S("conv_c"), l + 1)
                act.activation(csq, ca, ACT.Square).then_inc(S("conv_sq"), 1)
                fa = w2.rearrange("p (b n) -> p b n", n=512)
                for b in range(4):
                    act.wait_ge(S("fft_ch"), 4 * l + b + 1)
                    act.activation(fa[:, b, :], MB[:, b, :], ACT.Copy).then_inc(S("fft_a"), 1)
                act.wait_ge(S("conv_var"), l + 1)
                act.activation(nstd, GB[:, 3, 0:T], ACT.Sqrt, bias=eps[:, :], scale=1.0 / 512).then_inc(S("conv_std"), 1)
                fy = Z[:, 0:4, :]
                for b in range(2):
                    act.wait_ge(S("fft_tok"), 2 * l + b + 1)
                    act.activation(fy[:, 2 * b:2 * b + 2, :], MB[:, b, :].rearrange("p (a k) -> p a k", k=T), ACT.Copy).then_inc(S("fft_y"), 1)
                act.wait_ge(S("conv_n"), 4 * l + 4)
                act.activation(ca, ca, ACT.Silu).then_inc(S("conv_s"), 1)

                def na_exp(h):
                    pr = w2[:, h % 2 * 512:h % 2 * 512 + 512].rearrange("p (a k) -> p a k", k=T)
                    act.wait_ge(S("na_max"), 8 * l + h + 1)
                    for a in range(TT):
                        act.activation(pr[:, a, :], MB[:, h % 2, a * T:a * T + T], ACT.Exp, scale=DH ** -0.5, bias=NAS[:, 4 * (h % 2) + a:4 * (h % 2) + a + 1],
                                       accum_out=NAS[:, 4 * (h % 2) + 2 + a:4 * (h % 2) + 3 + a]).then_inc(S("na_exp"), 1)
                na_exp(0)
                for h in range(HEADS):
                    dt = Z[:, 40 + h % 2 * 2:42 + h % 2 * 2, :]
                    act.wait_ge(S("decay_e"), 8 * l + h + 1)
                    act.activation(dt, dt, ACT.Exp).then_inc(S("decay"), 1)
                    if h + 1 < HEADS:
                        na_exp(h + 1)
                    pt = w2[:, 1024 + h % 2 * 512:1536 + h % 2 * 512]
                    act.wait_ge(S("na_ptr"), 8 * l + h + 1)
                    act.activation(pt, MB[:, 2, :], ACT.Copy).then_inc(S("na_pt"), 1)

                def mixed_hi(g, n):
                    act.wait_ge(S("mixed"), 4 * l + n)
                    act.activation(xh[:, 4 * g:4 * g + 4, :], Y[:, 4 * g:4 * g + 4, :], ACT.Copy).then_inc(S("mix_hi"), 1)
                act.wait_ge(S("ret_o"), 4 * l + 4)
                act.activation(Z[:, 8:12, :], Z[:, 28:32, :], ACT.Square).then_inc(S("ret_sq"), 1)
                mixed_hi(0, 1)
                act.wait_ge(S("ret_ms"), l + 1)
                act.activation(Z[:, 8:12, :].rearrange("p c t -> p (c t)"), MB[:, 0:2, :].rearrange("p b n -> p (b n)"), ACT.Sqrt,
                               bias=eps[:, :], scale=1.0 / DH).then_inc(S("ret_std"), 1)
                mixed_hi(3, 2)
                mixed_hi(1, 3)
                mixed_hi(2, 4)
                linear(f"mix{l}")
            read_out(act, "end")
            norm_sq(7, XT[:, :, :])
            for g in range(8):
                act.wait_ge(S("out_tr"), g + 1)
                act.activation(W[:, g * 512:g * 512 + 512], MB[:, g % 4, :], ACT.Copy).then_inc(S("out_rows"), 1)

        @block.vector
        def _(dve):
            steps = [0]

            def link(ins, wait=True):
                steps[0] += 1
                ins.then_inc(S("dve_step"), 1)
                if wait:
                    dve.wait_ge(S("dve_step"), steps[0])

            def split(ph, j, i=0):
                b, s = at[ph][0] + j, at[ph][1] + j
                dve.wait_ge(hi_done, s + 1 + 4 * i)
                dve.scalar_tensor_tensor(w_lo[:, s % SPL, :], raw[:, b % RAW, :], W_SCALE, w_hi[:, s % SPL, :],
                                         ALU.mult, ALU.subtract).then_inc(raw_taken[b % RAW], 1)

            def linear(ph, add=False, gate=None):
                def evict(u, i):
                    done(dve, ph, 2 * u + 1, i)
                    if gate is None:
                        x = XT[:, bass.ds(i * 4 + 2 * u, 2), :]
                        dve.scalar_tensor_tensor(x, GB[:, u, :].rearrange("p (c t) -> p c t", t=T), INV, x,
                                                 ALU.mult, ALU.add).then_inc(bank_free[u], 1)
                        return
                    for k in range(2):
                        x = XT[:, bass.ds(i * 4 + 2 * u + k, 1), :]
                        ins = dve.scalar_tensor_tensor(x, GB[:, u:u + 1, k * T:k * T + T], gate[:, bass.ds(i * 4 + 2 * u + k, 1)], x,
                                                       ALU.mult, ALU.add)
                    ins.then_inc(bank_free[u], 1)

                def body(i, first):
                    for u in range(2):
                        split(ph, 2 * u, i)
                        split(ph, 2 * u + 1, i)
                        if add and not (first and u == 0):
                            evict(1 - u, i - 1 + u)
                n = at[ph][2] // 4
                body(0, True)
                with dve.Fori(1, n) as i:
                    body(i, False)
                if add:
                    evict(1, n - 1)

            def inverse_root(r, root, v):
                link(dve.reciprocal(r, root))
                link(dve.tensor_tensor(root, r, r, ALU.mult))
                link(dve.scalar_tensor_tensor(root, root, -0.5, v, ALU.mult, ALU.mult))
                link(dve.scalar_tensor_tensor(r, root, 1.5, r, ALU.add, ALU.mult))

            def norm(n, src, gain, parts=None, dst=None, shift=None, squares=Zn):
                dve.wait_ge(S("norm_sq"), n + 1)
                dve.tensor_reduce(ssum, squares.rearrange("p c t -> p t c"), AX.X, ALU.add).then_inc(S("norm_sum"), 1)
                dve.wait_ge(S("norm_ms"), n + 1)
                dve.tensor_scalar(ssum, MB[:, 0, 0:T], 1.0 / D, EPS, ALU.mult, ALU.add).then_inc(S("norm_var"), 1)
                dve.wait_ge(S("norm_std"), n + 1)
                inverse_root(rstd, nstd, ssum)
                dst = Zn if dst is None else dst
                for g in range(4):
                    for c in range(4 * g, 4 * g + 4):
                        ins = dve.scalar_tensor_tensor(dst[:, c, :], src[:, c, :], gain(c), rstd, ALU.mult, ALU.mult)
                        if shift is not None:
                            link(ins)
                            ins = dve.tensor_scalar(dst[:, c, :], dst[:, c, :], shift(c), None, ALU.add)
                    ins.then_inc(S("norm_h" if parts is not None else f"norm_out{n}"), 1)
                if parts is not None:
                    for g in range(4):
                        dve.wait_ge(S("norm_hi"), 4 * parts + g + 1)
                        dve.tensor_tensor(xl[:, 4 * g:4 * g + 4, :], Zn[:, 4 * g:4 * g + 4, :], xh[:, 4 * g:4 * g + 4, :],
                                          ALU.subtract).then_inc(S("norm_lo"), 1)

            def mix_parts(k):
                dve.wait_ge(S("mix_hi"), k + 1)
                dve.tensor_tensor(xl, Y[:, :, :], xh, ALU.subtract).then_inc(S("mix_lo"), 1)

            dve.wait_ge(S("cols"), ROW_TILES)
            dve.tensor_tensor(SM[:, 0:8], col("hgrn_lb_logits", 0, 8), col("hgrn_lb_logits", 8, 8), ALU.subtract).then_inc(S("lb_diff"), 1)
            norm(0, XT, lambda c: col("norm_mix", c), parts=0)
            linear("w_in")

            read_out(dve, "pool_w")
            dve.wait_ge(S("consts"), 16)
            dve.wait_ge(S("counts_in"), 16)
            u = Z[:, 0:8, :]
            src, sums = u, []
            for k in range(4):
                dst = chunks((w0, w1)[k % 2])
                d = 1 << k
                link(dve.tensor_copy(dst[:, 2 * k:, 0:d], src[:, 2 * k:, 0:d]), wait=False)
                link(dve.tensor_tensor(dst[:, 2 * k:, d:], src[:, 2 * k:, d:], src[:, 2 * k:, 0:T - d], ALU.add))
                sums.append(dst[:, 2 * k:2 * k + 2, :])
                src = dst
            count = Z[:, 48:52, :]
            for g in range(4):
                link(dve.tensor_tensor(sums[g], sums[g], count[:, g:g + 1, :].broadcast_to([P, 2, T]), ALU.mult))
                dve.tensor_tensor(chunks(H0)[:, 2 * g:2 * g + 2, :], sums[g], u[:, 2 * g:2 * g + 2, :], ALU.subtract).then_inc(S("pooled"), 1)

            Fh = Z[:, 16:24, :]
            F = Fh.rearrange("p h t -> p (h t)")
            Q = Z[:, 8:16, :].rearrange("p h t -> p (h t)")
            dve.wait_ge(S("f_sig"), 1)
            dve.wait_ge(S("lb"), 2)
            for h in range(HEADS):
                link(dve.tensor_scalar(Fh[:, h, :], Fh[:, h, :], SM[:, 16 + h:17 + h], SM[:, 8 + h:9 + h], ALU.mult, ALU.add), wait=h == HEADS - 1)
            dve.wait_ge(S("pooled"), 4)
            dve.tensor_scalar(w0, F, -1.0, 1.0, ALU.mult, ALU.add).then_inc(S("k_ready"), 1)
            dve.wait_ge(S("log_f"), 1)

            def by_chunk(ap):
                return ap.rearrange("p (g s) -> p g s", s=SUB)
            src = by_chunk(F)
            for k in range(5):
                dst = by_chunk(w1 if k % 2 == 0 else F)
                d = 1 << k
                link(dve.tensor_copy(dst[:, :, 0:d], src[:, :, 0:d]), wait=False)
                link(dve.tensor_tensor(dst[:, :, d:], src[:, :, d:], src[:, :, 0:SUB - d], ALU.add))
                src = dst
            a = by_chunk(w1)
            ah = w1.rearrange("p (g s) -> p g s", s=HALF)
            EO = Z[:, 48:52, :].rearrange("p h t -> p (h t)").rearrange("p (g s) -> p g s", s=HALF)
            Y1 = Y[:, 8:16, :].rearrange("p h t -> p (h t)")
            NG = HEADS * NCH
            dve.tensor_tensor(F.rearrange("p (g s) -> p g s", s=HALF), ah, ah[:, :, HALF // 2 - 1:HALF // 2].broadcast_to([P, 2 * NG, HALF]),
                              ALU.subtract).then_inc(S("exponents"), 1)
            dve.tensor_tensor(EO, a[:, :, HALF + HALF // 2 - 1:HALF + HALF // 2].broadcast_to([P, NG, HALF]), a[:, :, 0:HALF], ALU.subtract).then_inc(S("exponents"), 1)
            dve.tensor_tensor(by_chunk(Y1), a[:, :, SUB - 1:SUB].broadcast_to([P, NG, SUB]), a, ALU.subtract).then_inc(S("exponents"), 1)
            k0 = by_chunk(Z[:, 0:8, :].rearrange("p h t -> p (h t)"))
            k1 = by_chunk(Z[:, 24:32, :].rearrange("p h t -> p (h t)"))
            kk = by_chunk(w0)
            dve.wait_ge(S("exp_q"), 1)
            dve.wait_ge(S("q_silu"), 1)
            dve.tensor_tensor(w2, w2, Q, ALU.mult).then_inc(S("q_intra"), 1)
            dve.wait_ge(S("exp_k"), 3)
            dve.wait_ge(S("k0_zero"), 1)
            dve.wait_ge(S("v_tr"), 4)
            fk = by_chunk(F)
            dve.tensor_tensor(k0[:, :, 0:HALF], kk[:, :, 0:HALF], fk[:, :, 0:HALF], ALU.mult).then_inc(S("k_intra"), 1)
            dve.tensor_tensor(k1[:, :, HALF:], kk[:, :, HALF:], fk[:, :, HALF:], ALU.mult).then_inc(S("k_intra"), 1)
            dve.tensor_tensor(k1[:, :, 0:HALF], kk[:, :, 0:HALF], EO, ALU.mult).then_inc(S("k_intra"), 1)
            dve.tensor_tensor(Y1, Y1, w0, ALU.mult).then_inc(S("state_k"), 1)
            dve.wait_ge(S("exp_a"), 1)
            dve.wait_ge(S("q_intra"), 1)
            dve.tensor_tensor(Q, Q, H0, ALU.mult).then_inc(S("q_inter"), 1)
            bd = w3.rearrange("p (a h t) -> p a h t", a=TT, t=P)
            causal = const("causal")
            dve.wait_ge(S("bd_zero"), 1)
            for t in range(TT):
                dve.wait_ge(S("scores"), t + 1)
                for c in range(4):
                    r = slice(SUB * c, SUB * c + SUB)
                    dve.tensor_tensor(bd[r, t, :, r], MB[r, t, 0:T].rearrange("p (h s) -> p h s", s=SUB),
                                      causal[r, None, :].broadcast_to([SUB, HEADS, SUB]), ALU.mult).then_inc(S("bd"), 1)
            dec = H0.rearrange("p (h t) -> p h t", t=T)
            st = w1.rearrange("p (b h v) -> p b h v", b=2, v=P)
            tmp = EO.rearrange("p g s -> p (g s)").rearrange("p (h v) -> p h v", v=P)
            dve.wait_ge(S("exp_a"), 1)
            for c in range(NCH - 1):
                kv = MB[:, 2:4, :].rearrange("p b (h v) -> p (b h) v", v=P)
                if c:
                    last = dec[:, :, c * SUB + SUB - 1:c * SUB + SUB]
                    dve.wait_ge(S("state"), c)
                    link(dve.tensor_tensor(tmp, st[:, c % 2], last.broadcast_to([P, HEADS, P]), ALU.mult))
                dve.wait_ge(S("kv"), c + 1)
                if c:
                    dve.tensor_tensor(st[:, (c + 1) % 2], tmp, kv, ALU.add).then_inc(S("state"), 1)
                else:
                    dve.tensor_copy(st[:, 1], kv).then_inc(S("state"), 1)
            R = Z[:, 24:32, :].rearrange("p h t -> p (h t)")
            VAR = Z[:, 0:8, :].rearrange("p h t -> p (h t)")
            dve.wait_ge(S("o_ms"), 1)
            dve.tensor_scalar(VAR, MB[:, :, :].rearrange("p b n -> p (b n)"), 1.0 / P, EPS, ALU.mult, ALU.add).then_inc(S("o_var"), 1)
            dve.wait_ge(S("o_std"), 1)
            inverse_root(w0, R, VAR)
            R = w0
            link(dve.scalar_tensor_tensor(Y1, F, col("hgrn_norm"), R, ALU.mult, ALU.mult))
            dve.wait_ge(S("g_silu"), 1)
            dve.wait_ge(S("pool_out"), 8)
            dve.tensor_tensor(Y1, Y1, Z[:, 32:40, :].rearrange("p h t -> p (h t)"), ALU.mult).then_inc(S("hgrn_y"), 1)
            mix_parts(0)
            linear("w_out", add=True)

            norm(1, Y, lambda c: col("norm_mem", c), parts=1)
            linear("wk")
            linear("wv")
            norm(2, XT, lambda c: col("norm_xattn", c), parts=2)
            linear("wq")
            p = w2.rearrange("p (b a k) -> p b a k", b=4, k=T)
            for h in range(X_HEADS):
                dve.wait_ge(S("x_sc"), h + 1)
                m = NAS[:, 4 * h:4 * h + 2]
                link(dve.tensor_reduce(m, MB[:, h % 2, :].rearrange("p (a k) -> p a k", k=T), AX.X, ALU.max))
                dve.tensor_scalar(m, m, -(X_DH ** -0.5), None, ALU.mult).then_inc(S("x_max"), 1)
                dve.wait_ge(S("x_exp"), 2 * h + 2)
                s = NAS[:, 4 * h + 2:4 * h + 4]
                link(dve.reciprocal(s, s))
                for t in range(TT):
                    dve.tensor_scalar(p[:, h, t, :], p[:, h, t, :], s[:, t:t + 1], None, ALU.mult).then_inc(S("x_p"), 1)
            mix_parts(1)
            linear("wo", add=True)
            norm(3, XT, lambda c: col("norm_ffn", c), parts=3)

            def v2(a, n):
                return RT[:, a:a + 2 * n].rearrange("p (t n) -> p t n", t=2)

            def spread(ap, n):
                return ap.broadcast_to([P, 2, n])
            lg = RT[:, 0:40].rearrange("p (t n) -> p t n", t=2)
            lgg = lg[:, :, 0:GROUPS]
            prio = const("prio")[:, None, :].broadcast_to([P, 2, 4])
            mx, shift, ssm, pg, eq, gsel = v2(40, 1), v2(48, 4), v2(56, 1), v2(58, 1), v2(60, 4), v2(68, 4)
            sel, m1, oh1, sel2, m2, oh2 = v2(76, 4), v2(84, 1), v2(86, 4), v2(94, 4), v2(102, 1), v2(104, 4)
            gap, den, wa, wb, ce = v2(116, 1), v2(118, 1), v2(120, 1), v2(122, 1), v2(124, 4)
            big = CMB[:, :].rearrange("p (t g e) -> p t g e", t=2, e=4)
            dve.wait_ge(S("r_logits"), 2)

            def first_max(dst, vals, m):
                link(dve.tensor_reduce(m, vals, AX.X, ALU.max))
                link(dve.tensor_tensor(eq, vals, spread(m, 4), ALU.is_ge))
                link(dve.tensor_tensor(eq, eq, prio, ALU.mult))
                link(dve.tensor_reduce(ssm, eq, AX.X, ALU.max))
                link(dve.tensor_tensor(dst, eq, spread(ssm, 4), ALU.is_ge))
            first_max(gsel, lgg, mx)
            dve.tensor_tensor(shift, lgg, spread(mx, 4), ALU.subtract).then_inc(S("r_exp_in"), 1)
            dve.wait_ge(S("r_exp"), 1)
            link(dve.tensor_reduce(ssm, shift, AX.X, ALU.add))
            link(dve.reciprocal(pg, ssm))
            for g in range(GROUPS):
                part = lg[:, :, GROUPS + 4 * g:GROUPS + 4 * g + 4]
                link(dve.tensor_tensor(big[:, :, g, :], part, spread(gsel[:, :, g:g + 1], 4), ALU.mult))
            link(dve.tensor_reduce(sel, big.rearrange("p t g e -> p t e g"), AX.X, ALU.add))
            first_max(oh1, sel, m1)
            link(dve.scalar_tensor_tensor(sel2, oh1, NEG, sel, ALU.mult, ALU.add))
            first_max(oh2, sel2, m2)
            dve.tensor_tensor(gap, m2, m1, ALU.subtract).then_inc(S("r_exp_in"), 1)
            dve.wait_ge(S("r_exp"), 2)
            link(dve.tensor_scalar(den, gap, 1.0, None, ALU.add))
            link(dve.reciprocal(wa, den))
            link(dve.tensor_tensor(wa, wa, pg, ALU.mult))
            link(dve.tensor_tensor(wb, wa, gap, ALU.mult))
            link(dve.tensor_tensor(oh1, oh1, spread(wa, 4), ALU.mult))
            link(dve.tensor_tensor(oh2, oh2, spread(wb, 4), ALU.mult))
            link(dve.tensor_tensor(ce, oh1, oh2, ALU.add))
            for g in range(GROUPS):
                dve.tensor_tensor(big[:, :, g, :], ce, spread(gsel[:, :, g:g + 1], 4), ALU.mult).then_inc(S("combine"), 1)

            sg = w0[:, 0:1024].rearrange("p (u c t) -> p u c t", u=2, t=T)
            hid = w0[:, 1024:2048].rearrange("p (u c t) -> p u c t", u=2, t=T)
            hh = w2[:, 0:512].bitcast(F16).rearrange("p (c t) -> p c t", t=T)
            hl = w2[:, 512:1024].bitcast(F16).rearrange("p (c t) -> p c t", t=T)
            comb = Y
            dve.wait_ge(S("comb"), 8)
            dve.wait_ge(S("c_silu"), 1)
            dve.wait_ge(S("norm_lo"), 16)
            dve.wait_ge(S("r_mm"), TT)

            def modulate(e, q, first):
                n = e * (N_SUMS // 2) + q // 2
                dve.wait_ge(ada_full[q % 2], n * 16 + 16)
                sums, w = SUMS[:, q * BLK:(q + 1) * BLK], ADA[:, q % 2, :]
                if first:
                    dve.tensor_scalar(sums, w, SM[:, 24:25], None, ALU.mult).then_inc(ada_used[q % 2], 1)
                    return
                dve.wait_ge(ada_used[q % 2], n - (N_SUMS // 2 - 1))
                dve.scalar_tensor_tensor(sums, w, SM[:, bass.ds(e + 24, 1)], sums, ALU.mult, ALU.add).then_inc(ada_used[q % 2], 1)

            base = uses["moe"]

            def lo(j, i):
                split("moe", j, i)

            def weigh(e, u, read):
                dve.wait_ge(bank_free[2 * u], read)
                dve.tensor_tensor(sg[:, u], sg[:, u], comb[:, bass.ds(e, 1), :].broadcast_to([P, 2, T]), ALU.mult).then_inc(S("weighted"), 1)

            def make_hid(e, u, j, i):
                done(dve, "moe", j, i)
                step = e * 2 + u + 1
                dve.wait_ge(S("weighted"), step)
                dve.scalar_tensor_tensor(hid[:, u], GB[:, 2 * u + 1, :].rearrange("p (c t) -> p c t", t=T), INV, sg[:, u],
                                         ALU.mult, ALU.mult).then_inc(S("hid"), 1)
                dve.wait_ge(S("hid"), step)
                dve.sem_inc(bank_free[2 * u + 1], 1)

            def hid_lo(e, u):
                dve.wait_ge(S("hid_hi"), e * 2 + u + 1)
                dve.tensor_tensor(hl[:, 2 * u:2 * u + 2, :], hid[:, u], hh[:, 2 * u:2 * u + 2, :], ALU.subtract).then_inc(S("hid_lo"), 1)

            def add(d, j, i):
                done(dve, "moe", j + d, i)
                for q in range(2):
                    c, b = 4 * d + 2 * q, (2 * d + q + 2) % 4
                    dve.scalar_tensor_tensor(XT[:, c:c + 2, :], GB[:, b, :].rearrange("p (c t) -> p c t", t=T), INV, XT[:, c:c + 2, :],
                                             ALU.mult, ALU.add).then_inc(bank_free[b], 1)
            for j in range(8):
                lo(j, 0)
                if j < N_SUMS:
                    modulate(0, j, True)
                if j == 4:
                    weigh(0, 0, base[0] + 1)
                if j == 5:
                    make_hid(0, 0, 3, 0)
                    hid_lo(0, 0)
            weigh(0, 1, base[2] + 1)
            with dve.Fori(0, N_EXP - 1) as n:
                e, i = n + 1, n * 3
                for j in range(12):
                    lo(8 + j, i)
                    if j == 1:
                        make_hid(n, 1, 7, i)
                    if j == 2:
                        hid_lo(n, 1)
                    if j == 4:
                        weigh(e, 0, n * 3 + base[0] + 2)
                    if j == 5:
                        make_hid(e, 0, 8 + 3, i)
                    if 6 <= j <= 9:
                        add(j - 6, 8 + 4, i)
                    if j == 9:
                        hid_lo(e, 0)
                    if j == 11:
                        weigh(e, 1, n * 3 + base[2] + 4)
                    if j % 2 == 0:
                        modulate(e, j // 2, False)
            last = 3 * (N_EXP - 1)
            for j in range(4):
                lo(8 + j, last)
                if j == 1:
                    make_hid(N_EXP - 1, 1, 7, last)
                    hid_lo(N_EXP - 1, 1)
                if j >= 2:
                    add(j - 2, 8, last)
            add(2, 8, last)
            add(3, 8, last)
            norm(4, XT, lambda c: col("norm_final", c), dst=XT, squares=Y)
            dve.wait_ge(S("norm_out4"), 4)
            dve.sem_inc(S("hid_free"), 1)

            dve.wait_ge(S("logits_in"), 32)
            dve.scalar_tensor_tensor(LG[:, 32:64], LG[:, 0:32], -1.0, LG[:, 0:32], ALU.mult, ALU.max).then_inc(S("lg_abs"), 1)
            dve.wait_ge(S("lg_exp"), 1)
            y1p, y = LG[:, 32:64], LG[:, 64:96]
            dve.tensor_scalar(y1p, y, 1.0, None, ALU.add).then_inc(S("lg_u"), 1)
            dve.wait_ge(S("lg_u"), 1)
            um, isone = RT[:, 0:32], RT[:, 32:64]
            link(dve.tensor_scalar(um, y1p, -1.0, 1e-30, ALU.add, ALU.max))
            link(dve.reciprocal(um, um))
            link(dve.tensor_scalar(isone, y1p, 1.0, None, ALU.is_le))
            link(dve.tensor_tensor(isone, isone, y, ALU.mult))
            dve.wait_ge(S("lg_ln"), 1)
            link(dve.tensor_tensor(um, um, y, ALU.mult))
            link(dve.tensor_tensor(um, um, RT[:, 64:96], ALU.mult))
            link(dve.tensor_tensor(um, um, isone, ALU.add))
            link(dve.scalar_tensor_tensor(LG[:, 0:32], LG[:, 0:32], 0.0, um, ALU.min, ALU.subtract))

            for l in range(LAYERS):
                read_out(dve, f"z{l}")
                if l == 0:
                    dve.wait_ge(S("ada"), LAYERS)
                    link(dve.tensor_tensor(MOD[:, :, :].rearrange("p l c -> p (l c)"), MB[:, 1, 0:LAYERS * 3 * KC], col("b_ada_2", 0, LAYERS * 3 * KC), ALU.add))
                link(dve.scalar_tensor_tensor(GAIN[:, :], MOD[:, l, KC:2 * KC], 1.0, col("norm_g_2", KC * l, KC), ALU.add, ALU.mult))
                link(dve.tensor_scalar(MOD[:, l, 2 * KC:], MOD[:, l, 2 * KC:], INV, None, ALU.mult))
                dve.sem_inc(S("x_ready"), 1)
                norm(5 + l, XT, lambda c: GAIN[:, c:c + 1], parts=4 + l, shift=lambda c: MOD[:, l, c:c + 1])
                ph = f"z{l}"
                late = 4 * (PIECES - EARLY)
                with dve.Fori(0, PIECES - EARLY + 1) as i:
                    for j in range(4):
                        split(ph, j, i)
                pad = TAPS // 2
                link(dve.memset(CU[:, :, 0:pad], 0.0), wait=False)
                link(dve.memset(CU[:, :, pad + T:], 0.0), wait=False)
                dve.wait_ge(S("b_sig"), l + 1)
                link(dve.tensor_tensor(CU[:, :, pad:pad + T], Z[:, 40:44, :], Z[:, 44:48, :], ALU.mult))

                def tap_at(c, k):
                    return CU[:, c, bass.ds(k, T)], PC[:, bass.ds(k * 4 + (row_at["conv_w_2"] + l * TAPS * 4 + c), 1)]
                n_taps = 4 * TAPS * l
                for c in range(4):
                    dve.tensor_scalar(ca[:, c, :], CU[:, c, 0:T], col("conv_w_2", l * TAPS * 4 + c), col("conv_b_2", 4 * l + c),
                                      ALU.mult, ALU.add).then_inc(S("tap"), 1)

                def tap(c, k, tail=False):
                    dve.wait_ge(S("tap"), k * 4 + (n_taps + c - 3))
                    x, w = (CU[:, c, k:k + T], col("conv_w_2", (l * TAPS + k) * 4 + c)) if tail else tap_at(c, k)
                    dve.scalar_tensor_tensor(ca[:, c, :], x, w, ca[:, c, :], ALU.mult, ALU.add).then_inc(S("tap"), 1)
                with dve.Fori(0, EARLY - 1) as i:
                    for j in range(4):
                        split(ph, late + 4 + j, i)
                        for n in range(3 * j, 3 * j + 3):
                            tap(n % 4, i * 3 + (1 + n // 4))
                for k in range(3 * (EARLY - 1) + 1, TAPS):
                    for c in range(4):
                        tap(c, k, True)
                dve.wait_ge(S("tap"), n_taps + 4 * TAPS)
                dve.sem_inc(S("conv_a"), 1)
                read_out(dve, f"fft{l}")
                dve.wait_ge(S("conv_mean"), l + 1)
                dve.tensor_tensor(ca, ca, ssum[:, None, :].broadcast_to([P, 4, T]), ALU.subtract).then_inc(S("conv_c"), 1)
                cos, sin = const("rope_cos"), const("rope_sin")

                def rotary(c):
                    tmp = RO[:, c % 2, :]
                    dve.wait_ge(S("rot"), 8 * l + c + 1)
                    link(dve.tensor_tensor(tmp, GB[:, c % 2, 0:T], sin, ALU.mult))
                    link(dve.tensor_tensor(Z[:, 24 + c, :], Z[:, 24 + c, :], cos, ALU.mult))
                    dve.tensor_tensor(Z[:, 24 + c, :], Z[:, 24 + c, :], tmp, ALU.add).then_inc(S("rotated"), 1)
                for c in range(6):
                    rotary(c)
                dve.wait_ge(S("conv_std"), l + 1)
                dve.wait_ge(S("conv_c"), l + 1)
                link(dve.reciprocal(rstd, nstd))
                link(dve.tensor_tensor(ca, ca, rstd[:, None, :].broadcast_to([P, 4, T]), ALU.mult))
                for c in range(4):
                    dve.tensor_scalar(ca[:, c, :], ca[:, c, :], col("conv_ln_g_2", 4 * l + c), col("conv_ln_b_2", 4 * l + c), ALU.mult, ALU.add).then_inc(S("conv_n"), 1)
                rotary(6)
                rotary(7)
                dve.wait_ge(S("gates"), 4 * l + 4)
                dve.wait_ge(S("fft_w"), l + 1)
                dve.tensor_tensor(Y[:, 0:4, :], MB[:, 2:4, :].rearrange("p b (a k) -> p (b a) k", k=T), Z[:, 4:8, :], ALU.mult).then_inc(S("mixed"), 1)

                def na_gate(c):
                    dve.wait_ge(S("na_o"), 4 * l + c + 1)
                    dve.tensor_tensor(Y[:, 4 + c, :], GB[:, c % 2, 0:T], Z[:, 20 + c, :], ALU.mult).then_inc(S("na_y"), 1)

                def ret_copy(c):
                    dve.wait_ge(S("ret_pv"), 8 * l + 2 * c + 2)
                    dve.tensor_copy(Z[:, 28 + c, :], GB[:, 2 + c % 2, 0:T]).then_inc(S("ret_o"), 1)

                def na_max(h):
                    dve.wait_ge(S("na_sc"), 8 * l + h + 1)
                    m = NAS[:, 4 * (h % 2):4 * (h % 2) + 2]
                    link(dve.tensor_reduce(m, MB[:, h % 2, :].rearrange("p (a k) -> p a k", k=T), AX.X, ALU.max))
                    dve.tensor_scalar(m, m, -(DH ** -0.5), None, ALU.mult).then_inc(S("na_max"), 1)
                ahead, behind = const("ahead"), const("behind")
                na_max(0)
                for h in range(HEADS):
                    dt, pw = (Z[:, z + h % 2 * 2:z + h % 2 * 2 + 2, :].rearrange("p a k -> p (a k)") for z in (40, 44))
                    link(dve.tensor_scalar(dt, behind, LG[:, 16 + 8 * l + h:17 + 8 * l + h], None, ALU.mult))
                    dve.scalar_tensor_tensor(dt, ahead, LG[:, 8 * l + h:8 * l + h + 1], dt, ALU.mult, ALU.add).then_inc(S("decay_e"), 1)
                    if h + 1 < HEADS:
                        na_max(h + 1)
                    if h == 0:
                        dve.wait_ge(S("conv_w"), l + 1)
                        dve.tensor_tensor(ca, GB[:, 2:4, :].rearrange("p b (a k) -> p (b a) k", k=T), Z[:, 48:52, :], ALU.mult).then_inc(S("mixed"), 1)
                    pr = w2[:, h % 2 * 512:h % 2 * 512 + 512].rearrange("p (a k) -> p a k", k=T)
                    s = NAS[:, 4 * (h % 2) + 2:4 * (h % 2) + 4]
                    dve.wait_ge(S("na_exp"), 16 * l + 2 * h + 2)
                    link(dve.reciprocal(s, s))
                    for t in range(TT):
                        dve.tensor_scalar(pr[:, t, :], pr[:, t, :], s[:, t:t + 1], None, ALU.mult).then_inc(S("na_p"), 1)
                    if h >= 2 and h % 2 == 0:
                        na_gate(h // 2 - 1)
                        ret_copy(h // 2 - 1)
                    if h >= 2:
                        dve.wait_ge(S("ret_pv"), 8 * l + h - 1)
                    dve.wait_ge(S("decay"), 8 * l + h + 1)
                    dve.wait_ge(S("ret_sc"), 8 * l + h + 1)
                    dve.scalar_tensor_tensor(pw, MB[:, 3, :], DH ** -0.5, dt, ALU.mult, ALU.mult).then_inc(S("ret_p"), 1)
                ret_copy(3)
                na_gate(3)
                dve.wait_ge(S("na_y"), 4 * l + 4)
                dve.sem_inc(S("mixed"), 1)

                def mixed_lo(g, n):
                    dve.wait_ge(S("mix_hi"), 2 + 4 * l + n)
                    dve.tensor_tensor(xl[:, 4 * g:4 * g + 4, :], Y[:, 4 * g:4 * g + 4, :], xh[:, 4 * g:4 * g + 4, :], ALU.subtract).then_inc(S("mix_lo"), 1)
                mixed_lo(0, 1)
                r = Z[:, 8:12, :]
                dve.wait_ge(S("ret_std"), l + 1)
                link(dve.reciprocal(r, r))
                link(dve.tensor_tensor(Y[:, 8:12, :], Z[:, 28:32, :], r, ALU.mult))
                dve.tensor_tensor(Y[:, 8:12, :], Y[:, 8:12, :], Z[:, 36:40, :], ALU.mult).then_inc(S("mixed"), 1)
                mixed_lo(3, 2)
                mixed_lo(1, 3)
                mixed_lo(2, 4)
                linear(f"mix{l}", add=True, gate=MOD[:, l, 2 * KC:])
            norm(7, XT, lambda c: col("final_g_2", c))

        @block.tensor
        def _(pe):
            def product(ph, j, i, b, kc, k0, cols, uses_b, xs, start, stop):
                s = at[ph][1] + j
                x_hi, x_lo = xs
                hi = w_hi[:, s % SPL, :].rearrange("p (c n) -> p c n", c=kc)
                lo = w_lo[:, s % SPL, :].rearrange("p (c n) -> p c n", c=kc)
                for q, n in enumerate(cols):
                    o = GB[:, b, q * T:q * T + T]
                    for k in range(kc):
                        w, v = hi[:, k, n * P:n * P + P], lo[:, k, n * P:n * P + P]
                        first = start and q == 0 and k == 0
                        pe.matmul(o, w, x_hi[:, k0 + k, :], start=first, stop=False, skip_group_check=True)
                        pe.matmul(o, w, x_lo[:, k0 + k, :], start=False, stop=False, skip_group_check=True)
                        last = pe.matmul(o, v, x_hi[:, k0 + k, :], start=False, stop=stop and k == kc - 1, skip_group_check=True)
                return last

            def linear(ph):
                with pe.Fori(0, at[ph][2] // 4) as i:
                    for j in range(4):
                        s = at[ph][1] + j
                        taken(pe, ph, j, i)
                        if j % 2 == 0:
                            pe.wait_ge(bank_free[j // 2], uses[ph][j // 2] + i)
                        last = product(ph, j, i, j // 2, 8, j % 2 * 8, (0, 1), None, (xh, xl), j % 2 == 0, j % 2 == 1)
                        last.then_inc(block_done[s % SPL], 1)

            def norm(n):
                pe.wait_ge(S("norm_sum"), n + 1)
                pe.matmul(MB[:, 0, 0:T], ones[:, :], ssum, start=True, stop=True).then_inc(S("norm_ms"), 1)

            pe.wait_ge(S("consts"), 16)
            pe.wait_ge(S("rows_in"), 16 * N_LOADS)
            for g in range(ROW_TILES):
                if g >= 4:
                    pe.wait_ge(S("cols"), g - 3)
                pe.transpose(MB[:, g % 4, 0:P], PR[:, g, :], ident).then_inc(S("rows_t"), 1)

            def turn(src, ready, copied, before):
                for g in range(8):
                    pe.wait_ge(*before(g))
                    for k in range(4):
                        c = g % 4 * 4 + k
                        ins = pe.transpose(MB[:, g % 4, k * P:k * P + P], src[:, g // 4, c * P:c * P + P], ident)
                    ins.then_inc(S(ready), 1)
            rows = W[:, 0:2 * BLK].rearrange("p (a d) -> p a d", a=TT)
            pe.wait_ge(S("x_in"), 16)
            turn(rows, "x_tr", "x_t", lambda g: (S("cols"), ROW_TILES) if g < 4 else (S("x_t"), g - 3))
            pe.wait_ge(S("fills"), 2)
            norm(0)
            pe.wait_ge(S("norm_lo"), 4)
            linear("w_in")

            read_out(pe, "pool_w")
            for g in range(4):
                for k in range(4):
                    h = g % 2 * 4 + k
                    ins = pe.transpose(MB[:, g, k * P:k * P + P], Z[:, 24 + h, g // 2 * P:g // 2 * P + P], ident)
                ins.then_inc(S("v_tr"), 1)
            b = at["pool_w"][0]
            pe.wait_ge(raw_full[b % RAW], 16 * (b // RAW + 1))
            pe.wait_ge(S("pooled"), 4)
            pe.wait_ge(S("v_rows"), 4)
            pw = raw[:, b % RAW, :].rearrange("p (k n) -> p k n", n=T)
            pooled = chunks(H0)
            for g in range(4):
                for n in range(2):
                    for k in range(2):
                        ins = pe.matmul(MB[:, g, n * T:n * T + T], pw[:, 2 * g + k, n * P:n * P + P], pooled[:, 2 * g + k, :],
                                        start=n == 0 and k == 0, stop=k == 1, skip_group_check=True)
            ins.then_inc(raw_taken[b % RAW], 1)
            pe.wait_ge(raw_taken[b % RAW], b // RAW + 1)
            pe.sem_inc(S("pool_mm"), 1)
            k0 = Z[:, 0:8, :].rearrange("p h t -> p (h t)")
            k1 = Z[:, 24:32, :].rearrange("p h t -> p (h t)")
            pe.wait_ge(S("pool_out"), 8)
            pe.wait_ge(S("q_intra"), 1)
            pe.wait_ge(S("k_intra"), 3)
            for t in range(TT):
                for c in range(4):
                    r = slice(SUB * c, SUB * c + SUB)
                    for h in range(HEADS):
                        at_ = h * T + t * P + c * SUB
                        for half, k in enumerate((k0, k1)):
                            q = w2[:, at_ + half * HALF:at_ + half * HALF + HALF]
                            ins = pe.matmul(MB[r, t, h * SUB + half * HALF:h * SUB + half * HALF + HALF], k[:, at_:at_ + SUB], q,
                                            start=h == 0 and half == 0, stop=True, skip_group_check=True)
                ins.then_inc(S("scores"), 1)
            pe.wait_ge(S("state_k"), 1)
            for g in range(4):
                if g >= 2:
                    pe.wait_ge(S("kt_rows"), g - 1)
                for k in range(4):
                    h = g % 2 * 4 + k
                    ins = pe.transpose(MB[:, 2 + g % 2, k * P:k * P + P], Y[:, 8 + h, g // 2 * P:g // 2 * P + P], ident)
                ins.then_inc(S("kt_tr"), 1)
            V = Z[:, 40:48, :].rearrange("p c t -> p (c t)").rearrange("p (a h v) -> p a h v", a=TT, v=P)
            Kt = w0.rearrange("p (a h d) -> p a h d", a=TT, d=P)
            bd = w3.rearrange("p (a h t) -> p a h t", a=TT, t=P)
            st = w1.rearrange("p (b h v) -> p b h v", b=2, v=P)
            Q = Z[:, 8:16, :]
            pe.wait_ge(S("kt_rows"), 4)
            pe.wait_ge(S("bd"), 8)
            pe.wait_ge(S("q_inter"), 1)
            for t in range(TT):
                if t:
                    pe.wait_ge(S("o_copied"), t)
                for h in range(HEADS):
                    pe.matmul(MB[:, h // 4, h % 4 * P:h % 4 * P + P], V[:, t, h, :], bd[:, t, h, :], start=h % 4 == 0, stop=False, skip_group_check=True)
                for c in range(4):
                    n = 4 * t + c
                    r = slice(SUB * c, SUB * c + SUB)
                    if n:
                        pe.wait_ge(S("state"), n)
                    if n < NCH - 1:
                        for h in range(HEADS):
                            ins = pe.matmul(MB[:, 2 + h // 4, h % 4 * P:h % 4 * P + P], Kt[r, t, h, :], V[r, t, h, :],
                                            start=h % 4 == 0, stop=True, skip_group_check=True)
                        ins.then_inc(S("kv"), 1)
                    if n:
                        for h in range(HEADS):
                            ins = pe.matmul(MB[:, h // 4, h % 4 * P + c * SUB:h % 4 * P + c * SUB + SUB], st[:, n % 2, h, :],
                                            Q[:, h, n * SUB:n * SUB + SUB], start=False, stop=True, skip_group_check=True)
                ins.then_inc(S("o_done"), 1)
            pe.wait_ge(S("o_sq"), 1)
            for b in range(4):
                ins = pe.matmul(MB[:, b, :], ones[:, :], Z[:, 2 * b:2 * b + 2, :].rearrange("p h t -> p (h t)"), start=True, stop=True)
            ins.then_inc(S("o_ms"), 1)
            pe.wait_ge(S("mix_lo"), 1)
            linear("w_out")

            pe.wait_ge(S("mem_in"), 16)
            pe.wait_ge(S("o_std"), 1)
            turn(rows, "x_tr", "x_t", lambda g: (S("o_std"), 1) if g < 4 else (S("x_t"), 8 + g - 3))
            norm(1)
            pe.wait_ge(S("norm_lo"), 8)
            linear("wk")
            linear("wv")
            norm(2)
            pe.wait_ge(S("norm_lo"), 12)
            linear("wq")
            read_out(pe, "wo")
            K, V, Q = Z[:, 0:16, :], Z[:, 16:32, :], Z[:, 32:48, :]
            pe.wait_ge(S("norm_std"), 3)
            for g in range(8):
                if g >= 2:
                    pe.wait_ge(S("xv_rows"), g - 1)
                for k in range(4):
                    ins = pe.transpose(MB[:, 2 + g % 2, k * P:k * P + P], V[:, g % 4 * 4 + k, g // 4 * P:g // 4 * P + P], ident)
                ins.then_inc(S("xv_tr"), 1)
            Vs = W[:, 0:2 * BLK].rearrange("p (a d) -> p a d", a=TT)
            p = w2.rearrange("p (b a k) -> p b a k", b=4, k=T)
            pT = w3.rearrange("p (b a k) -> p b a k", b=4, k=T)
            for h in range(X_HEADS):
                if h >= 2:
                    pe.wait_ge(S("x_exp"), 2 * h - 2)
                for a in range(TT):
                    for c in range(4):
                        ins = pe.matmul(MB[:, h % 2, a * T:a * T + T], Q[:, 4 * h + c, a * P:a * P + P], K[:, 4 * h + c, :],
                                        start=a == 0 and c == 0, stop=c == 3, skip_group_check=True)
                ins.then_inc(S("x_sc"), 1)
            pe.wait_ge(S("xv_rows"), 8)
            for h in range(X_HEADS):
                pe.wait_ge(S("x_p"), 2 * h + 2)
                if h:
                    pe.wait_ge(S("x_pt"), h)
                for k in range(TT):
                    for a in range(TT):
                        ins = pe.transpose(MB[:, 2, k * T + a * P:k * T + a * P + P], p[:, h, a, k * P:k * P + P], ident)
                ins.then_inc(S("x_ptr"), 1)
                pe.wait_ge(S("x_pt"), h + 1)
                for b in range(2):
                    if h == 0:
                        pe.wait_ge(S("x_exp"), 8)
                    else:
                        pe.wait_ge(S("x_y"), 2 * h - 1 + b)
                    for c in range(2):
                        for k in range(TT):
                            d = h * X_DH + (2 * b + c) * P
                            ins = pe.matmul(MB[:, b, c * T:c * T + T], Vs[:, k, d:d + P], pT[:, h, k, :], start=c == 0 and k == 0, stop=k == 1, skip_group_check=True)
                    ins.then_inc(S("x_o"), 1)
            pe.wait_ge(S("mix_lo"), 2)
            linear("wo")
            norm(3)
            pe.wait_ge(S("norm_h"), 16)
            pe.wait_ge(S("router_in"), 32)
            for a in range(TT):
                for c in range(KC):
                    ins = pe.matmul(MB[:, 1, 20 * a:20 * a + 20], Zn[:, c, a * P:a * P + P], RW[:, c, :], start=a == 0 and c == 0, stop=c == KC - 1, skip_group_check=True)
                ins.then_inc(S("r_mm"), 1)
            pe.wait_ge(S("combine"), 4)
            pe.wait_ge(S("r_logits"), 2)
            for a in range(TT):
                ins = pe.transpose(MB[0:16, 1, a * P:a * P + P], CMB[:, 16 * a:16 * a + 16], ident)
            ins.then_inc(S("r_tr"), 1)
            pe.wait_ge(S("r_t"), 1)
            for g in range(8):
                if g >= 2:
                    pe.wait_ge(S("comb"), g - 1)
                for k in range(2):
                    e = 2 * g + k
                    ins = pe.matmul(MB[:, 2 + g % 2, k * T:k * T + T], ident[0:16, e:e + 1].broadcast_to([16, P]), RT[0:16, 136:392],
                                    start=k == 0, stop=True, skip_group_check=True)
                ins.then_inc(S("r_bc"), 1)
            pe.wait_ge(S("norm_lo"), 16)
            hh = w2[:, 0:512].bitcast(F16).rearrange("p (c t) -> p c t", t=T)
            hl = w2[:, 512:1024].bitcast(F16).rearrange("p (c t) -> p c t", t=T)

            def half(u, j, i, free):
                for k in range(4):
                    b, s = 2 * u + k // 2, at["moe"][1] + j + k
                    taken(pe, "moe", j + k, i)
                    if k % 2 == 0:
                        pe.wait_ge(bank_free[b], free + uses["moe"][b])
                    product("moe", j + k, i, b, 8, k % 2 * 8, (0, 1), None, (xh, xl), k % 2 == 0, k % 2 == 1).then_inc(block_done[s % SPL], 1)

            def down(j, i, e, free):
                pe.wait_ge(S("hid_lo"), e * 2 + 2)
                for k in range(4):
                    s = at["moe"][1] + j + k
                    taken(pe, "moe", j + k, i)
                    for q in range(2):
                        b = (2 * k + q + 2) % 4
                        pe.wait_ge(bank_free[b], free[b // 2] + uses["moe"][b] + k // 2)
                        last = product("moe", j + k, i, b, 4, 0, (2 * q, 2 * q + 1), None, (hh, hl), True, True)
                    last.then_inc(block_done[s % SPL], 1)
            half(0, 0, 0, 0)
            half(1, 4, 0, 0)
            with pe.Fori(0, N_EXP - 1) as n:
                i = n * 3
                half(0, 8, i, i + 1)
                down(12, i, n, (i + 2, i + 1))
                half(1, 16, i, i + 3)
            used = 3 * (N_EXP - 1) + 1
            down(8, 3 * (N_EXP - 1), N_EXP - 1, (used, used))
            def modulation(l):
                for j in range(2):
                    pe.wait_ge(ada_used[j], N_EXP * N_SUMS // 2)
                for n in range(3 * KC):
                    at_ = (l * 3 * KC + n) * P
                    ins = pe.matmul(MB[:, 1, l * 3 * KC + n:l * 3 * KC + n + 1], SUMS[:, at_:at_ + P], ones[:, 0:1],
                                    start=l == 0 and n == 0, stop=True, skip_group_check=True)
                ins.then_inc(S("ada"), 1)
            modulation(0)
            norm(4)
            modulation(1)

            for l in range(LAYERS):
                norm(5 + l)
                pe.wait_ge(S("norm_lo"), 20 + 4 * l)
                linear(f"z{l}")
                read_out(pe, f"fft{l}")
                rot = const("rot")

                def rotate(c):
                    if c >= 2:
                        pe.wait_ge(S("rotated"), 8 * l + c - 1)
                    pe.matmul(GB[:, c % 2, 0:T], rot, Z[:, 24 + c, :], start=True, stop=True).then_inc(S("rot"), 1)
                pe.wait_ge(S("conv_a"), l + 1)
                for c in range(4):
                    ins = pe.matmul(GB[:, 2, 0:T], ones[:, :], ca[:, c, :], start=c == 0, stop=c == 3)
                ins.then_inc(S("conv_sum"), 1)
                rotate(0)
                rotate(1)
                pe.wait_ge(S("norm_std"), 6 + l)
                pe.wait_ge(S("x_ready"), l + 1)
                for k, z in enumerate((16, 32)):
                    for a in range(TT):
                        for c in range(4):
                            ins = pe.transpose(MB[:, 2 * k + a, c * P:c * P + P], Z[:, z + c, a * P:a * P + P], ident)
                        ins.then_inc(S("zv_tr"), 1)
                rotate(2)
                rotate(3)
                for a in range(TT):
                    for g in range(4):
                        if g % 2 == 0:
                            pe.wait_ge(S("zv_rows"), 4 * l + 2 * a + g // 2 + 1)
                        ins = pe.matmul(MB[:, 2 * a + g // 2, g % 2 * T:g % 2 * T + T], Z[:, g, a * P:a * P + P], const("dft_ch"),
                                        start=g % 2 == 0, stop=True, skip_group_check=True)
                        if g % 2:
                            ins.then_inc(S("fft_ch"), 1)
                rotate(4)
                rotate(5)
                pe.wait_ge(S("conv_sq"), l + 1)
                for c in range(4):
                    ins = pe.matmul(GB[:, 3, 0:T], ones[:, :], csq[:, c, :], start=c == 0, stop=c == 3)
                ins.then_inc(S("conv_var"), 1)
                fa = w2.rearrange("p (a g n) -> p a g n", a=TT, g=4)
                dcos = const("dft_cos").rearrange("p (a t) -> p a t", t=T)
                dsin = const("dft_nsin").rearrange("p (a t) -> p a t", t=T)
                pe.wait_ge(S("fft_a"), 4 * l + 4)
                for g in range(4):
                    for a in range(TT):
                        for k, m in enumerate((dcos, dsin)):
                            ins = pe.matmul(MB[:, g // 2, g % 2 * T:g % 2 * T + T], fa[:, a, g, k * P:k * P + P], m[:, a, :],
                                            start=g % 2 == 0 and a == 0 and k == 0, stop=a == 1 and k == 1, skip_group_check=True)
                    if g % 2:
                        ins.then_inc(S("fft_tok"), 1)
                rotate(6)
                rotate(7)

                def small(ph, x, banks, ready):
                    b = at[ph][0]
                    pe.wait_ge(raw_full[b % RAW], 16 * (b // RAW + 1))
                    w = raw[:, b % RAW, :].rearrange("p (c n) -> p c n", n=512)
                    for n in range(4):
                        for k in range(4):
                            ins = pe.matmul(banks[:, n // 2, n % 2 * T:n % 2 * T + T], w[:, k, n * P:n * P + P], x[:, k, :],
                                            start=n % 2 == 0 and k == 0, stop=k == 3, skip_group_check=True)
                    ins.then_inc(raw_taken[b % RAW], 1)
                    pe.wait_ge(raw_taken[b % RAW], b // RAW + 1)
                    pe.sem_inc(S(ready), 1)
                pe.wait_ge(S("fft_y"), 2 * l + 2)
                small(f"fft{l}", Z[:, 0:4, :], MB[:, 2:4, :], "fft_w")
                nv = w3[:, 1024:2048].rearrange("p (a n) -> p a n", a=TT)
                rv = w3[:, 0:1024].rearrange("p (a n) -> p a n", a=TT)
                bias = W[:, 0:2 * BLK].rearrange("p (q h k) -> p q h k", q=TT, k=T)

                def na_scores(h):
                    c, r = h // 2, slice(DH * (h % 2), DH * (h % 2) + DH)
                    if h >= 2:
                        pe.wait_ge(S("na_exp"), 16 * l + 2 * h - 2)
                    for a in range(TT):
                        o = MB[:, h % 2, a * T:a * T + T]
                        pe.matmul(o, const("unflip"), bias[:, a, h, :], start=a == 0, stop=False, skip_group_check=True)
                        ins = pe.matmul(o, Z[r, 8 + c, a * P:a * P + P], Z[r, 12 + c, :], start=False, stop=True, skip_group_check=True)
                    ins.then_inc(S("na_sc"), 1)
                pe.wait_ge(S("bias_masked"), 2 * l + 2)
                na_scores(0)
                na_scores(1)
                pe.wait_ge(S("conv_s"), l + 1)
                small(f"pw{l}", ca, GB[:, 2:4, :], "conv_w")
                pe.wait_ge(S("rotated"), 8 * l + 8)
                pe.wait_ge(S("mixed"), 4 * l + 1)
                for h in range(HEADS):
                    c, r = h // 2, slice(DH * (h % 2), DH * (h % 2) + DH)
                    if h:
                        pe.wait_ge(S("ret_p"), 8 * l + h)
                    for a in range(TT):
                        ins = pe.matmul(MB[:, 3, a * T:a * T + T], Z[r, 28 + c, a * P:a * P + P], Z[r, 24 + c, :], start=a == 0, stop=True, skip_group_check=True)
                    ins.then_inc(S("ret_sc"), 1)
                    pr = w2[:, h % 2 * 512:h % 2 * 512 + 512].rearrange("p (a k) -> p a k", k=T)
                    pt = w2[:, 1024 + h % 2 * 512:1536 + h % 2 * 512].rearrange("p (a k) -> p a k", k=T)
                    pe.wait_ge(S("na_p"), 16 * l + 2 * h + 2)
                    if h:
                        pe.wait_ge(S("na_pt"), 8 * l + h)
                    for k in range(TT):
                        for a in range(TT):
                            ins = pe.transpose(MB[:, 2, k * T + a * P:k * T + a * P + P], pr[:, a, k * P:k * P + P], ident)
                    ins.then_inc(S("na_ptr"), 1)
                    pw = Z[:, 44 + h % 2 * 2:46 + h % 2 * 2, :]
                    pe.wait_ge(S("ret_p"), 8 * l + h + 1)
                    if h == 0:
                        pe.wait_ge(S("mixed"), 4 * l + 2)
                    if h % 2 == 0 and c >= 2:
                        pe.wait_ge(S("ret_o"), 4 * l + c - 1)
                    for k in range(TT):
                        ins = pe.matmul(GB[r, 2 + c % 2, 0:T], rv[:, k, h * DH:h * DH + DH], pw[:, k, :], start=k == 0, stop=k == 1, skip_group_check=True)
                    ins.then_inc(S("ret_pv"), 1)
                    pe.wait_ge(S("na_pt"), 8 * l + h + 1)
                    if h % 2 == 0 and c >= 2:
                        pe.wait_ge(S("na_y"), 4 * l + c - 1)
                    for k in range(TT):
                        ins = pe.matmul(GB[r, c % 2, 0:T], nv[:, k, h * DH:h * DH + DH], pt[:, k, :], start=k == 0, stop=k == 1, skip_group_check=True)
                    if h % 2:
                        ins.then_inc(S("na_o"), 1)
                    if h + 2 < HEADS:
                        na_scores(h + 2)
                pe.wait_ge(S("ret_sq"), l + 1)
                for b in range(2):
                    ins = pe.matmul(MB[:, b, :], const("pair"), Z[:, 8 + 2 * b:10 + 2 * b, :].rearrange("p c t -> p (c t)"), start=True, stop=True)
                ins.then_inc(S("ret_ms"), 1)
                pe.wait_ge(S("mix_lo"), 2 + 4 * (l + 1))
                linear(f"mix{l}")
            norm(7)
            for g in range(8):
                pe.wait_ge(S("norm_out7"), g % 4 + 1)
                if g >= 4:
                    pe.wait_ge(S("out_rows"), g - 3)
                for k in range(4):
                    ins = pe.transpose(MB[:, g % 4, k * P:k * P + P], Zn[:, g % 4 * 4 + k, g // 4 * P:g // 4 * P + P], ident)
                ins.then_inc(S("out_tr"), 1)


def row_loads():
    n, loads = 0, 0
    for _, k in ROWS:
        r = 0
        while r < k:
            r += min(k - r, P - (n + r) % P)
            loads += 1
        n += k
    return loads


N_LOADS = row_loads()


INPUTS = ["x", "mem", "norm_mix", "w_in", "pool_w", "pool_scale", "hgrn_lb_logits", "hgrn_norm", "w_out",
          "norm_xattn", "norm_mem", "xattn_wq", "xattn_wk", "xattn_wv", "xattn_wo", "norm_ffn", "router_group",
          "router_expert", "w_gate", "w_up", "w_down", "norm_final", "c_2", "norm_g_2", "w_ada_2", "b_ada_2",
          "w_in_2", "w_fft_2", "na_rel_bias_2", "ret_logit_fwd_2", "ret_logit_bwd_2", "conv_w_2", "conv_b_2",
          "conv_ln_g_2", "conv_ln_b_2", "conv_w_pw_2", "w_out_2", "final_g_2"]


def lay_out(inputs, nc):
    tables = constants()
    arrays, A, const_at, at = {}, {}, {}, 0
    for name in INPUTS:
        arrays[name] = np.ascontiguousarray(inputs[name])
        A[name] = nc.dram_tensor(name, arrays[name].shape, F32, kind="ExternalInput").ap()
    for name, v in tables.items():
        const_at[name] = (at, v.shape[1])
        at += v.shape[1]
    arrays["table"] = np.concatenate(list(tables.values()), 1)
    arrays["window_counts"] = counts()
    table = nc.dram_tensor("table", arrays["table"].shape, F32, kind="ExternalInput").ap()
    window_counts = nc.dram_tensor("window_counts", arrays["window_counts"].shape, F32, kind="ExternalInput").ap()
    out = nc.dram_tensor("out", (1, T, D), F32, kind="ExternalOutput").ap()
    build(nc, A, table, const_at, window_counts, out)
    return arrays


def kernel(**inputs):
    from concourse import bacc
    from concourse.bass_utils import run_bass_kernel_spmd

    nc = bacc.Bacc("TRN2", target_bir_lowering=False, num_devices=1)
    arrays = lay_out(inputs, nc)
    r = run_bass_kernel_spmd(nc, [arrays], core_ids=[0])
    return r.results[0]["out"]
```

```python
from contextlib import ExitStack

import numpy as np

import concourse.bass as bass
from concourse import mybir

F32 = mybir.dt.float32
F16 = mybir.dt.float16
ALU = mybir.AluOpType
ACT = mybir.ActivationFunctionType
AX = mybir.AxisListType

P = 128
T = 256
TT = T // P
D = 2048
KC = D // P
EPS = 1e-6
W_SCALE = 256.0
BLK = 2048
RAW = 4
SPL = 2
IN_ORDER = [(4, 6), (0, 4), (6, 10)]
POOL_WINDOWS = (2, 4, 8, 16)
HEADS = 8
SUB = 32
HALF = SUB // 2
NCH = T // SUB
X_HEADS = 4
X_DH = D // X_HEADS
GROUPS, PER_GROUP = 4, 4
N_EXP = GROUPS * PER_GROUP
D_EXP = 512
LAYERS = 2
PIECES = 13
EARLY = 10
N_SUMS = LAYERS * 3
GRID_W, NA_KW, NA_KH = 64, 16, 8
REL_H, REL_W = 2 * NA_KH - 1, 2 * NA_KW - 1
TAPS = 31
DH = 64
NEG = -1.0e30


def constants():
    p, t = np.arange(P), np.arange(T)
    out = {"ident": np.eye(P)}
    ang = 2 * np.pi * np.outer(p, p) / P
    out["dft_ch"] = np.concatenate([np.cos(ang), np.sin(ang)], 1)
    ang = 2 * np.pi * (np.outer(t, t) % T) / T
    norm = 1.0 / np.sqrt(T * P)
    for name, m in (("dft_cos", np.cos(ang) * norm), ("dft_nsin", -np.sin(ang) * norm)):
        out[name] = m.reshape(TT, P, T).transpose(1, 0, 2).reshape(P, TT * T)
    half = DH // 2
    inv = (np.float32(10000.0) ** (-np.arange(half, dtype=np.float32) / np.float32(half))).astype(np.float32)
    rope = (t.astype(np.float32)[None, :] * inv[p % half][:, None]).astype(np.float32)
    out["rope_cos"], out["rope_sin"] = np.cos(rope), np.sin(rope)
    rot = np.zeros((P, P))
    for m in range(P):
        if m % DH < half:
            rot[m + half, m] = -1.0
        else:
            rot[m - half, m] = 1.0
    out["rot"] = rot
    d = t[None, :] - t[:, None]
    for name, m in (("ahead", np.maximum(d, 0)), ("behind", np.maximum(-d, 0))):
        out[name] = m.reshape(TT, P, T).transpose(1, 0, 2).reshape(P, TT * T)
    c, k = GRID_W - 1 - p % GRID_W, t % GRID_W
    start = np.clip(c - NA_KW // 2, 0, GRID_W - NA_KW)
    rel = k[None, :] - start[:, None]
    out["na_mask"] = np.where((rel >= 0) & (rel < NA_KW), 0.0, NEG)
    out["unflip"] = ((p[:, None] // GRID_W == p[None, :] // GRID_W) & (p[:, None] % GRID_W == GRID_W - 1 - p[None, :] % GRID_W)) * DH ** 0.5
    out["causal"] = (p[:, None] % SUB <= np.arange(SUB)[None, :]) * 1.0
    out["prio"] = np.tile(np.arange(4, 0, -1), (P, 1))
    out["pair"] = (p[:, None] // DH == p[None, :] // DH) * 1.0
    return {n: np.ascontiguousarray(v, dtype=np.float32) for n, v in out.items()}


def counts():
    t = np.arange(T)
    return np.concatenate([np.tile(1.0 / np.minimum(t + 1, w), (P, 1)) for w in POOL_WINDOWS], 1).astype(np.float32)


ROWS = [("norm_mix", 16), ("pool_scale", 8), ("hgrn_lb_logits", 16), ("hgrn_norm", 1), ("norm_xattn", 16),
        ("norm_mem", 16), ("norm_ffn", 16), ("norm_final", 16), ("c_2", 16), ("norm_g_2", 32),
        ("b_ada_2", 96), ("conv_w_2", 248), ("conv_b_2", 8), ("conv_ln_g_2", 8), ("conv_ln_b_2", 8),
        ("final_g_2", 16)]
N_ROWS = sum(n for _, n in ROWS)
ROW_TILES = -(-N_ROWS // P)

STREAM = [("w_in", 40, True), ("pool_w", 1, False), ("w_out", 16, True), ("wk", 16, True), ("wv", 16, True),
          ("wq", 16, True), ("wo", 16, True), ("moe", 12 * N_EXP, True)]
for _l in range(LAYERS):
    STREAM += [(f"z{_l}", 52, True), (f"fft{_l}", 1, False), (f"pw{_l}", 1, False),
               (f"mix{_l}", 16, True)]


def places():
    out, b, s = {}, 0, 0
    for name, n, split in STREAM:
        out[name] = (b, s, n)
        b, s = b + n, s + n * split
    return out


def bank_uses():
    out, used = {}, [0] * 4
    for name, n, split in STREAM:
        out[name] = list(used)
        if name == "moe":
            used = [x + 3 * N_EXP for x in used]
        elif split:
            used = [used[0] + n // 4, used[1] + n // 4] + used[2:]
    out["end"] = used
    return out


def build(nc, A, table, const_at, window_counts, out, dbg=()):
    ctx = ExitStack()
    with ctx:
        def sb(name, shape, dt=F32):
            return ctx.enter_context(nc.sbuf_tensor(name, shape, dt))

        sems = {}

        def S(name):
            if name not in sems:
                sems[name] = ctx.enter_context(nc.semaphore(name))
            return sems[name]

        raw_full = [S(f"raw_full{j}") for j in range(RAW)]
        raw_taken = [S(f"raw_taken{j}") for j in range(RAW)]
        hi_done = S("hi_done")
        block_done = [S(f"block_done{j}") for j in range(SPL)]
        ada_full = [S(f"ada_full{j}") for j in range(2)]
        ada_used = [S(f"ada_used{j}") for j in range(2)]
        bank_free = [S(f"bank_free{j}") for j in range(4)]

        raw = sb("raw", [P, RAW, BLK])
        w_hi = sb("w_hi", [P, SPL, BLK], F16)
        w_lo = sb("w_lo", [P, SPL, BLK], F16)
        XT = sb("XT", [P, KC, T])
        H = sb("H", [P, 2 * BLK])
        xh = H[:, 0:BLK].bitcast(F16).rearrange("p (c t) -> p c t", t=T)
        xl = H[:, BLK:2 * BLK].bitcast(F16).rearrange("p (c t) -> p c t", t=T)
        H0 = H[:, 0:BLK]
        Z = sb("Z", [P, 52, T])
        Y = sb("Y", [P, KC, T])
        W = sb("W", [P, 4 * BLK])
        w0, w1, w2, w3 = (W[:, k * BLK:(k + 1) * BLK] for k in range(4))
        CT = sb("CT", [P, table.shape[1]])
        PR = w3[:, 0:ROW_TILES * P].rearrange("p (a b) -> p a b", b=P)
        PCt = sb("PCt", [P, ROW_TILES, P])
        PC = PCt[:, :, :].rearrange("p a b -> p (a b)")
        ones = sb("ones", [P, P])
        eps = sb("eps", [P, 1])
        NS = sb("NS", [P, 3, T])
        ssum, nstd, rstd = NS[:, 0, :], NS[:, 1, :], NS[:, 2, :]
        RW = sb("RW", [P, KC, GROUPS + N_EXP])
        RT = sb("RT", [P, 400])
        MOD = sb("MOD", [P, LAYERS, 3 * KC])
        GAIN = sb("GAIN", [P, KC])
        SM = sb("SM", [P, 64])
        LG = sb("LG", [P, 96])
        NAS = sb("NAS", [P, 32])
        CMB = sb("CMB", [P, TT * N_EXP])
        CU = Y[:, :, :].rearrange("p c t -> p (c t)")[:, 0:4 * (T + TAPS - 1)].rearrange("p (c t) -> p c t", c=4)
        ca, csq = Y[:, 12:16, :], Y[:, 8:12, :]
        RO = H[:, BLK:BLK + 2 * T].rearrange("p (c t) -> p c t", t=T)
        GB = ctx.enter_context(nc.psum_tensor("GB", [P, 4, 512], F32))
        MB = ctx.enter_context(nc.psum_tensor("MB", [P, 4, 512], F32))

        def const(name, rows=P):
            at, n = const_at[name]
            return CT[0:rows, at:at + n]

        ident = const("ident")
        row_at, n = {}, 0
        for name, k in ROWS:
            row_at[name] = n
            n += k

        def col(name, i=0, n=1):
            return PC[:, row_at[name] + i:row_at[name] + i + n]

        def chunks(ap):
            return ap.rearrange("p (c t) -> p c t", t=T)

        at = places()
        uses = bank_uses()
        Zn = Z[:, 32:48, :]
        SUMS = Z[:, 0:48, :].rearrange("p c t -> p (c t)")
        ADA = W[:, :].rearrange("p (a b n) -> p a b n", b=2, n=BLK)[:, :, 1, :]
        INV = 1.0 / W_SCALE

        def taken(eng, ph, j, i=0):
            b = at[ph][0] + j
            eng.wait_ge(raw_taken[b % RAW], b // RAW + 1 + i)

        def done(eng, ph, j, i=0):
            s = at[ph][1] + j
            eng.wait_ge(block_done[s % SPL], s // SPL + 1 + 2 * i)

        def read_out(eng, ph):
            for b in range(4):
                eng.wait_ge(bank_free[b], uses[ph][b])

        LIN = {"w_in": ("w_in", None), "w_out": ("w_out", None), "wk": ("xattn_wk", None), "wv": ("xattn_wv", None),
               "wq": ("xattn_wq", None), "wo": ("xattn_wo", None)}
        for l in range(LAYERS):
            LIN |= {f"z{l}": ("w_in_2", l), f"mix{l}": ("w_out_2", l)}
        AFTER = {}
        names = [n for n, _, _ in STREAM]
        for a, b in zip(names, names[1:] + ["end"]):
            AFTER[a] = b

        def steps_between(eng, n, body, steps=()):
            k = 1
            for end, f in (*steps, (n, None)):
                if end > k:
                    with eng.Fori(k, end) as i:
                        body(i, False)
                if f is not None:
                    f()
                k = end

        EARLY_SUMS = (3, 6, 7)

        block = ctx.enter_context(nc.Block())

        @block.sync
        def _(sp):
            sp.dma_start(CT[:, 0:P], table[:, 0:P]).then_inc(S("ident_in"), 16)
            sp.dma_start(chunks(W[:, 0:2 * BLK]).rearrange("p (a c) t -> p a (c t)", a=TT),
                         A["x"].rearrange("o (a p) d -> p (o a) d", p=P)).then_inc(S("x_in"), 16)
            sp.dma_start(CT[:, P:], table[:, P:]).then_inc(S("consts"), 16)
            sp.dma_start(Z[:, 48:52, :].rearrange("p c t -> p (c t)"), window_counts).then_inc(S("counts_in"), 16)

            def load(ph, j, src, shape, i=0):
                b = at[ph][0] + j
                sp.wait_ge(raw_taken[b % RAW], b // RAW + i)
                n = int(np.prod(shape[1:]))
                dst = raw[:, b % RAW, 0:n].rearrange("p (c n) -> p c n", n=shape[-1])
                sp.dma_start(dst, src).then_inc(raw_full[b % RAW], 16)

            def linear(ph, pieces=None):
                name, l = LIN[ph]
                w = A[name][l or 0].rearrange("(h c p) n -> h p c n", c=8, p=P)
                before = 0
                for start, end in pieces or [(0, at[ph][2] // 4)]:
                    with sp.Fori(0, end - start) as i:
                        for j in range(4):
                            load(ph, j + 4 * before, w[j % 2][:, :, bass.ds(i * 512 + start * 512 + j // 2 * 256, 256)], [P, 8, 256], i)
                    before += end - start

            linear("w_in", IN_ORDER)
            load("pool_w", 0, A["pool_w"].rearrange("o g (c p) n -> p (o g c) n", p=P), [P, 8, 256])
            for ph in ("w_out", "wk", "wv", "wq", "wo"):
                linear(ph)
            wg = A["w_gate"].rearrange("o e (h c p) n -> h p (o e) c n", c=8, p=P)
            wu = A["w_up"].rearrange("o e (h c p) n -> h p (o e) c n", c=8, p=P)
            wd = A["w_down"].rearrange("o e (c p) n -> p (o e) c n", p=P)

            def load_moe(j, i, src):
                b = at["moe"][0] + j
                sp.wait_ge(raw_taken[b % RAW], b // RAW + 3 * i)
                dst = raw[:, b % RAW, :].rearrange("p (a c n) -> p a c n", a=1, n=src.shape[-1])
                sp.dma_start(dst, src).then_inc(raw_full[b % RAW], 16)

            def load_unit(j, i, e, u):
                for k in range(4):
                    load_moe(j + k, i, (wg, wu)[k // 2][k % 2][:, bass.ds(e, 1), :, u * 256:u * 256 + 256])

            def load_down(j, i, e):
                for k in range(4):
                    load_moe(j + k, i, wd[:, bass.ds(e, 1), :, k * 512:(k + 1) * 512])
            load_unit(0, 0, 0, 0)
            load_unit(4, 0, 0, 1)
            with sp.Fori(0, N_EXP - 1) as i:
                load_unit(8, i, i + 1, 0)
                load_down(12, i, i)
                load_unit(16, i, i + 1, 1)
            load_down(8, N_EXP - 1, N_EXP - 1)
            for l in range(LAYERS):
                linear(f"z{l}", [(EARLY, PIECES), (0, EARLY)])
                load(f"fft{l}", 0, A["w_fft_2"][l].rearrange("(c p) n -> p c n", p=P), [P, 4, 512])
                load(f"pw{l}", 0, A["conv_w_pw_2"][l].rearrange("(c p) n -> p c n", p=P), [P, 4, 512])
                linear(f"mix{l}")
            sp.wait_ge(S("out_rows"), 8)
            sp.dma_start(out.rearrange("o (a p) d -> p (o a) d", p=P),
                         chunks(W[:, 0:2 * BLK]).rearrange("p (a c) t -> p a (c t)", a=TT)).then_inc(S("stored"), 16)
            sp.wait_ge(S("stored"), 16)

        @block.gpsimd
        def _(gp):
            gp.memset(ones[:, :], 1.0).then_inc(S("fills"), 1)
            gp.memset(eps[:, :], EPS).then_inc(S("fills"), 1)
            gp.memset(PR[:, ROW_TILES - 1, :], 0.0).then_inc(S("fills"), 1)
            gp.wait_ge(S("fills"), 3)
            loads = 0
            for name, n in ROWS:
                v = A[name]
                while len(v.shape) > 1:
                    v = v.rearrange("a b c -> (a b) c" if len(v.shape) == 3 else "a b -> (a b)")
                v = v.rearrange("(r f) -> r f", f=P)
                a, r = row_at[name], 0
                while r < n:
                    k = min(n - r, P - (a + r) % P)
                    gp.dma_start(PR[(a + r) % P:(a + r) % P + k, (a + r) // P, :], v[r:r + k]).then_inc(S("rows_in"), 16)
                    loads += 1
                    r += k
            assert loads == N_LOADS
            gp.dma_start(RW[:, :, 0:GROUPS], A["router_group"].rearrange("o (c p) n -> p (o c) n", p=P)).then_inc(S("router_in"), 16)
            gp.dma_start(RW[:, :, GROUPS:], A["router_expert"].rearrange("o (c p) n -> p (o c) n", p=P)).then_inc(S("router_in"), 16)
            for k, name in enumerate(("ret_logit_fwd_2", "ret_logit_bwd_2")):
                gp.dma_start(LG[:, 16 * k:16 * k + 16], A[name].rearrange("a b -> (a b)").partition_broadcast(P)).then_inc(S("logits_in"), 16)
            gp.wait_ge(S("cols"), ROW_TILES)
            gp.memset(w3, 0.0).then_inc(S("zeros"), 1)
            gp.wait_ge(S("counts_in"), 16)
            for b in range(2):
                gp.wait_ge(bank_free[b], 4)
            u = Z[:, 0:8, :]
            src, trailing, fills = u, [], [3]

            def link(ins):
                ins.then_inc(S("fills"), 1)
                fills[0] += 1
            for k in range(4):
                dst = Z[:, 32 + 8 * (k % 2):40 + 8 * (k % 2), :]
                d = 1 << k
                link(gp.tensor_copy(dst[:, 2 * k:, 0:d], src[:, 2 * k:, 0:d]))
                link(gp.tensor_tensor(dst[:, 2 * k:, d:], src[:, 2 * k:, d:], src[:, 2 * k:, 0:T - d], ALU.add))
                gp.wait_ge(S("fills"), fills[0])
                trailing.append(dst[:, 2 * k:2 * k + 2, :])
                src = dst
            count = Z[:, 48:52, :]
            for g in range(4):
                link(gp.tensor_tensor(trailing[g], trailing[g], count[:, g:g + 1, :].broadcast_to([P, 2, T]), ALU.mult))
                gp.wait_ge(S("fills"), fills[0])
                gp.tensor_tensor(Y[:, 2 * g:2 * g + 2, :], trailing[g], u[:, 2 * g:2 * g + 2, :], ALU.subtract).then_inc(S("pooled"), 1)
            gp.wait_ge(S("pooled"), 4)
            gp.memset(Z[:, 0:8, :].rearrange("p h (c s) -> p (h c) s", s=SUB)[:, :, HALF:SUB], 0.0).then_inc(S("zeros"), 1)
            gp.wait_ge(S("mix_lo"), 3)
            gp.dma_start(chunks(W[:, 0:2 * BLK]).rearrange("p (a c) t -> p a (c t)", a=TT),
                         A["mem"].rearrange("o (a p) d -> p (o a) d", p=P)).then_inc(S("mem_in"), 16)
            gp.wait_ge(S("r_mm"), 1)
            wa = A["w_ada_2"].rearrange("l (c p) (u n) -> l u p c n", p=P, n=BLK)
            with gp.Fori(0, N_EXP) as e:
                for q in range(N_SUMS):
                    gp.wait_ge(ada_used[q % 2], e * (N_SUMS // 2) + q // 2)
                    gp.dma_start(ADA[:, q % 2:q % 2 + 1, :], wa[q // 3, q % 3][:, bass.ds(e, 1), :]).then_inc(ada_full[q % 2], 16)
            bias = W[:, 0:2 * BLK].rearrange("p (q h k) -> p q h k", q=TT, k=T)
            mask = const("na_mask")
            for l in range(LAYERS):
                gp.wait_ge(S("norm_out4"), 4) if l == 0 else gp.wait_ge(S("na_sc"), HEADS * l)
                rb = A["na_rel_bias_2"]
                for h in range(HEADS):
                    for r in range(T // GRID_W):
                        src = bass.AP(rb.tensor, ((l * HEADS + h) * REL_H + NA_KH - 1 - r) * REL_W + NA_KW - GRID_W,
                                      [[1, GRID_W], [REL_W, T // GRID_W], [1, GRID_W]])
                        q = r * GRID_W % P
                        dst = bias[q:q + GRID_W, r * GRID_W // P, h].rearrange("p (a k) -> p a k", k=GRID_W)
                        gp.dma_start(dst, src).then_inc(S("bias_in"), 16)
                gp.wait_ge(S("bias_in"), 16 * HEADS * (T // GRID_W) * (l + 1))
                gp.wait_ge(S("consts"), 16)
                for q in range(TT):
                    gp.tensor_tensor(bias[:, q], bias[:, q], mask[:, None, :].broadcast_to([P, HEADS, T]), ALU.add).then_inc(S("bias_masked"), 1)

        @block.scalar
        def _(act):
            def split(ph, j, i=0):
                b, s = at[ph][0] + j, at[ph][1] + j
                act.wait_ge(raw_full[b % RAW], 16 * (b // RAW + 1) + 16 * i)
                act.wait_ge(block_done[s % SPL], s // SPL + 2 * i)
                act.activation(w_hi[:, s % SPL, :], raw[:, b % RAW, :], ACT.Copy, scale=W_SCALE).then_inc(hi_done, 1)

            def linear(ph, z=None, then=None, steps=()):
                def evict(u, i):
                    done(act, ph, 2 * u + 1, i)
                    act.activation(Z[:, bass.ds(i * 4 + z + 2 * u, 2), :], GB[:, u, :].rearrange("p (c t) -> p c t", t=T),
                                   ACT.Copy, scale=INV).then_inc(bank_free[u], 1)

                def body(i, first):
                    for u in range(2):
                        if not (first and u == 0):
                            split(ph, 2 * u, i)
                            split(ph, 2 * u + 1, i)
                        if z is not None and not (first and u == 0):
                            evict(1 - u, i - 1 + u)
                n = at[ph][2] // 4
                body(0, True)
                steps_between(act, n, body, steps)
                if z is not None:
                    if then is not None:
                        split(then, 0)
                    evict(1, n - 1)

            def ahead_of(ph):
                split(ph, 0)
                split(ph, 1)

            def square(n, src, squares=Zn):
                c = 12 if n in EARLY_SUMS else 0
                read_out(act, before.get(n, "w_in"))
                act.activation(squares[:, c:, :], src[:, c:, :], ACT.Square).then_inc(S("norm_sq"), 1)

            def square_early(ph):
                def step():
                    for b in range(2):
                        act.wait_ge(bank_free[b], uses[ph][b] + 3)
                    act.activation(Zn[:, 0:12, :], XT[:, 0:12, :], ACT.Square).then_inc(S("early_sq"), 1)
                return [(4, step)]

            def root(n):
                act.wait_ge(S("norm_var"), n + 1)
                act.activation(nstd, ssum, ACT.Sqrt).then_inc(S("norm_std"), 1)

            def norm_sq(n, src, squares=Zn, ph=None):
                if ph is not None:
                    split(ph, 0)
                square(n, src, squares)
                if ph is not None:
                    split(ph, 1)
                root(n)

            def norm_parts(k, shift=None, src=Zn):
                for g in range(4):
                    act.wait_ge(S("norm_h"), 4 * k + g + 1)
                    if shift is not None:
                        for c in range(4 * g, 4 * g + 4):
                            ins = act.activation(xh[:, c, :], src[:, c, :], ACT.Identity, bias=shift(c))
                        ins.then_inc(S("norm_hi"), 1)
                        continue
                    act.activation(xh[:, 4 * g:4 * g + 4, :], src[:, 4 * g:4 * g + 4, :], ACT.Copy).then_inc(S("norm_hi"), 1)

            for g in range(8):
                act.wait_ge(S("x_tr"), g + 1)
                act.activation(XT[:, g % 4 * 4:g % 4 * 4 + 4, g // 4 * P:g // 4 * P + P],
                               MB[:, g % 4, :].rearrange("p (c t) -> p c t", t=P), ACT.Copy).then_inc(S("x_t"), 1)
            act.wait_ge(S("x_t"), 8)
            before = {2: "wk", 3: "moe", 4: "z0", 6: "z1", 7: "end"}
            square(0, XT[:, :, :])
            ahead_of("w_in")
            root(0)
            for g in range(ROW_TILES):
                act.wait_ge(S("rows_t"), g + 1)
                act.activation(PCt[:, g, :], MB[:, 1 + g % 3, 0:P], ACT.Copy).then_inc(S("cols"), 1)
            act.wait_ge(S("cols"), ROW_TILES)
            act.activation(SM[:, 24:40], col("c_2", 0, 16), ACT.Silu).then_inc(S("c_silu"), 1)
            norm_parts(0)
            F = Z[:, 16:24, :].rearrange("p h t -> p (h t)")
            EO = Z[:, 48:52, :].rearrange("p h t -> p (h t)")
            Y1 = Y[:, 8:16, :].rearrange("p h t -> p (h t)")
            pieces = [n for start, end in IN_ORDER for n in range(start, end)]

            def evict_in(k, u):
                done(act, "w_in", 4 * k + 2 * u + 1)
                c = 4 * pieces[k] + 2 * u
                act.activation(Z[:, c:c + 2, :], GB[:, u, :].rearrange("p (c t) -> p c t", t=T), ACT.Copy, scale=INV).then_inc(bank_free[u], 1)

            def copied(k):
                for b in range(2):
                    act.wait_ge(bank_free[b], k)
            for k in range(len(pieces)):
                if k:
                    split("w_in", 4 * k)
                    split("w_in", 4 * k + 1)
                    evict_in(k - 1, 1)
                split("w_in", 4 * k + 2)
                split("w_in", 4 * k + 3)
                if k == 2:
                    copied(2)
                    act.activation(Z[:, 16:24, :], Z[:, 16:24, :], ACT.Sigmoid).then_inc(S("f_sig"), 1)
                    act.wait_ge(S("lb_diff"), 1)
                    act.activation(SM[:, 8:16], SM[:, 0:8], ACT.Sigmoid).then_inc(S("lb"), 1)
                    act.activation(SM[:, 16:24], SM[:, 0:8], ACT.Sigmoid, scale=-1.0).then_inc(S("lb"), 1)
                if k == 4:
                    act.wait_ge(S("k_ready"), 1)
                    act.activation(Z[:, 16:24, :], Z[:, 16:24, :], ACT.Ln).then_inc(S("log_f"), 1)
                if k == 3:
                    act.wait_ge(S("lg_abs"), 1)
                    act.activation(LG[:, 64:96], LG[:, 32:64], ACT.Exp, scale=-1.0).then_inc(S("lg_exp"), 1)
                if k == 5:
                    act.wait_ge(S("lg_u"), 1)
                    act.activation(RT[:, 64:96], LG[:, 32:64], ACT.Ln).then_inc(S("lg_ln"), 1)
                if k == 6:
                    copied(6)
                    act.activation(Z[:, 8:16, :], Z[:, 8:16, :], ACT.Silu).then_inc(S("q_silu"), 1)
                if k == 8:
                    act.wait_ge(S("pooled"), 4)
                evict_in(k, 0)
            act.wait_ge(S("exponents"), 3)
            act.activation(w2, F, ACT.Exp).then_inc(S("exp_q"), 1)
            act.wait_ge(S("exp_q"), 1)
            act.activation(F, F, ACT.Exp, scale=-1.0).then_inc(S("exp_k"), 1)
            act.activation(EO, EO, ACT.Exp).then_inc(S("exp_k"), 1)
            act.activation(Y1, Y1, ACT.Exp).then_inc(S("exp_k"), 1)
            evict_in(len(pieces) - 1, 1)
            read_out(act, "pool_w")
            act.activation(H0, w1, ACT.Exp).then_inc(S("exp_a"), 1)
            for g in range(4):
                act.wait_ge(S("v_tr"), g + 1)
                act.activation(Z[:, 40 + 2 * g:42 + 2 * g, :].rearrange("p c t -> p (c t)"), MB[:, g, :], ACT.Copy).then_inc(S("v_rows"), 1)
            act.activation(Z[:, 32:40, :], Z[:, 32:40, :], ACT.Silu).then_inc(S("g_silu"), 1)
            act.wait_ge(S("pool_mm"), 1)
            for c in range(8):
                act.activation(Y[:, c, :], GB[:, c // 2, c % 2 * T:c % 2 * T + T], ACT.Copy, scale=col("pool_scale", c)).then_inc(S("pool_out"), 1)
            act.wait_ge(S("state_k"), 1)
            for g in range(4):
                act.wait_ge(S("kt_tr"), g + 1)
                act.activation(w0[:, g * 512:g * 512 + 512], MB[:, 2 + g % 2, :], ACT.Copy).then_inc(S("kt_rows"), 1)
            Fh = Z[:, 16:24, :]
            ahead_of("w_out")
            for a in range(TT):
                act.wait_ge(S("o_done"), a + 1)
                act.activation(Fh[:, :, a * P:a * P + P], MB[:, 0:2, :].rearrange("p b (h t) -> p (b h) t", t=P), ACT.Copy).then_inc(S("o_copied"), 1)
            act.wait_ge(S("o_copied"), TT)
            act.activation(Z[:, 0:8, :], Fh, ACT.Square).then_inc(S("o_sq"), 1)
            act.wait_ge(S("pool_out"), 8)
            act.activation(xh[:, 0:8, :], Y[:, 0:8, :], ACT.Copy).then_inc(S("mix_hi"), 1)
            act.wait_ge(S("o_ms"), 1)
            act.activation(Z[:, 24:32, :].rearrange("p h t -> p (h t)"), MB[:, :, :].rearrange("p b n -> p (b n)"), ACT.Ln,
                           bias=eps[:, :], scale=1.0 / P).then_inc(S("o_std"), 1)
            act.wait_ge(S("o_std"), 1)
            act.activation(w0, Z[:, 24:32, :].rearrange("p h t -> p (h t)"), ACT.Exp, scale=-0.5).then_inc(S("o_std"), 1)
            for g in (2, 3):
                act.wait_ge(S("hgrn_y"), g - 1)
                act.activation(xh[:, 4 * g:4 * g + 4, :], Y[:, 4 * g:4 * g + 4, :], ACT.Copy).then_inc(S("mix_hi"), 1)
            def mem_columns():
                for g in range(8):
                    act.wait_ge(S("x_tr"), 8 + g + 1)
                    act.activation(Y[:, g % 4 * 4:g % 4 * 4 + 4, g // 4 * P:g // 4 * P + P],
                                   MB[:, g % 4, :].rearrange("p (c t) -> p c t", t=P), ACT.Copy).then_inc(S("x_t"), 1)

            def mem_square():
                act.wait_ge(S("x_t"), 16)
                square(1, Y[:, :, :])
            linear("w_out", steps=[(1, mem_columns), (2, mem_square), (4, lambda: root(1))])

            split("wk", 0)
            done(act, "w_out", 15)
            norm_parts(1)
            split("wk", 1)
            linear("wk", 0, then="wv", steps=[(1, lambda: square(2, XT[:, :, :]))])
            split("wv", 1)
            linear("wv", 16, then="wq", steps=[(2, lambda: root(2))])
            norm_parts(2)
            split("wq", 1)
            linear("wq", 32, then="wo")
            p = w2.rearrange("p (b a k) -> p b a k", b=4, k=T)
            pT = w3.rearrange("p (b a k) -> p b a k", b=4, k=T)
            for g in range(8):
                act.wait_ge(S("xv_tr"), g + 1)
                act.activation(W[:, g * 512:g * 512 + 512], MB[:, 2 + g % 2, :], ACT.Copy).then_inc(S("xv_rows"), 1)
            split("wo", 1)
            for h in range(X_HEADS):
                act.wait_ge(S("x_max"), h + 1)
                for a in range(TT):
                    act.activation(p[:, h, a, :], MB[:, h % 2, a * T:a * T + T], ACT.Exp, bias=NAS[:, 4 * h + a:4 * h + a + 1],
                                   scale=X_DH ** -0.5, accum_out=NAS[:, 4 * h + 2 + a:4 * h + 3 + a]).then_inc(S("x_exp"), 1)
            def x_hi(h):
                act.wait_ge(S("x_y"), 2 * h + 2)
                act.activation(xh[:, 4 * h:4 * h + 4, :], Y[:, 4 * h:4 * h + 4, :], ACT.Copy).then_inc(S("mix_hi"), 1)
            for h in range(X_HEADS):
                act.wait_ge(S("x_ptr"), h + 1)
                act.activation(pT[:, h], MB[:, 2, :].rearrange("p (a k) -> p a k", k=T), ACT.Copy).then_inc(S("x_pt"), 1)
                if h:
                    x_hi(h - 1)
                for b in range(2):
                    act.wait_ge(S("x_o"), 2 * h + b + 1)
                    act.activation(Y[:, 4 * h + 2 * b:4 * h + 2 * b + 2, :], MB[:, b, :].rearrange("p (a k) -> p a k", k=T), ACT.Copy).then_inc(S("x_y"), 1)
            x_hi(3)
            linear("wo", steps=square_early("wo"))
            norm_sq(3, XT[:, :, :], ph="moe")
            norm_parts(3)
            for a in range(TT):
                act.wait_ge(S("r_mm"), 1)
                act.activation(RT[:, 20 * a:20 * a + 20], MB[:, 1, 20 * a:20 * a + 20], ACT.Copy).then_inc(S("r_logits"), 1)
            act.wait_ge(S("r_exp_in"), 1)
            act.activation(RT[:, 48:56], RT[:, 48:56], ACT.Exp).then_inc(S("r_exp"), 1)
            act.wait_ge(S("r_exp_in"), 2)
            act.activation(RT[:, 116:118], RT[:, 116:118], ACT.Exp).then_inc(S("r_exp"), 1)

            def spread_weights():
                act.wait_ge(S("r_tr"), 1)
                act.activation(RT[0:16, 136:392], MB[0:16, 1, 0:T], ACT.Copy).then_inc(S("r_t"), 1)
                comb = Y
                for g in range(8):
                    act.wait_ge(S("r_bc"), g + 1)
                    act.activation(comb[:, 2 * g:2 * g + 2, :], MB[:, 2 + g % 2, :].rearrange("p (a k) -> p a k", k=T), ACT.Copy).then_inc(S("comb"), 1)
            sg = w0[:, 0:1024].rearrange("p (u c t) -> p u c t", u=2, t=T)
            hid = w0[:, 1024:2048].rearrange("p (u c t) -> p u c t", u=2, t=T)
            hh = w2[:, 0:512].bitcast(F16).rearrange("p (c t) -> p c t", t=T)

            def silu(e, u, j, i):
                done(act, "moe", j, i)
                act.activation(sg[:, u], GB[:, 2 * u, :].rearrange("p (c t) -> p c t", t=T), ACT.Silu, scale=INV).then_inc(bank_free[2 * u], 1)

            def hid_hi(e, u):
                act.wait_ge(S("hid"), e * 2 + u + 1)
                act.activation(hh[:, 2 * u:2 * u + 2, :], hid[:, u], ACT.Copy).then_inc(S("hid_hi"), 1)
            for j in range(8):
                if j >= 2:
                    split("moe", j)
                if j == 4:
                    spread_weights()
                    silu(0, 0, 1, 0)
                if j == 5:
                    hid_hi(0, 0)
                if j == 7:
                    silu(0, 1, 5, 0)
            with act.Fori(0, N_EXP - 1) as n:
                e, i = n + 1, n * 3
                for j in range(12):
                    split("moe", 8 + j, i)
                    if j == 1:
                        hid_hi(n, 1)
                    if j == 3:
                        silu(e, 0, 8 + 1, i)
                    if j == 9:
                        done(act, "moe", 8 + 7, i)
                        hid_hi(e, 0)
                    if j == 11:
                        silu(e, 1, 8 + 9, i)
            for j in range(4):
                split("moe", 8 + j, 3 * (N_EXP - 1))
                if j == 1:
                    hid_hi(N_EXP - 1, 1)
            norm_sq(4, XT[:, :, :], Y[:, :, :], ph="z0")

            for l in range(LAYERS):
                if l:
                    split(f"z{l}", 0)
                if l == 0:
                    act.wait_ge(S("norm_out4"), 4)
                norm_sq(5 + l, XT[:, :, :], Zn if l else Y[:, :, :])
                if l:
                    split(f"z{l}", 1)
                norm_parts(4 + l, shift=lambda c: MOD[:, l, c:c + 1], src=Y)
                ph = f"z{l}"

                def evict(chunk, u, i, j=0):
                    done(act, ph, 2 * u + 1 + j, i)
                    act.activation(Z[:, bass.ds(chunk, 2), :], GB[:, u, :].rearrange("p (c t) -> p c t", t=T),
                                   ACT.Copy, scale=INV).then_inc(bank_free[u], 1)

                def piece(n, i, j, last):
                    if last is not None:
                        split(ph, j, i)
                        split(ph, j + 1, i)
                        evict(last, 1, i, j - 4)
                    split(ph, j + 2, i)
                    split(ph, j + 3, i)
                    evict(n * 4, 0, i, j)
                piece(EARLY, 0, 0, None)
                with act.Fori(0, PIECES - EARLY - 1) as i:
                    piece(i + EARLY + 1, i, 4, i * 4 + (4 * EARLY + 2))
                late = 4 * (PIECES - EARLY)
                piece(0, 0, late, 4 * PIECES - 2)
                read_early = uses[ph][1] + PIECES - EARLY
                act.wait_ge(bank_free[1], read_early)
                act.activation(Z[:, 44:48, :], Z[:, 44:48, :], ACT.Sigmoid).then_inc(S("b_sig"), 1)
                act.activation(Z[:, 48:52, :], Z[:, 48:52, :], ACT.Silu).then_inc(S("gates"), 1)
                with act.Fori(0, EARLY - 1) as i:
                    piece(i + 1, i, late + 4, i * 4 + 2)
                evict(4 * EARLY - 2, 1, EARLY - 1, late)
                read_out(act, f"fft{l}")
                act.wait_ge(S("conv_sum"), l + 1)
                act.activation(ssum, GB[:, 2, 0:T], ACT.Copy, scale=1.0 / 512).then_inc(S("conv_mean"), 1)
                for c in (4, 20, 36):
                    act.activation(Z[:, c:c + 4, :], Z[:, c:c + 4, :], ACT.Silu).then_inc(S("gates"), 1)
                nv = w3[:, 1024:2048].rearrange("p (a n) -> p a n", a=TT)
                rv = w3[:, 0:1024].rearrange("p (a n) -> p a n", a=TT)
                for k, dst in enumerate((nv, rv)):
                    for a in range(TT):
                        act.wait_ge(S("zv_tr"), 4 * l + 2 * k + a + 1)
                        act.activation(dst[:, a, :], MB[:, 2 * k + a, :], ACT.Copy).then_inc(S("zv_rows"), 1)
                act.wait_ge(S("conv_c"), l + 1)
                act.activation(csq, ca, ACT.Square).then_inc(S("conv_sq"), 1)
                fa = w2.rearrange("p (b n) -> p b n", n=512)
                for b in range(4):
                    act.wait_ge(S("fft_ch"), 4 * l + b + 1)
                    act.activation(fa[:, b, :], MB[:, b, :], ACT.Copy).then_inc(S("fft_a"), 1)
                act.wait_ge(S("conv_var"), l + 1)
                act.activation(nstd, GB[:, 3, 0:T], ACT.Sqrt, bias=eps[:, :], scale=1.0 / 512).then_inc(S("conv_std"), 1)
                fy = Z[:, 0:4, :]
                for b in range(2):
                    act.wait_ge(S("fft_tok"), 2 * l + b + 1)
                    act.activation(fy[:, 2 * b:2 * b + 2, :], MB[:, b, :].rearrange("p (a k) -> p a k", k=T), ACT.Copy).then_inc(S("fft_y"), 1)
                act.wait_ge(S("conv_n"), 4 * l + 4)
                act.activation(ca, ca, ACT.Silu).then_inc(S("conv_s"), 1)

                def na_exp(h):
                    pr = w2[:, h % 2 * 512:h % 2 * 512 + 512].rearrange("p (a k) -> p a k", k=T)
                    act.wait_ge(S("na_max"), 8 * l + h + 1)
                    for a in range(TT):
                        act.activation(pr[:, a, :], MB[:, h % 2, a * T:a * T + T], ACT.Exp, scale=DH ** -0.5, bias=NAS[:, 4 * (h % 2) + a:4 * (h % 2) + a + 1],
                                       accum_out=NAS[:, 4 * (h % 2) + 2 + a:4 * (h % 2) + 3 + a]).then_inc(S("na_exp"), 1)
                ahead_of(f"mix{l}")

                def mixed_hi(g, n):
                    act.wait_ge(S("mixed"), 4 * l + n)
                    act.activation(xh[:, 4 * g:4 * g + 4, :], Y[:, 4 * g:4 * g + 4, :], ACT.Copy).then_inc(S("mix_hi"), 1)
                na_exp(0)
                for h in range(HEADS):
                    dt = Z[:, 40 + h % 2 * 2:42 + h % 2 * 2, :]
                    act.wait_ge(S("decay_e"), 8 * l + h + 1)
                    act.activation(dt, dt, ACT.Exp).then_inc(S("decay"), 1)
                    if h + 1 < HEADS:
                        na_exp(h + 1)
                    pt = w2[:, 1024 + h % 2 * 512:1536 + h % 2 * 512]
                    act.wait_ge(S("na_ptr"), 8 * l + h + 1)
                    act.activation(pt, MB[:, 2, :], ACT.Copy).then_inc(S("na_pt"), 1)
                    if h == 3:
                        mixed_hi(0, 1)
                    if h == 5:
                        mixed_hi(3, 2)
                act.wait_ge(S("ret_o"), 4 * l + 4)
                act.activation(Z[:, 8:12, :], Z[:, 28:32, :], ACT.Square).then_inc(S("ret_sq"), 1)
                mixed_hi(1, 3)
                act.wait_ge(S("ret_ms"), l + 1)
                ms = MB[:, 0:2, :].rearrange("p b (a k) -> p (b a) k", k=T)
                act.activation(Z[:, 8:12, :], ms, ACT.Ln, bias=eps[:, :], scale=1.0 / DH).then_inc(S("ret_std"), 1)
                act.wait_ge(S("ret_std"), 2 * l + 1)
                act.activation(Z[:, 8:12, :], Z[:, 8:12, :], ACT.Exp, scale=-0.5).then_inc(S("ret_std"), 1)
                mixed_hi(2, 4)
                linear(f"mix{l}", steps=square_early(f"mix{l}"))
            norm_sq(7, XT[:, :, :])
            for g in range(8):
                act.wait_ge(S("out_tr"), g + 1)
                act.activation(W[:, g * 512:g * 512 + 512], MB[:, g % 4, :], ACT.Copy).then_inc(S("out_rows"), 1)

        @block.vector
        def _(dve):
            steps = [0]

            def link(ins, wait=True):
                steps[0] += 1
                ins.then_inc(S("dve_step"), 1)
                if wait:
                    dve.wait_ge(S("dve_step"), steps[0])

            def split(ph, j, i=0):
                b, s = at[ph][0] + j, at[ph][1] + j
                dve.wait_ge(hi_done, s + 1 + 4 * i)
                dve.scalar_tensor_tensor(w_lo[:, s % SPL, :], raw[:, b % RAW, :], W_SCALE, w_hi[:, s % SPL, :],
                                         ALU.mult, ALU.subtract).then_inc(raw_taken[b % RAW], 1)

            def linear(ph, add=False, gate=None, steps=(), then=None):
                def evict(u, i):
                    done(dve, ph, 2 * u + 1, i)
                    if gate is None:
                        x = XT[:, bass.ds(i * 4 + 2 * u, 2), :]
                        dve.scalar_tensor_tensor(x, GB[:, u, :].rearrange("p (c t) -> p c t", t=T), INV, x,
                                                 ALU.mult, ALU.add).then_inc(bank_free[u], 1)
                        return
                    for k in range(2):
                        x = XT[:, bass.ds(i * 4 + 2 * u + k, 1), :]
                        ins = dve.scalar_tensor_tensor(x, GB[:, u:u + 1, k * T:k * T + T], gate[:, bass.ds(i * 4 + 2 * u + k, 1)], x,
                                                       ALU.mult, ALU.add)
                    ins.then_inc(bank_free[u], 1)

                def body(i, first):
                    for u in range(2):
                        if not (first and u == 0):
                            split(ph, 2 * u, i)
                            split(ph, 2 * u + 1, i)
                        if add and not (first and u == 0):
                            evict(1 - u, i - 1 + u)
                n = at[ph][2] // 4
                body(0, True)
                steps_between(dve, n, body, steps)
                if then is not None:
                    split(then, 0)
                if add:
                    evict(1, n - 1)

            def newton(r, tmp, v):
                link(dve.tensor_tensor(tmp, r, r, ALU.mult))
                link(dve.scalar_tensor_tensor(tmp, tmp, -0.5, v, ALU.mult, ALU.mult))
                link(dve.scalar_tensor_tensor(r, tmp, 1.5, r, ALU.add, ALU.mult))

            def inverse_root(r, root, v):
                link(dve.reciprocal(r, root))
                newton(r, root, v)

            def ahead_of(ph):
                split(ph, 0)
                split(ph, 1)

            def sum_early(n):
                def step():
                    dve.wait_ge(S("early_sq"), EARLY_SUMS.index(n) + 1)
                    dve.tensor_reduce(rstd, Zn[:, 0:12, :].rearrange("p c t -> p t c"), AX.X, ALU.add).then_inc(S("early_sum"), 1)
                return [(4, step)]

            def sums(n, squares=Zn):
                dve.wait_ge(S("norm_sq"), n + 1)
                c = 12 if n in EARLY_SUMS else 0
                dve.tensor_reduce(ssum, squares[:, c:, :].rearrange("p c t -> p t c"), AX.X, ALU.add).then_inc(S("norm_sum"), 1)

            def means(n):
                dve.wait_ge(S("norm_ms"), n + 1)
                dve.tensor_scalar(ssum, MB[:, 0, 0:T], 1.0 / D, EPS, ALU.mult, ALU.add).then_inc(S("norm_var"), 1)

            def norm_root(n):
                dve.wait_ge(S("norm_std"), n + 1)
                inverse_root(rstd, nstd, ssum)
                if n == 0:
                    dve.wait_ge(S("cols"), ROW_TILES)

            def apply(n, g, src, gain, dst=Zn, ready="norm_h"):
                for c in range(4 * g, 4 * g + 4):
                    ins = dve.scalar_tensor_tensor(dst[:, c, :], src[:, c, :], gain(c), rstd, ALU.mult, ALU.mult)
                ins.then_inc(S(ready), 1)

            def norm_lo(k, g, shift=None, src=Zn):
                dve.wait_ge(S("norm_hi"), 4 * k + g + 1)
                if shift is not None:
                    for c in range(4 * g, 4 * g + 4):
                        ins = dve.scalar_tensor_tensor(xl[:, c, :], src[:, c, :], shift(c), xh[:, c, :], ALU.add, ALU.subtract)
                    ins.then_inc(S("norm_lo"), 1)
                    return
                dve.tensor_tensor(xl[:, 4 * g:4 * g + 4, :], src[:, 4 * g:4 * g + 4, :], xh[:, 4 * g:4 * g + 4, :],
                                  ALU.subtract).then_inc(S("norm_lo"), 1)

            def finish_norm(n, src, gain, parts, shift=None, ph=None, dst=Zn):
                norm_root(n)
                for half in (0, 2):
                    apply(n, half, src, gain, dst)
                    apply(n, half + 1, src, gain, dst)
                    norm_lo(parts, half, shift, dst)
                    norm_lo(parts, half + 1, shift, dst)
                    if ph is not None and half == 0:
                        split(ph, 1)

            def norm(n, src, gain, parts, shift=None, ph=None, squares=Zn, dst=Zn):
                sums(n, squares)
                means(n)
                finish_norm(n, src, gain, parts, shift, ph, dst)

            def norm_out(n, gain, dst=Zn, squares=Zn, ph=None):
                if ph is not None:
                    split(ph, 0)
                sums(n, squares)
                means(n)
                norm_root(n)
                for g in range(4):
                    apply(n, g, XT, gain, dst, ready=f"norm_out{n}")
                    if ph is not None and g == 1:
                        split(ph, 1)

            sums(0)
            split("w_in", 0)
            means(0)
            finish_norm(0, XT, lambda c: col("norm_mix", c), parts=0, ph="w_in")
            dve.wait_ge(S("cols"), ROW_TILES)
            dve.tensor_tensor(SM[:, 0:8], col("hgrn_lb_logits", 0, 8), col("hgrn_lb_logits", 8, 8), ALU.subtract).then_inc(S("lb_diff"), 1)
            Fh = Z[:, 16:24, :]
            F = Fh.rearrange("p h t -> p (h t)")
            Q = Z[:, 8:16, :].rearrange("p h t -> p (h t)")
            EO = Z[:, 48:52, :].rearrange("p h t -> p (h t)").rearrange("p (g s) -> p g s", s=HALF)
            Y1 = Y[:, 8:16, :].rearrange("p h t -> p (h t)")
            NG = HEADS * NCH

            def by_chunk(ap):
                return ap.rearrange("p (g s) -> p g s", s=SUB)
            a = by_chunk(w1)
            ah = w1.rearrange("p (g s) -> p g s", s=HALF)

            def gates():
                dve.wait_ge(S("f_sig"), 1)
                dve.wait_ge(S("lb"), 2)
                for h in range(HEADS):
                    link(dve.tensor_scalar(Fh[:, h, :], Fh[:, h, :], SM[:, 16 + h:17 + h], SM[:, 8 + h:9 + h], ALU.mult, ALU.add), wait=h == HEADS - 1)

            def keys():
                dve.tensor_scalar(w0, F, -1.0, 1.0, ALU.mult, ALU.add).then_inc(S("k_ready"), 1)

            def running(k):
                if k == 0:
                    dve.wait_ge(S("log_f"), 1)
                src, dst = (by_chunk(w) for w in ((F, w1), (w1, F))[k % 2])
                d = 1 << k
                link(dve.tensor_copy(dst[:, :, 0:d], src[:, :, 0:d]), wait=False)
                link(dve.tensor_tensor(dst[:, :, d:], src[:, :, d:], src[:, :, 0:SUB - d], ALU.add))

            def exponents(k):
                if k == 0:
                    dve.tensor_tensor(F.rearrange("p (g s) -> p g s", s=HALF), ah, ah[:, :, HALF // 2 - 1:HALF // 2].broadcast_to([P, 2 * NG, HALF]),
                                      ALU.subtract).then_inc(S("exponents"), 1)
                elif k == 1:
                    dve.wait_ge(S("pooled"), 4)
                    dve.tensor_tensor(EO, a[:, :, HALF + HALF // 2 - 1:HALF + HALF // 2].broadcast_to([P, NG, HALF]), a[:, :, 0:HALF],
                                      ALU.subtract).then_inc(S("exponents"), 1)
                else:
                    dve.tensor_tensor(by_chunk(Y1), a[:, :, SUB - 1:SUB].broadcast_to([P, NG, SUB]), a, ALU.subtract).then_inc(S("exponents"), 1)
            y1p, y, um, isone = LG[:, 32:64], LG[:, 64:96], RT[:, 0:32], RT[:, 32:64]

            def decay_abs():
                dve.wait_ge(S("logits_in"), 32)
                dve.scalar_tensor_tensor(y1p, LG[:, 0:32], -1.0, LG[:, 0:32], ALU.mult, ALU.max).then_inc(S("lg_abs"), 1)

            def decay_u():
                dve.wait_ge(S("lg_exp"), 1)
                dve.tensor_scalar(y1p, y, 1.0, None, ALU.add).then_inc(S("lg_u"), 1)
                dve.wait_ge(S("lg_u"), 1)
                link(dve.tensor_scalar(um, y1p, -1.0, 1e-30, ALU.add, ALU.max))
                link(dve.reciprocal(um, um))
                link(dve.tensor_scalar(isone, y1p, 1.0, None, ALU.is_le))
                link(dve.tensor_tensor(isone, isone, y, ALU.mult))

            def decay_log():
                dve.wait_ge(S("lg_ln"), 1)
                link(dve.tensor_tensor(um, um, y, ALU.mult))
                link(dve.tensor_tensor(um, um, RT[:, 64:96], ALU.mult))
                link(dve.tensor_tensor(um, um, isone, ALU.add))
                link(dve.scalar_tensor_tensor(LG[:, 0:32], LG[:, 0:32], 0.0, um, ALU.min, ALU.subtract))
            beside = {8: decay_abs, 13: gates, 15: keys, 18: decay_u, 26: decay_log}
            for k in range(5):
                beside[21 + 2 * k] = lambda k=k: running(k)
            for k in range(3):
                beside[31 + 2 * k] = lambda k=k: exponents(k)
            for j in range(2, 40):
                split("w_in", j)
                if j in beside:
                    beside[j]()
            k0 = by_chunk(Z[:, 0:8, :].rearrange("p h t -> p (h t)"))
            k1 = by_chunk(Z[:, 24:32, :].rearrange("p h t -> p (h t)"))
            kk = by_chunk(w0)
            dve.wait_ge(S("exp_q"), 1)
            dve.wait_ge(S("q_silu"), 1)
            dve.tensor_tensor(w2, w2, Q, ALU.mult).then_inc(S("q_intra"), 1)
            dve.wait_ge(S("exp_k"), 3)
            dve.wait_ge(S("zeros"), 2)
            fk = by_chunk(F)
            dve.tensor_tensor(k0[:, :, 0:HALF], kk[:, :, 0:HALF], fk[:, :, 0:HALF], ALU.mult).then_inc(S("k_intra"), 1)
            dve.wait_ge(S("v_tr"), 4)
            dve.tensor_tensor(k1[:, :, HALF:], kk[:, :, HALF:], fk[:, :, HALF:], ALU.mult).then_inc(S("k_intra"), 1)
            dve.tensor_tensor(k1[:, :, 0:HALF], kk[:, :, 0:HALF], EO, ALU.mult).then_inc(S("k_intra"), 1)
            dve.tensor_tensor(Y1, Y1, w0, ALU.mult).then_inc(S("state_k"), 1)
            dve.wait_ge(S("exp_a"), 1)
            dve.wait_ge(S("q_intra"), 1)
            dve.tensor_tensor(Q, Q, H0, ALU.mult).then_inc(S("q_inter"), 1)
            bd = w3.rearrange("p (a h t) -> p a h t", a=TT, t=P)
            causal = const("causal")
            dve.wait_ge(S("zeros"), 1)
            for t in range(TT):
                dve.wait_ge(S("scores"), t + 1)
                for c in range(4):
                    r = slice(SUB * c, SUB * c + SUB)
                    dve.tensor_tensor(bd[r, t, :, r], MB[r, t, 0:T].rearrange("p (h s) -> p h s", s=SUB),
                                      causal[r, None, :].broadcast_to([SUB, HEADS, SUB]), ALU.mult).then_inc(S("bd"), 1)
            dec = H0.rearrange("p (h t) -> p h t", t=T)
            st = w1.rearrange("p (b h v) -> p b h v", b=2, v=P)
            tmp = EO.rearrange("p g s -> p (g s)").rearrange("p (h v) -> p h v", v=P)
            dve.wait_ge(S("exp_a"), 1)
            for c in range(NCH - 1):
                kv = MB[:, 2:4, :].rearrange("p b (h v) -> p (b h) v", v=P)
                if c:
                    last = dec[:, :, c * SUB + SUB - 1:c * SUB + SUB]
                    dve.wait_ge(S("state"), c)
                    link(dve.tensor_tensor(tmp, st[:, c % 2], last.broadcast_to([P, HEADS, P]), ALU.mult))
                dve.wait_ge(S("kv"), c + 1)
                if c:
                    dve.tensor_tensor(st[:, (c + 1) % 2], tmp, kv, ALU.add).then_inc(S("state"), 1)
                else:
                    dve.tensor_copy(st[:, 1], kv).then_inc(S("state"), 1)
            G = Z[:, 32:40, :].rearrange("p h t -> p (h t)")
            R = Z[:, 24:32, :].rearrange("p h t -> p (h t)")
            VAR = Z[:, 0:8, :].rearrange("p h t -> p (h t)")
            dve.wait_ge(S("g_silu"), 1)
            link(dve.tensor_scalar(G, G, col("hgrn_norm"), None, ALU.mult))
            split("w_out", 0)
            dve.wait_ge(S("o_copied"), TT)
            link(dve.tensor_tensor(Y1, F, G, ALU.mult))
            split("w_out", 1)
            dve.wait_ge(S("mix_hi"), 1)
            dve.tensor_tensor(xl[:, 0:8, :], Y[:, 0:8, :], xh[:, 0:8, :], ALU.subtract).then_inc(S("mix_lo"), 1)
            dve.wait_ge(S("o_std"), 1)
            dve.tensor_scalar(VAR, MB[:, :, :].rearrange("p b n -> p (b n)"), 1.0 / P, EPS, ALU.mult, ALU.add).then_inc(S("o_var"), 1)
            dve.wait_ge(S("o_var"), 1)
            dve.wait_ge(S("o_std"), 2)
            newton(w0, R, VAR)
            for g in (2, 3):
                dve.tensor_tensor(Y[:, 4 * g:4 * g + 4, :], Y[:, 4 * g:4 * g + 4, :], chunks(w0)[:, 4 * g - 8:4 * g - 4, :], ALU.mult).then_inc(S("hgrn_y"), 1)
            for g in (2, 3):
                dve.wait_ge(S("mix_hi"), g)
                dve.tensor_tensor(xl[:, 4 * g:4 * g + 4, :], Y[:, 4 * g:4 * g + 4, :], xh[:, 4 * g:4 * g + 4, :], ALU.subtract).then_inc(S("mix_lo"), 1)

            def finish_memory(g):
                apply(1, g, Y, lambda c: col("norm_mem", c))
                apply(1, g + 1, Y, lambda c: col("norm_mem", c))

            def start_memory():
                means(1)
                norm_root(1)
                split("wk", 0)
                finish_memory(0)
            linear("w_out", add=True, steps=[(3, lambda: sums(1)), (4, start_memory)])

            norm_lo(1, 0)
            norm_lo(1, 1)
            finish_memory(2)
            norm_lo(1, 2)
            norm_lo(1, 3)
            split("wk", 1)
            linear("wk", steps=[(2, lambda: sums(2))])
            ahead_of("wv")

            def finish_queries(g):
                apply(2, g, XT, lambda c: col("norm_xattn", c))
                apply(2, g + 1, XT, lambda c: col("norm_xattn", c))

            def start_queries():
                norm_root(2)
                finish_queries(0)
            linear("wv", steps=[(1, lambda: means(2)), (3, start_queries), (4, lambda: finish_queries(2))])
            split("wq", 0)
            for g in range(4):
                norm_lo(2, g)
            split("wq", 1)
            linear("wq")
            ahead_of("wo")
            p = w2.rearrange("p (b a k) -> p b a k", b=4, k=T)
            for h in range(X_HEADS):
                dve.wait_ge(S("x_sc"), h + 1)
                m = NAS[:, 4 * h:4 * h + 2]
                link(dve.tensor_reduce(m, MB[:, h % 2, :].rearrange("p (a k) -> p a k", k=T), AX.X, ALU.max))
                dve.tensor_scalar(m, m, -(X_DH ** -0.5), None, ALU.mult).then_inc(S("x_max"), 1)
                dve.wait_ge(S("x_exp"), 2 * h + 2)
                s = NAS[:, 4 * h + 2:4 * h + 4]
                link(dve.reciprocal(s, s))
                for t in range(TT):
                    dve.tensor_scalar(p[:, h, t, :], p[:, h, t, :], s[:, t:t + 1], None, ALU.mult).then_inc(S("x_p"), 1)
            for h in range(X_HEADS):
                dve.wait_ge(S("mix_hi"), 3 + h + 1)
                dve.tensor_tensor(xl[:, 4 * h:4 * h + 4, :], Y[:, 4 * h:4 * h + 4, :], xh[:, 4 * h:4 * h + 4, :], ALU.subtract).then_inc(S("mix_lo"), 1)
            linear("wo", add=True, steps=sum_early(3), then="moe")
            norm(3, XT, lambda c: col("norm_ffn", c), parts=3, ph="moe")

            def v2(a, n):
                return RT[:, a:a + 2 * n].rearrange("p (t n) -> p t n", t=2)

            def spread(ap, n):
                return ap.broadcast_to([P, 2, n])
            lg = RT[:, 0:40].rearrange("p (t n) -> p t n", t=2)
            lgg = lg[:, :, 0:GROUPS]
            prio = const("prio")[:, None, :].broadcast_to([P, 2, 4])
            mx, shift, ssm, pg, eq, gsel = v2(40, 1), v2(48, 4), v2(56, 1), v2(58, 1), v2(60, 4), v2(68, 4)
            sel, m1, oh1, sel2, m2, oh2 = v2(76, 4), v2(84, 1), v2(86, 4), v2(94, 4), v2(102, 1), v2(104, 4)
            gap, den, wa, wb, ce = v2(116, 1), v2(118, 1), v2(120, 1), v2(122, 1), v2(124, 4)
            big = CMB[:, :].rearrange("p (t g e) -> p t g e", t=2, e=4)
            dve.wait_ge(S("r_logits"), 2)

            def first_max(dst, vals, m):
                link(dve.tensor_reduce(m, vals, AX.X, ALU.max))
                link(dve.tensor_tensor(eq, vals, spread(m, 4), ALU.is_ge))
                link(dve.tensor_tensor(eq, eq, prio, ALU.mult))
                link(dve.tensor_reduce(ssm, eq, AX.X, ALU.max))
                link(dve.tensor_tensor(dst, eq, spread(ssm, 4), ALU.is_ge))
            first_max(gsel, lgg, mx)
            dve.tensor_tensor(shift, lgg, spread(mx, 4), ALU.subtract).then_inc(S("r_exp_in"), 1)
            dve.wait_ge(S("r_exp"), 1)
            link(dve.tensor_reduce(ssm, shift, AX.X, ALU.add))
            link(dve.reciprocal(pg, ssm))
            for g in range(GROUPS):
                part = lg[:, :, GROUPS + 4 * g:GROUPS + 4 * g + 4]
                link(dve.tensor_tensor(big[:, :, g, :], part, spread(gsel[:, :, g:g + 1], 4), ALU.mult))
            link(dve.tensor_reduce(sel, big.rearrange("p t g e -> p t e g"), AX.X, ALU.add))
            first_max(oh1, sel, m1)
            link(dve.scalar_tensor_tensor(sel2, oh1, NEG, sel, ALU.mult, ALU.add))
            first_max(oh2, sel2, m2)
            dve.tensor_tensor(gap, m2, m1, ALU.subtract).then_inc(S("r_exp_in"), 1)
            dve.wait_ge(S("r_exp"), 2)
            link(dve.tensor_scalar(den, gap, 1.0, None, ALU.add))
            link(dve.reciprocal(wa, den))
            link(dve.tensor_tensor(wa, wa, pg, ALU.mult))
            link(dve.tensor_tensor(wb, wa, gap, ALU.mult))
            link(dve.tensor_tensor(oh1, oh1, spread(wa, 4), ALU.mult))
            link(dve.tensor_tensor(oh2, oh2, spread(wb, 4), ALU.mult))
            link(dve.tensor_tensor(ce, oh1, oh2, ALU.add))
            for g in range(GROUPS):
                dve.tensor_tensor(big[:, :, g, :], ce, spread(gsel[:, :, g:g + 1], 4), ALU.mult).then_inc(S("combine"), 1)

            sg = w0[:, 0:1024].rearrange("p (u c t) -> p u c t", u=2, t=T)
            hid = w0[:, 1024:2048].rearrange("p (u c t) -> p u c t", u=2, t=T)
            hh = w2[:, 0:512].bitcast(F16).rearrange("p (c t) -> p c t", t=T)
            hl = w2[:, 512:1024].bitcast(F16).rearrange("p (c t) -> p c t", t=T)
            comb = Y
            dve.wait_ge(S("c_silu"), 1)
            dve.wait_ge(S("norm_lo"), 16)
            dve.wait_ge(S("r_mm"), 1)

            def modulate(e, q, first):
                n = e * (N_SUMS // 2) + q // 2
                dve.wait_ge(ada_full[q % 2], n * 16 + 16)
                sums, w = SUMS[:, q * BLK:(q + 1) * BLK], ADA[:, q % 2, :]
                if first:
                    dve.tensor_scalar(sums, w, SM[:, 24:25], None, ALU.mult).then_inc(ada_used[q % 2], 1)
                    return
                dve.wait_ge(ada_used[q % 2], n - (N_SUMS // 2 - 1))
                dve.scalar_tensor_tensor(sums, w, SM[:, bass.ds(e + 24, 1)], sums, ALU.mult, ALU.add).then_inc(ada_used[q % 2], 1)

            base = uses["moe"]

            def lo(j, i):
                split("moe", j, i)

            def weigh(e, u, read):
                dve.wait_ge(bank_free[2 * u], read)
                dve.tensor_tensor(sg[:, u], sg[:, u], comb[:, bass.ds(e, 1), :].broadcast_to([P, 2, T]), ALU.mult).then_inc(S("weighted"), 1)

            def make_hid(e, u, j, i):
                done(dve, "moe", j, i)
                step = e * 2 + u + 1
                dve.wait_ge(S("weighted"), step)
                dve.scalar_tensor_tensor(hid[:, u], GB[:, 2 * u + 1, :].rearrange("p (c t) -> p c t", t=T), INV, sg[:, u],
                                         ALU.mult, ALU.mult).then_inc(S("hid"), 1)
                dve.wait_ge(S("hid"), step)
                dve.sem_inc(bank_free[2 * u + 1], 1)

            def hid_lo(e, u):
                dve.wait_ge(S("hid_hi"), e * 2 + u + 1)
                dve.tensor_tensor(hl[:, 2 * u:2 * u + 2, :], hid[:, u], hh[:, 2 * u:2 * u + 2, :], ALU.subtract).then_inc(S("hid_lo"), 1)

            def add(d, j, i):
                done(dve, "moe", j + d, i)
                for q in range(2):
                    c, b = 4 * d + 2 * q, (2 * d + q + 2) % 4
                    dve.scalar_tensor_tensor(XT[:, c:c + 2, :], GB[:, b, :].rearrange("p (c t) -> p c t", t=T), INV, XT[:, c:c + 2, :],
                                             ALU.mult, ALU.add).then_inc(bank_free[b], 1)
            for j in range(8):
                if j >= 2:
                    lo(j, 0)
                if j < N_SUMS:
                    modulate(0, j, True)
                if j == 4:
                    dve.wait_ge(S("comb"), 8)
                    weigh(0, 0, base[0] + 1)
                if j == 5:
                    make_hid(0, 0, 3, 0)
                    hid_lo(0, 0)
            weigh(0, 1, base[2] + 1)
            with dve.Fori(0, N_EXP - 1) as n:
                e, i = n + 1, n * 3
                for j in range(12):
                    lo(8 + j, i)
                    if j == 1:
                        make_hid(n, 1, 7, i)
                    if j == 2:
                        hid_lo(n, 1)
                    if j == 4:
                        weigh(e, 0, n * 3 + base[0] + 2)
                    if j == 5:
                        make_hid(e, 0, 8 + 3, i)
                    if 6 <= j <= 9:
                        add(j - 6, 8 + 4, i)
                    if j == 9:
                        hid_lo(e, 0)
                    if j == 11:
                        weigh(e, 1, n * 3 + base[2] + 4)
                    if j % 2 == 0:
                        modulate(e, j // 2, False)
            last = 3 * (N_EXP - 1)
            for j in range(4):
                lo(8 + j, last)
                if j == 1:
                    make_hid(N_EXP - 1, 1, 7, last)
                    hid_lo(N_EXP - 1, 1)
                if j >= 2:
                    add(j - 2, 8, last)
            add(2, 8, last)
            add(3, 8, last)
            norm_out(4, lambda c: col("norm_final", c), dst=XT, squares=Y, ph="z0")

            for l in range(LAYERS):
                read_out(dve, f"z{l}")
                if l == 0:
                    dve.wait_ge(S("ada"), 2)
                    link(dve.tensor_tensor(MOD[:, 0, :], MB[:, 1, 0:3 * KC], col("b_ada_2", 0, 3 * KC), ALU.add))
                link(dve.scalar_tensor_tensor(GAIN[:, :], MOD[:, l, KC:2 * KC], 1.0, col("norm_g_2", KC * l, KC), ALU.add, ALU.mult))
                link(dve.tensor_scalar(MOD[:, l, 2 * KC:], MOD[:, l, 2 * KC:], INV, None, ALU.mult))
                dve.sem_inc(S("x_ready"), 1)
                norm(5 + l, XT, lambda c: GAIN[:, c:c + 1], parts=4 + l, shift=lambda c: MOD[:, l, c:c + 1], ph=f"z{l}" if l else None, squares=Zn if l else Y, dst=Y)
                if l == 0:
                    dve.wait_ge(S("ada"), 4)
                    link(dve.tensor_tensor(MOD[:, 1, :], MB[:, 2, 0:3 * KC], col("b_ada_2", 3 * KC, 3 * KC), ALU.add))
                ph = f"z{l}"
                late = 4 * (PIECES - EARLY)
                split(ph, 2)
                split(ph, 3)
                with dve.Fori(1, PIECES - EARLY + 1) as i:
                    for j in range(4):
                        split(ph, j, i)
                pad = TAPS // 2
                link(dve.memset(CU[:, :, 0:pad], 0.0), wait=False)
                link(dve.memset(CU[:, :, pad + T:], 0.0), wait=False)
                dve.wait_ge(S("b_sig"), l + 1)
                link(dve.tensor_tensor(CU[:, :, pad:pad + T], Z[:, 40:44, :], Z[:, 44:48, :], ALU.mult))

                def tap_at(c, k):
                    return CU[:, c, bass.ds(k, T)], PC[:, bass.ds(k * 4 + (row_at["conv_w_2"] + l * TAPS * 4 + c), 1)]
                n_taps = 4 * TAPS * l
                for c in range(4):
                    dve.tensor_scalar(ca[:, c, :], CU[:, c, 0:T], col("conv_w_2", l * TAPS * 4 + c), col("conv_b_2", 4 * l + c),
                                      ALU.mult, ALU.add).then_inc(S("tap"), 1)

                def tap(c, k, tail=False):
                    dve.wait_ge(S("tap"), k * 4 + (n_taps + c - 3))
                    x, w = (CU[:, c, k:k + T], col("conv_w_2", (l * TAPS + k) * 4 + c)) if tail else tap_at(c, k)
                    dve.scalar_tensor_tensor(ca[:, c, :], x, w, ca[:, c, :], ALU.mult, ALU.add).then_inc(S("tap"), 1)
                with dve.Fori(0, EARLY - 1) as i:
                    for j in range(4):
                        split(ph, late + 4 + j, i)
                        for n in range(3 * j, 3 * j + 3):
                            tap(n % 4, i * 3 + (1 + n // 4))
                for k in range(3 * (EARLY - 1) + 1, TAPS):
                    for c in range(4):
                        tap(c, k, True)
                dve.wait_ge(S("tap"), n_taps + 4 * TAPS)
                dve.sem_inc(S("conv_a"), 1)
                read_out(dve, f"fft{l}")
                dve.wait_ge(S("conv_mean"), l + 1)
                dve.tensor_tensor(ca, ca, ssum[:, None, :].broadcast_to([P, 4, T]), ALU.subtract).then_inc(S("conv_c"), 1)
                cos, sin = const("rope_cos"), const("rope_sin")

                def rotary(c):
                    tmp = RO[:, c % 2, :]
                    dve.wait_ge(S("rot"), 8 * l + c + 1)
                    link(dve.tensor_tensor(tmp, GB[:, c % 2, 0:T], sin, ALU.mult))
                    link(dve.tensor_tensor(Z[:, 24 + c, :], Z[:, 24 + c, :], cos, ALU.mult))
                    dve.tensor_tensor(Z[:, 24 + c, :], Z[:, 24 + c, :], tmp, ALU.add).then_inc(S("rotated"), 1)
                for c in range(6):
                    rotary(c)
                dve.wait_ge(S("conv_std"), l + 1)
                dve.wait_ge(S("conv_c"), l + 1)
                link(dve.reciprocal(rstd, nstd))
                link(dve.tensor_tensor(ca, ca, rstd[:, None, :].broadcast_to([P, 4, T]), ALU.mult))
                for c in range(4):
                    dve.tensor_scalar(ca[:, c, :], ca[:, c, :], col("conv_ln_g_2", 4 * l + c), col("conv_ln_b_2", 4 * l + c), ALU.mult, ALU.add).then_inc(S("conv_n"), 1)
                rotary(6)
                rotary(7)
                dve.wait_ge(S("gates"), 4 * l + 4)
                dve.wait_ge(S("fft_w"), l + 1)
                dve.tensor_tensor(Y[:, 0:4, :], MB[:, 2:4, :].rearrange("p b (a k) -> p (b a) k", k=T), Z[:, 4:8, :], ALU.mult).then_inc(S("mixed"), 1)

                def na_gate(c):
                    dve.wait_ge(S("na_o"), 4 * l + c + 1)
                    dve.tensor_tensor(Y[:, 4 + c, :], GB[:, c % 2, 0:T], Z[:, 20 + c, :], ALU.mult).then_inc(S("na_y"), 1)

                def ret_copy(c):
                    dve.wait_ge(S("ret_pv"), 8 * l + 2 * c + 2)
                    dve.tensor_copy(Z[:, 28 + c, :], GB[:, 2 + c % 2, 0:T]).then_inc(S("ret_o"), 1)

                def na_max(h):
                    dve.wait_ge(S("na_sc"), 8 * l + h + 1)
                    m = NAS[:, 4 * (h % 2):4 * (h % 2) + 2]
                    link(dve.tensor_reduce(m, MB[:, h % 2, :].rearrange("p (a k) -> p a k", k=T), AX.X, ALU.max))
                    dve.tensor_scalar(m, m, -(DH ** -0.5), None, ALU.mult).then_inc(S("na_max"), 1)
                ahead, behind = const("ahead"), const("behind")
                ahead_of(f"mix{l}")
                def mixed_lo(g, n):
                    dve.wait_ge(S("mix_hi"), 7 + 4 * l + n)
                    dve.tensor_tensor(xl[:, 4 * g:4 * g + 4, :], Y[:, 4 * g:4 * g + 4, :], xh[:, 4 * g:4 * g + 4, :], ALU.subtract).then_inc(S("mix_lo"), 1)
                na_max(0)
                for h in range(HEADS):
                    dt, pw = (Z[:, z + h % 2 * 2:z + h % 2 * 2 + 2, :].rearrange("p a k -> p (a k)") for z in (40, 44))
                    link(dve.tensor_scalar(dt, behind, LG[:, 16 + 8 * l + h:17 + 8 * l + h], None, ALU.mult))
                    dve.scalar_tensor_tensor(dt, ahead, LG[:, 8 * l + h:8 * l + h + 1], dt, ALU.mult, ALU.add).then_inc(S("decay_e"), 1)
                    if h + 1 < HEADS:
                        na_max(h + 1)
                    if h == 0:
                        dve.wait_ge(S("conv_w"), l + 1)
                        dve.tensor_tensor(ca, GB[:, 2:4, :].rearrange("p b (a k) -> p (b a) k", k=T), Z[:, 48:52, :], ALU.mult).then_inc(S("mixed"), 1)
                    pr = w2[:, h % 2 * 512:h % 2 * 512 + 512].rearrange("p (a k) -> p a k", k=T)
                    s = NAS[:, 4 * (h % 2) + 2:4 * (h % 2) + 4]
                    dve.wait_ge(S("na_exp"), 16 * l + 2 * h + 2)
                    link(dve.reciprocal(s, s))
                    for t in range(TT):
                        dve.tensor_scalar(pr[:, t, :], pr[:, t, :], s[:, t:t + 1], None, ALU.mult).then_inc(S("na_p"), 1)
                    if h == 5:
                        mixed_lo(0, 1)
                    if h == 7:
                        mixed_lo(3, 2)
                    if h >= 2 and h % 2 == 0:
                        na_gate(h // 2 - 1)
                        ret_copy(h // 2 - 1)
                    if h >= 2:
                        dve.wait_ge(S("ret_pv"), 8 * l + h - 1)
                    dve.wait_ge(S("decay"), 8 * l + h + 1)
                    dve.wait_ge(S("ret_sc"), 8 * l + h + 1)
                    dve.scalar_tensor_tensor(pw, MB[:, 3, :], DH ** -0.5, dt, ALU.mult, ALU.mult).then_inc(S("ret_p"), 1)
                ret_copy(3)
                na_gate(3)
                dve.wait_ge(S("na_y"), 4 * l + 4)
                dve.sem_inc(S("mixed"), 1)

                mixed_lo(1, 3)
                r, var = Z[:, 8:12, :], Z[:, 40:44, :]
                dve.wait_ge(S("ret_std"), 2 * l + 2)
                link(dve.tensor_scalar(var, MB[:, 0:2, :].rearrange("p b (a k) -> p (b a) k", k=T), 1.0 / DH, EPS, ALU.mult, ALU.add))
                newton(r, Z[:, 44:48, :], var)
                link(dve.tensor_tensor(Y[:, 8:12, :], Z[:, 28:32, :], r, ALU.mult))
                dve.tensor_tensor(Y[:, 8:12, :], Y[:, 8:12, :], Z[:, 36:40, :], ALU.mult).then_inc(S("mixed"), 1)
                mixed_lo(2, 4)
                linear(f"mix{l}", add=True, gate=MOD[:, l, 2 * KC:], steps=sum_early(6 + l), then=None if l else "z1")
            norm_out(7, lambda c: col("final_g_2", c))

        @block.tensor
        def _(pe):
            def product(ph, j, b, kc, k0, cols, xs, start, stop):
                s = at[ph][1] + j
                x_hi, x_lo = xs
                hi = w_hi[:, s % SPL, :].rearrange("p (c n) -> p c n", c=kc)
                lo = w_lo[:, s % SPL, :].rearrange("p (c n) -> p c n", c=kc)
                for q, n in enumerate(cols):
                    o = GB[:, b, q * T:q * T + T]
                    for k in range(kc):
                        w, v = hi[:, k, n * P:n * P + P], lo[:, k, n * P:n * P + P]
                        first = start and q == 0 and k == 0
                        pe.matmul(o, w, x_hi[:, k0 + k, :], start=first, stop=False, skip_group_check=True)
                        pe.matmul(o, w, x_lo[:, k0 + k, :], start=False, stop=False, skip_group_check=True)
                        last = pe.matmul(o, v, x_hi[:, k0 + k, :], start=False, stop=stop and k == kc - 1, skip_group_check=True)
                return last

            def linear(ph, parts, steps=()):
                def body(i, first):
                    for j in range(4):
                        s = at[ph][1] + j
                        if first and j < 2 and parts is not None:
                            pe.wait_ge(S(parts[0]), parts[1 + j])
                        taken(pe, ph, j, i)
                        if j % 2 == 0:
                            pe.wait_ge(bank_free[j // 2], uses[ph][j // 2] + i)
                        last = product(ph, j, j // 2, 8, j % 2 * 8, (0, 1), (xh, xl), j % 2 == 0, j % 2 == 1)
                        last.then_inc(block_done[s % SPL], 1)
                body(0, True)
                steps_between(pe, at[ph][2] // 4, body, steps)

            def norm(n):
                early = n in EARLY_SUMS
                if early:
                    pe.wait_ge(S("early_sum"), EARLY_SUMS.index(n) + 1)
                    pe.matmul(MB[:, 0, 0:T], ones[:, :], rstd, start=True, stop=False)
                pe.wait_ge(S("norm_sum"), n + 1)
                pe.matmul(MB[:, 0, 0:T], ones[:, :], ssum, start=not early, stop=True).then_inc(S("norm_ms"), 1)

            def turn(src, ready, copied, before):
                for g in range(8):
                    pe.wait_ge(*before(g))
                    for k in range(4):
                        c = g % 4 * 4 + k
                        ins = pe.transpose(MB[:, g % 4, k * P:k * P + P], src[:, g // 4, c * P:c * P + P], ident)
                    ins.then_inc(S(ready), 1)
            rows = W[:, 0:2 * BLK].rearrange("p (a d) -> p a d", a=TT)
            pe.wait_ge(S("ident_in"), 16)
            pe.wait_ge(S("x_in"), 16)
            turn(rows, "x_tr", "x_t", lambda g: (S("ident_in"), 16) if g < 4 else (S("x_t"), g - 3))
            pe.wait_ge(S("fills"), 1)
            norm(0)
            pe.wait_ge(S("x_t"), 8)
            pe.wait_ge(S("rows_in"), 16 * N_LOADS)
            for g in range(ROW_TILES):
                if g >= 3:
                    pe.wait_ge(S("cols"), g - 2)
                pe.transpose(MB[:, 1 + g % 3, 0:P], PR[:, g, :], ident).then_inc(S("rows_t"), 1)
            linear("w_in", ("norm_lo", 2, 4))

            read_out(pe, "pool_w")
            for g in range(4):
                for k in range(4):
                    h = g % 2 * 4 + k
                    ins = pe.transpose(MB[:, g, k * P:k * P + P], Z[:, 24 + h, g // 2 * P:g // 2 * P + P], ident)
                ins.then_inc(S("v_tr"), 1)
            b = at["pool_w"][0]
            pe.wait_ge(raw_full[b % RAW], 16 * (b // RAW + 1))
            pe.wait_ge(S("pooled"), 4)
            pw = raw[:, b % RAW, :].rearrange("p (k n) -> p k n", n=T)
            pooled = Y[:, 0:8, :]
            for g in range(4):
                for n in range(2):
                    for k in range(2):
                        ins = pe.matmul(GB[:, g, n * T:n * T + T], pw[:, 2 * g + k, n * P:n * P + P], pooled[:, 2 * g + k, :],
                                        start=n == 0 and k == 0, stop=k == 1, skip_group_check=True)
            ins.then_inc(raw_taken[b % RAW], 1)
            pe.wait_ge(raw_taken[b % RAW], b // RAW + 1)
            pe.sem_inc(S("pool_mm"), 1)
            k0 = Z[:, 0:8, :].rearrange("p h t -> p (h t)")
            k1 = Z[:, 24:32, :].rearrange("p h t -> p (h t)")
            pe.wait_ge(S("v_rows"), 4)
            pe.wait_ge(S("q_intra"), 1)
            pe.wait_ge(S("k_intra"), 3)
            for t in range(TT):
                for c in range(4):
                    r = slice(SUB * c, SUB * c + SUB)
                    for h in range(HEADS):
                        at_ = h * T + t * P + c * SUB
                        for half, k in enumerate((k0, k1)):
                            q = w2[:, at_ + half * HALF:at_ + half * HALF + HALF]
                            ins = pe.matmul(MB[r, t, h * SUB + half * HALF:h * SUB + half * HALF + HALF], k[:, at_:at_ + SUB], q,
                                            start=h == 0 and half == 0, stop=True, skip_group_check=True)
                ins.then_inc(S("scores"), 1)
            pe.wait_ge(S("state_k"), 1)
            for g in range(4):
                if g >= 2:
                    pe.wait_ge(S("kt_rows"), g - 1)
                for k in range(4):
                    h = g % 2 * 4 + k
                    ins = pe.transpose(MB[:, 2 + g % 2, k * P:k * P + P], Y[:, 8 + h, g // 2 * P:g // 2 * P + P], ident)
                ins.then_inc(S("kt_tr"), 1)
            V = Z[:, 40:48, :].rearrange("p c t -> p (c t)").rearrange("p (a h v) -> p a h v", a=TT, v=P)
            Kt = w0.rearrange("p (a h d) -> p a h d", a=TT, d=P)
            bd = w3.rearrange("p (a h t) -> p a h t", a=TT, t=P)
            st = w1.rearrange("p (b h v) -> p b h v", b=2, v=P)
            Q = Z[:, 8:16, :]
            pe.wait_ge(S("kt_rows"), 4)
            pe.wait_ge(S("bd"), 8)
            pe.wait_ge(S("q_inter"), 1)
            for t in range(TT):
                if t:
                    pe.wait_ge(S("o_copied"), t)
                for h in range(HEADS):
                    pe.matmul(MB[:, h // 4, h % 4 * P:h % 4 * P + P], V[:, t, h, :], bd[:, t, h, :], start=h % 4 == 0, stop=False, skip_group_check=True)
                for c in range(4):
                    n = 4 * t + c
                    r = slice(SUB * c, SUB * c + SUB)
                    if n:
                        pe.wait_ge(S("state"), n)
                    if n < NCH - 1:
                        for h in range(HEADS):
                            ins = pe.matmul(MB[:, 2 + h // 4, h % 4 * P:h % 4 * P + P], Kt[r, t, h, :], V[r, t, h, :],
                                            start=h % 4 == 0, stop=True, skip_group_check=True)
                        ins.then_inc(S("kv"), 1)
                    if n:
                        for h in range(HEADS):
                            ins = pe.matmul(MB[:, h // 4, h % 4 * P + c * SUB:h % 4 * P + c * SUB + SUB], st[:, n % 2, h, :],
                                            Q[:, h, n * SUB:n * SUB + SUB], start=False, stop=True, skip_group_check=True)
                ins.then_inc(S("o_done"), 1)
            pe.wait_ge(S("o_sq"), 1)
            for b in range(4):
                ins = pe.matmul(MB[:, b, :], ones[:, :], Z[:, 2 * b:2 * b + 2, :].rearrange("p h t -> p (h t)"), start=True, stop=True)
            ins.then_inc(S("o_ms"), 1)

            def mem_columns():
                pe.wait_ge(S("mem_in"), 16)
                pe.wait_ge(S("o_var"), 1)
                turn(rows, "x_tr", "x_t", lambda g: (S("o_var"), 1) if g < 4 else (S("x_t"), 8 + g - 3))
            linear("w_out", ("mix_lo", 1, 3), steps=[(1, mem_columns), (3, lambda: norm(1))])
            linear("wk", ("norm_lo", 6, 8), steps=[(3, lambda: norm(2))])
            linear("wv", None)
            linear("wq", ("norm_lo", 10, 12))
            read_out(pe, "wo")
            K, V, Q = Z[:, 0:16, :], Z[:, 16:32, :], Z[:, 32:48, :]
            pe.wait_ge(S("norm_std"), 3)
            for g in range(8):
                if g >= 2:
                    pe.wait_ge(S("xv_rows"), g - 1)
                for k in range(4):
                    ins = pe.transpose(MB[:, 2 + g % 2, k * P:k * P + P], V[:, g % 4 * 4 + k, g // 4 * P:g // 4 * P + P], ident)
                ins.then_inc(S("xv_tr"), 1)
            Vs = W[:, 0:2 * BLK].rearrange("p (a d) -> p a d", a=TT)
            p = w2.rearrange("p (b a k) -> p b a k", b=4, k=T)
            pT = w3.rearrange("p (b a k) -> p b a k", b=4, k=T)
            for h in range(X_HEADS):
                if h >= 2:
                    pe.wait_ge(S("x_exp"), 2 * h - 2)
                for a in range(TT):
                    for c in range(4):
                        ins = pe.matmul(MB[:, h % 2, a * T:a * T + T], Q[:, 4 * h + c, a * P:a * P + P], K[:, 4 * h + c, :],
                                        start=a == 0 and c == 0, stop=c == 3, skip_group_check=True)
                ins.then_inc(S("x_sc"), 1)
            pe.wait_ge(S("xv_rows"), 8)
            for h in range(X_HEADS):
                pe.wait_ge(S("x_p"), 2 * h + 2)
                if h:
                    pe.wait_ge(S("x_pt"), h)
                for k in range(TT):
                    for a in range(TT):
                        ins = pe.transpose(MB[:, 2, k * T + a * P:k * T + a * P + P], p[:, h, a, k * P:k * P + P], ident)
                ins.then_inc(S("x_ptr"), 1)
                pe.wait_ge(S("x_pt"), h + 1)
                for b in range(2):
                    if h == 0:
                        pe.wait_ge(S("x_exp"), 8)
                    else:
                        pe.wait_ge(S("x_y"), 2 * h - 1 + b)
                    for c in range(2):
                        for k in range(TT):
                            d = h * X_DH + (2 * b + c) * P
                            ins = pe.matmul(MB[:, b, c * T:c * T + T], Vs[:, k, d:d + P], pT[:, h, k, :], start=c == 0 and k == 0, stop=k == 1, skip_group_check=True)
                    ins.then_inc(S("x_o"), 1)
            linear("wo", ("mix_lo", 3 + 2, 3 + 4))
            norm(3)
            pe.wait_ge(S("router_in"), 32)
            for c in range(KC):
                if c % 4 == 0:
                    pe.wait_ge(S("norm_h"), 12 + c // 4 + 1)
                for a in range(TT):
                    ins = pe.matmul(MB[:, 1, 20 * a:20 * a + 20], Zn[:, c, a * P:a * P + P], RW[:, c, :], start=a == 0 and c == 0, stop=c == KC - 1, skip_group_check=True)
            ins.then_inc(S("r_mm"), 1)

            def spread_weights():
                pe.wait_ge(S("combine"), 4)
                pe.wait_ge(S("r_logits"), 2)
                for a in range(TT):
                    ins = pe.transpose(MB[0:16, 1, a * P:a * P + P], CMB[:, 16 * a:16 * a + 16], ident)
                ins.then_inc(S("r_tr"), 1)
                pe.wait_ge(S("r_t"), 1)
                for g in range(8):
                    if g >= 2:
                        pe.wait_ge(S("comb"), g - 1)
                    for k in range(2):
                        e = 2 * g + k
                        ins = pe.matmul(MB[:, 2 + g % 2, k * T:k * T + T], ident[0:16, e:e + 1].broadcast_to([16, P]), RT[0:16, 136:392],
                                        start=k == 0, stop=True, skip_group_check=True)
                    ins.then_inc(S("r_bc"), 1)

            pe.wait_ge(S("norm_lo"), 16)
            hh = w2[:, 0:512].bitcast(F16).rearrange("p (c t) -> p c t", t=T)
            hl = w2[:, 512:1024].bitcast(F16).rearrange("p (c t) -> p c t", t=T)

            def half(u, j, i, free):
                for k in range(4):
                    b, s = 2 * u + k // 2, at["moe"][1] + j + k
                    taken(pe, "moe", j + k, i)
                    if k % 2 == 0:
                        pe.wait_ge(bank_free[b], free + uses["moe"][b])
                    product("moe", j + k, b, 8, k % 2 * 8, (0, 1), (xh, xl), k % 2 == 0, k % 2 == 1).then_inc(block_done[s % SPL], 1)

            def down(j, i, e, free):
                pe.wait_ge(S("hid_lo"), e * 2 + 2)
                for k in range(4):
                    s = at["moe"][1] + j + k
                    taken(pe, "moe", j + k, i)
                    for q in range(2):
                        b = (2 * k + q + 2) % 4
                        pe.wait_ge(bank_free[b], free[b // 2] + uses["moe"][b] + k // 2)
                        last = product("moe", j + k, b, 4, 0, (2 * q, 2 * q + 1), (hh, hl), True, True)
                    last.then_inc(block_done[s % SPL], 1)
            half(0, 0, 0, 0)
            spread_weights()
            half(1, 4, 0, 0)
            with pe.Fori(0, N_EXP - 1) as n:
                i = n * 3
                half(0, 8, i, i + 1)
                down(12, i, n, (i + 2, i + 1))
                half(1, 16, i, i + 3)
            used = 3 * (N_EXP - 1) + 1
            down(8, 3 * (N_EXP - 1), N_EXP - 1, (used, used))
            def modulation(l, start, end):
                for n in range(start, end):
                    at_ = (l * 3 * KC + n) * P
                    ins = pe.matmul(MB[:, 1 + l, n:n + 1], SUMS[:, at_:at_ + P], ones[:, 0:1], start=n == 0, stop=True, skip_group_check=True)
                ins.then_inc(S("ada"), 1)
            for j in range(2):
                pe.wait_ge(ada_used[j], N_EXP * N_SUMS // 2)
            modulation(0, 0, KC)
            norm(4)
            modulation(0, KC, 3 * KC)
            modulation(1, 0, KC)

            for l in range(LAYERS):
                norm(5 + l)
                if l == 0:
                    modulation(1, KC, 3 * KC)
                linear(f"z{l}", ("norm_lo", 18 + 4 * l, 20 + 4 * l))
                read_out(pe, f"fft{l}")
                rot = const("rot")

                def rotate(c):
                    if c >= 2:
                        pe.wait_ge(S("rotated"), 8 * l + c - 1)
                    pe.matmul(GB[:, c % 2, 0:T], rot, Z[:, 24 + c, :], start=True, stop=True).then_inc(S("rot"), 1)
                pe.wait_ge(S("conv_a"), l + 1)
                for c in range(4):
                    ins = pe.matmul(GB[:, 2, 0:T], ones[:, :], ca[:, c, :], start=c == 0, stop=c == 3)
                ins.then_inc(S("conv_sum"), 1)
                rotate(0)
                rotate(1)
                pe.wait_ge(S("norm_std"), 6 + l)
                pe.wait_ge(S("x_ready"), l + 1)
                for k, z in enumerate((16, 32)):
                    for a in range(TT):
                        for c in range(4):
                            ins = pe.transpose(MB[:, 2 * k + a, c * P:c * P + P], Z[:, z + c, a * P:a * P + P], ident)
                        ins.then_inc(S("zv_tr"), 1)
                rotate(2)
                rotate(3)
                for a in range(TT):
                    for g in range(4):
                        if g % 2 == 0:
                            pe.wait_ge(S("zv_rows"), 4 * l + 2 * a + g // 2 + 1)
                        ins = pe.matmul(MB[:, 2 * a + g // 2, g % 2 * T:g % 2 * T + T], Z[:, g, a * P:a * P + P], const("dft_ch"),
                                        start=g % 2 == 0, stop=True, skip_group_check=True)
                        if g % 2:
                            ins.then_inc(S("fft_ch"), 1)
                rotate(4)
                rotate(5)
                pe.wait_ge(S("conv_sq"), l + 1)
                for c in range(4):
                    ins = pe.matmul(GB[:, 3, 0:T], ones[:, :], csq[:, c, :], start=c == 0, stop=c == 3)
                ins.then_inc(S("conv_var"), 1)
                fa = w2.rearrange("p (a g n) -> p a g n", a=TT, g=4)
                dcos = const("dft_cos").rearrange("p (a t) -> p a t", t=T)
                dsin = const("dft_nsin").rearrange("p (a t) -> p a t", t=T)
                pe.wait_ge(S("fft_a"), 4 * l + 4)
                for g in range(4):
                    for a in range(TT):
                        for k, m in enumerate((dcos, dsin)):
                            ins = pe.matmul(MB[:, g // 2, g % 2 * T:g % 2 * T + T], fa[:, a, g, k * P:k * P + P], m[:, a, :],
                                            start=g % 2 == 0 and a == 0 and k == 0, stop=a == 1 and k == 1, skip_group_check=True)
                    if g % 2:
                        ins.then_inc(S("fft_tok"), 1)
                rotate(6)
                rotate(7)

                def small(ph, x, banks, ready):
                    b = at[ph][0]
                    pe.wait_ge(raw_full[b % RAW], 16 * (b // RAW + 1))
                    w = raw[:, b % RAW, :].rearrange("p (c n) -> p c n", n=512)
                    for n in range(4):
                        for k in range(4):
                            ins = pe.matmul(banks[:, n // 2, n % 2 * T:n % 2 * T + T], w[:, k, n * P:n * P + P], x[:, k, :],
                                            start=n % 2 == 0 and k == 0, stop=k == 3, skip_group_check=True)
                    ins.then_inc(raw_taken[b % RAW], 1)
                    pe.wait_ge(raw_taken[b % RAW], b // RAW + 1)
                    pe.sem_inc(S(ready), 1)
                pe.wait_ge(S("fft_y"), 2 * l + 2)
                small(f"fft{l}", Z[:, 0:4, :], MB[:, 2:4, :], "fft_w")
                nv = w3[:, 1024:2048].rearrange("p (a n) -> p a n", a=TT)
                rv = w3[:, 0:1024].rearrange("p (a n) -> p a n", a=TT)
                bias = W[:, 0:2 * BLK].rearrange("p (q h k) -> p q h k", q=TT, k=T)

                def na_scores(h):
                    c, r = h // 2, slice(DH * (h % 2), DH * (h % 2) + DH)
                    if h >= 2:
                        pe.wait_ge(S("na_exp"), 16 * l + 2 * h - 2)
                    for a in range(TT):
                        o = MB[:, h % 2, a * T:a * T + T]
                        pe.matmul(o, const("unflip"), bias[:, a, h, :], start=a == 0, stop=False, skip_group_check=True)
                        ins = pe.matmul(o, Z[r, 8 + c, a * P:a * P + P], Z[r, 12 + c, :], start=False, stop=True, skip_group_check=True)
                    ins.then_inc(S("na_sc"), 1)
                pe.wait_ge(S("bias_masked"), 2 * l + 2)
                na_scores(0)
                na_scores(1)
                pe.wait_ge(S("conv_s"), l + 1)
                small(f"pw{l}", ca, GB[:, 2:4, :], "conv_w")
                pe.wait_ge(S("rotated"), 8 * l + 8)
                pe.wait_ge(S("mixed"), 4 * l + 1)
                for h in range(HEADS):
                    c, r = h // 2, slice(DH * (h % 2), DH * (h % 2) + DH)
                    if h:
                        pe.wait_ge(S("ret_p"), 8 * l + h)
                    for a in range(TT):
                        ins = pe.matmul(MB[:, 3, a * T:a * T + T], Z[r, 28 + c, a * P:a * P + P], Z[r, 24 + c, :], start=a == 0, stop=True, skip_group_check=True)
                    ins.then_inc(S("ret_sc"), 1)
                    pr = w2[:, h % 2 * 512:h % 2 * 512 + 512].rearrange("p (a k) -> p a k", k=T)
                    pt = w2[:, 1024 + h % 2 * 512:1536 + h % 2 * 512].rearrange("p (a k) -> p a k", k=T)
                    pe.wait_ge(S("na_p"), 16 * l + 2 * h + 2)
                    if h:
                        pe.wait_ge(S("na_pt"), 8 * l + h)
                    for k in range(TT):
                        for a in range(TT):
                            ins = pe.transpose(MB[:, 2, k * T + a * P:k * T + a * P + P], pr[:, a, k * P:k * P + P], ident)
                    ins.then_inc(S("na_ptr"), 1)
                    pw = Z[:, 44 + h % 2 * 2:46 + h % 2 * 2, :]
                    pe.wait_ge(S("ret_p"), 8 * l + h + 1)
                    if h == 0:
                        pe.wait_ge(S("mixed"), 4 * l + 2)
                    if h % 2 == 0 and c >= 2:
                        pe.wait_ge(S("ret_o"), 4 * l + c - 1)
                    for k in range(TT):
                        ins = pe.matmul(GB[r, 2 + c % 2, 0:T], rv[:, k, h * DH:h * DH + DH], pw[:, k, :], start=k == 0, stop=k == 1, skip_group_check=True)
                    ins.then_inc(S("ret_pv"), 1)
                    pe.wait_ge(S("na_pt"), 8 * l + h + 1)
                    if h % 2 == 0 and c >= 2:
                        pe.wait_ge(S("na_y"), 4 * l + c - 1)
                    for k in range(TT):
                        ins = pe.matmul(GB[r, c % 2, 0:T], nv[:, k, h * DH:h * DH + DH], pt[:, k, :], start=k == 0, stop=k == 1, skip_group_check=True)
                    if h % 2:
                        ins.then_inc(S("na_o"), 1)
                    if h + 2 < HEADS:
                        na_scores(h + 2)
                pe.wait_ge(S("ret_sq"), l + 1)
                for b in range(2):
                    ins = pe.matmul(MB[:, b, :], const("pair"), Z[:, 8 + 2 * b:10 + 2 * b, :].rearrange("p c t -> p (c t)"), start=True, stop=True)
                ins.then_inc(S("ret_ms"), 1)
                linear(f"mix{l}", ("mix_lo", 7 + 4 * l + 3, 7 + 4 * l + 4))
            norm(7)
            for g in range(8):
                pe.wait_ge(S("norm_out7"), g % 4 + 1)
                if g >= 4:
                    pe.wait_ge(S("out_rows"), g - 3)
                for k in range(4):
                    ins = pe.transpose(MB[:, g % 4, k * P:k * P + P], Zn[:, g % 4 * 4 + k, g // 4 * P:g // 4 * P + P], ident)
                ins.then_inc(S("out_tr"), 1)


def row_loads():
    n, loads = 0, 0
    for _, k in ROWS:
        r = 0
        while r < k:
            r += min(k - r, P - (n + r) % P)
            loads += 1
        n += k
    return loads


N_LOADS = row_loads()


INPUTS = ["x", "mem", "norm_mix", "w_in", "pool_w", "pool_scale", "hgrn_lb_logits", "hgrn_norm", "w_out",
          "norm_xattn", "norm_mem", "xattn_wq", "xattn_wk", "xattn_wv", "xattn_wo", "norm_ffn", "router_group",
          "router_expert", "w_gate", "w_up", "w_down", "norm_final", "c_2", "norm_g_2", "w_ada_2", "b_ada_2",
          "w_in_2", "w_fft_2", "na_rel_bias_2", "ret_logit_fwd_2", "ret_logit_bwd_2", "conv_w_2", "conv_b_2",
          "conv_ln_g_2", "conv_ln_b_2", "conv_w_pw_2", "w_out_2", "final_g_2"]


def lay_out(inputs, nc):
    tables = constants()
    arrays, A, const_at, at = {}, {}, {}, 0
    for name in INPUTS:
        arrays[name] = np.ascontiguousarray(inputs[name])
        A[name] = nc.dram_tensor(name, arrays[name].shape, F32, kind="ExternalInput").ap()
    for name, v in tables.items():
        const_at[name] = (at, v.shape[1])
        at += v.shape[1]
    arrays["table"] = np.concatenate(list(tables.values()), 1)
    arrays["window_counts"] = counts()
    table = nc.dram_tensor("table", arrays["table"].shape, F32, kind="ExternalInput").ap()
    window_counts = nc.dram_tensor("window_counts", arrays["window_counts"].shape, F32, kind="ExternalInput").ap()
    out = nc.dram_tensor("out", (1, T, D), F32, kind="ExternalOutput").ap()
    build(nc, A, table, const_at, window_counts, out)
    return arrays


def kernel(**inputs):
    from concourse import bacc
    from concourse.bass_utils import run_bass_kernel_spmd

    nc = bacc.Bacc("TRN2", target_bir_lowering=False, num_devices=1)
    arrays = lay_out(inputs, nc)
    r = run_bass_kernel_spmd(nc, [arrays], core_ids=[0])
    return r.results[0]["out"]
```
